# Optimizing a Trainium2 kernel written in Bass

```python
import math
import jax, jax.numpy as jnp
from jax import lax
import numpy as np

'''
One inference step of a 2-layer hybrid autoregressive decoder trunk, run for a
prompt group and a sample group that share the same parameter arrays.

Layer (pre-norm, plain residual adds):
  a = RMSNorm(h); proj = a @ w_in  (single combined input projection whose columns are
  partitioned into  z | x,B,C | dt  for the Mamba-2 SSD head group and  u,v  for the
  chunked gMLP head group)
  SSD group : depthwise causal conv(width 4) on x/B/C -> SiLU -> chunked SSD scan with
              grouped B/C (8 heads, 2 groups, state 128) + D skip -> RMSNorm(y * SiLU(z))
  gMLP group: GELU(u,v); v <- RMSNorm(v); per head: u * (tril(W_s) v_chunk + b), chunks of
              128 aligned positions
  h += concat(ssd_out, gmlp_out) @ w_out
  h += HierMoE(RMSNorm(h))  (top-1 expert group, then top-2 experts inside it)
  h += sigmoid(RMSNorm(h) @ w_pg) * RMSNorm(p[i] @ w_ple)   (per-layer input embedding)
Final RMSNorm.

Inputs:
  x_prompt   (BATCH, SEQ, D_MODEL)            positions 0..SEQ-1
  x_sample   (DEC_BATCH, DEC_SEQ, D_MODEL)    positions PAST_LEN..PAST_LEN+DEC_SEQ-1
  state_conv (DEPTH, DEC_BATCH, CONV_WIDTH-1, CONV_DIM)  last raw x/B/C rows before the conv
  state_ssm  (DEPTH, DEC_BATCH, SSD_HEADS, SSD_HEAD_DIM, D_STATE)  SSD recurrent state
  p_prompt   (DEPTH, BATCH, SEQ, D_PLE);  p_sample (DEPTH, DEC_BATCH, DEC_SEQ, D_PLE)
  then the weights, stacked on a leading DEPTH axis (norm_final has no DEPTH axis).
Returns the tuple
  (y_prompt          (BATCH, SEQ, D_MODEL),
   y_sample          (DEC_BATCH, DEC_SEQ, D_MODEL),
   new_conv_prompt   (DEPTH, BATCH, CONV_WIDTH-1, CONV_DIM),
   new_ssm_prompt    (DEPTH, BATCH, SSD_HEADS, SSD_HEAD_DIM, D_STATE),
   new_conv_sample   (DEPTH, DEC_BATCH, CONV_WIDTH-1, CONV_DIM),
   new_ssm_sample    (DEPTH, DEC_BATCH, SSD_HEADS, SSD_HEAD_DIM, D_STATE),
   new_gmlp_v_sample (DEPTH, DEC_BATCH, DEC_SEQ, D_GMLP))  normalised v rows of the new chunk
'''

D_MODEL = 1024
BATCH = 1
SEQ = 1024
DEPTH = 1
DEC_BATCH = 8
DEC_SEQ = 4
PAST_LEN = 8192
PAGE_SIZE = 128

D_MIX = D_MODEL
D_SSD = D_MIX // 2
SSD_HEAD_DIM = 64
SSD_HEADS = D_SSD // SSD_HEAD_DIM
SSD_GROUPS = 2
D_STATE = 128
CONV_WIDTH = 4
SSD_CHUNK = 128
CONV_DIM = D_SSD + 2 * SSD_GROUPS * D_STATE
D_GMLP = D_MIX - D_SSD
GMLP_HEADS = 8
GMLP_HEAD_DIM = D_GMLP // GMLP_HEADS
GMLP_CHUNK = 128
IN_DIM = D_SSD + CONV_DIM + SSD_HEADS + 2 * D_GMLP
N_EXPERT_GROUPS = 4
EXPERTS_PER_GROUP = 4
N_EXPERTS = N_EXPERT_GROUPS * EXPERTS_PER_GROUP
TOP_K_GROUP = 1
TOP_K_EXPERT = 2
D_EXPERT = 512
D_PLE = 256
EPS = 1e-6

kernel_name = 'hymba_ssd_gmlp_hiermoe_step'

def rms_norm(x, g):
    xf = x.astype(jnp.float32)
    y = xf * lax.rsqrt(jnp.mean(xf * xf, axis=-1, keepdims=True) + EPS)
    return (y * g.astype(jnp.float32)).astype(x.dtype)

def gated_group_rms_norm(y, z, g):
    yf = y.astype(jnp.float32) * jax.nn.silu(z.astype(jnp.float32))
    shp = yf.shape
    yg = yf.reshape(shp[:-1] + (SSD_GROUPS, shp[-1] // SSD_GROUPS))
    yg = yg * lax.rsqrt(jnp.mean(yg * yg, axis=-1, keepdims=True) + EPS)
    return (yg.reshape(shp) * g.astype(jnp.float32)).astype(y.dtype)

def segsum(a):
    t = a.shape[-1]
    xe = jnp.broadcast_to(a[..., :, None], a.shape + (t,))
    strict = jnp.tril(jnp.ones((t, t), dtype=bool), -1)
    xs = jnp.cumsum(jnp.where(strict, xe, 0.0), axis=-2)
    incl = jnp.tril(jnp.ones((t, t), dtype=bool), 0)
    return jnp.where(incl, xs, -jnp.inf)

def causal_depthwise_conv(x_ext, w, b):
    c = x_ext.shape[-1]
    y = lax.conv_general_dilated(x_ext, w[:, None, :].astype(x_ext.dtype), window_strides=(1,),
                                 padding='VALID', dimension_numbers=('NWC', 'WIO', 'NWC'),
                                 feature_group_count=c)
    return y + b.astype(y.dtype)

def ssd_scan(x, dt, a, b_in, c_in, init_state):
    f32 = jnp.float32
    bt, seq_len, n_heads, head_dim = x.shape
    n_groups, d_state = b_in.shape[-2:]
    rep = n_heads // n_groups
    q = min(SSD_CHUNK, seq_len)
    n_chunks = -(-seq_len // q)
    pad = n_chunks * q - seq_len
    xf = x.astype(f32) * dt[..., None]
    da = dt * a
    bf = b_in.astype(f32)
    cf = c_in.astype(f32)
    if pad:
        padt = lambda t: jnp.pad(t, [(0, 0), (0, pad)] + [(0, 0)] * (t.ndim - 2))
        xf, da, bf, cf = padt(xf), padt(da), padt(bf), padt(cf)
    xf = xf.reshape(bt, n_chunks, q, n_groups, rep, head_dim)
    bf = bf.reshape(bt, n_chunks, q, n_groups, d_state)
    cf = cf.reshape(bt, n_chunks, q, n_groups, d_state)
    da = jnp.moveaxis(da.reshape(bt, n_chunks, q, n_groups, rep), 2, -1)
    cum = jnp.cumsum(da, axis=-1)
    decay = jnp.exp(segsum(da))
    cb = jnp.einsum('bclgn,bcsgn->bcgls', cf, bf)
    wts = cb[:, :, :, None] * decay
    y_diag = jnp.einsum('bcgrls,bcsgrp->bclgrp', wts, xf)
    decay_states = jnp.exp(cum[..., -1:] - cum)
    chunk_states = jnp.einsum('bclgn,bcgrl,bclgrp->bcgrpn', bf, decay_states, xf)
    init = init_state.astype(f32).reshape(bt, n_groups, rep, head_dim, d_state)
    states = jnp.concatenate([init[:, None], chunk_states], axis=1)
    tot = jnp.pad(jnp.moveaxis(cum[..., -1], 1, -1), [(0, 0), (0, 0), (0, 0), (1, 0)])
    dchunk = jnp.exp(segsum(tot))
    new_states = jnp.einsum('bgrzc,bcgrpn->bzgrpn', dchunk, states)
    y_off = jnp.einsum('bclgn,bcgrpn,bcgrl->bclgrp', cf, new_states[:, :-1], jnp.exp(cum))
    y = (y_diag + y_off).reshape(bt, n_chunks * q, n_heads, head_dim)[:, :seq_len]
    final = new_states[:, -1].reshape(bt, n_heads, head_dim, d_state)
    return y, final

def chunk_spatial_gating(u, v, w_s, b_s):
    bt, seq_len, n_h, d_h = v.shape
    n_chunks = -(-seq_len // GMLP_CHUNK)
    pad = n_chunks * GMLP_CHUNK - seq_len
    if pad:
        v = jnp.pad(v, [(0, 0), (0, pad), (0, 0), (0, 0)])
    vc = v.reshape(bt, n_chunks, GMLP_CHUNK, n_h, d_h)
    causal = jnp.tril(jnp.ones((GMLP_CHUNK, GMLP_CHUNK), dtype=bool))
    ws = jnp.where(causal, w_s, 0.0).astype(v.dtype)
    s = jnp.einsum('hts,bcshd->bcthd', ws, vc) + b_s.T.astype(v.dtype)[:, :, None]
    s = s.reshape(bt, n_chunks * GMLP_CHUNK, n_h, d_h)[:, :seq_len]
    return u * s

def hierarchical_moe(m, w_rg, b_rg, w_re, b_re, w_gate, w_up, w_down):
    shp = m.shape
    t = m.reshape(-1, shp[-1])
    n = t.shape[0]
    rows = jnp.arange(n)
    f32 = jnp.float32
    lg = (t @ w_rg).astype(f32) + b_rg.astype(f32)
    pg = jax.nn.softmax(lg, axis=-1)
    _, g_sel = lax.top_k(lg, TOP_K_GROUP)
    g_sel = g_sel[:, 0]
    p_sel = pg[rows, g_sel][:, None]
    le = ((t @ w_re).astype(f32) + b_re.astype(f32)).reshape(n, N_EXPERT_GROUPS, EXPERTS_PER_GROUP)
    le_g = le[rows, g_sel]
    top_v, top_i = lax.top_k(le_g, TOP_K_EXPERT)
    gates = jax.nn.softmax(top_v, axis=-1) * p_sel
    e_idx = g_sel[:, None] * EXPERTS_PER_GROUP + top_i
    comb = jnp.sum(jax.nn.one_hot(e_idx, N_EXPERTS, dtype=f32) * gates[..., None], axis=1)
    comb = comb.astype(t.dtype)
    y = jnp.zeros_like(t)
    for e in range(N_EXPERTS):
        hid = jax.nn.silu(t @ w_gate[e]) * (t @ w_up[e])
        y = y + comb[:, e:e + 1] * (hid @ w_down[e])
    return y.reshape(shp)

def decoder_layer(h, p_i, conv_state, ssm_state, norm_mix, w_in, conv_w, conv_b, dt_bias, a_log,
                  d_skip, ssd_norm, gmlp_norm, w_spatial, b_spatial, w_out, norm_ffn,
                  w_router_group, b_router_group, w_router_expert, b_router_expert,
                  w_gate, w_up, w_down, w_ple, norm_ple, norm_pg, w_pg):
    bt, seq_len, _ = h.shape
    a = rms_norm(h, norm_mix)
    proj = a @ w_in
    z, xbc, dt_raw, uv = jnp.split(proj, [D_SSD, D_SSD + CONV_DIM, D_SSD + CONV_DIM + SSD_HEADS], axis=-1)
    xbc_ext = jnp.concatenate([conv_state.astype(xbc.dtype), xbc], axis=1)
    new_conv = xbc_ext[:, -(CONV_WIDTH - 1):]
    xbc_c = jax.nn.silu(causal_depthwise_conv(xbc_ext, conv_w, conv_b))
    xs, bs, cs = jnp.split(xbc_c, [D_SSD, D_SSD + SSD_GROUPS * D_STATE], axis=-1)
    dt = jax.nn.softplus(dt_raw.astype(jnp.float32) + dt_bias.astype(jnp.float32))
    a_neg = -jnp.exp(a_log.astype(jnp.float32))
    xs_h = xs.reshape(bt, seq_len, SSD_HEADS, SSD_HEAD_DIM)
    y_ssd, new_ssm = ssd_scan(xs_h, dt, a_neg,
                              bs.reshape(bt, seq_len, SSD_GROUPS, D_STATE),
                              cs.reshape(bt, seq_len, SSD_GROUPS, D_STATE), ssm_state)
    y_ssd = y_ssd + d_skip.astype(jnp.float32)[:, None] * xs_h.astype(jnp.float32)
    y_ssd = gated_group_rms_norm(y_ssd.reshape(bt, seq_len, D_SSD).astype(h.dtype), z, ssd_norm)
    uv = jax.nn.gelu(uv, approximate=False)
    u, v = jnp.split(uv, 2, axis=-1)
    v = rms_norm(v, gmlp_norm)
    y_gm = chunk_spatial_gating(u.reshape(bt, seq_len, GMLP_HEADS, GMLP_HEAD_DIM),
                                v.reshape(bt, seq_len, GMLP_HEADS, GMLP_HEAD_DIM),
                                w_spatial, b_spatial).reshape(bt, seq_len, D_GMLP)
    h = h + jnp.concatenate([y_ssd, y_gm], axis=-1) @ w_out
    h = h + hierarchical_moe(rms_norm(h, norm_ffn), w_router_group, b_router_group,
                             w_router_expert, b_router_expert, w_gate, w_up, w_down)
    e = rms_norm(p_i.astype(h.dtype) @ w_ple, norm_ple)
    gate = jax.nn.sigmoid(rms_norm(h, norm_pg) @ w_pg)
    h = h + gate * e
    return h, new_conv, new_ssm.astype(ssm_state.dtype), v

def trunk(x, p, conv_states, ssm_states, norm_mix, w_in, conv_w, conv_b, dt_bias, a_log, d_skip,
          ssd_norm, gmlp_norm, w_spatial, b_spatial, w_out, norm_ffn, w_router_group,
          b_router_group, w_router_expert, b_router_expert, w_gate, w_up, w_down, w_ple,
          norm_ple, norm_pg, w_pg, norm_final):
    h = x
    convs, ssms, vs = [], [], []
    for i in range(DEPTH):
        h, c_i, s_i, v_i = decoder_layer(
            h, p[i], conv_states[i], ssm_states[i], norm_mix[i], w_in[i], conv_w[i], conv_b[i],
            dt_bias[i], a_log[i], d_skip[i], ssd_norm[i], gmlp_norm[i], w_spatial[i], b_spatial[i],
            w_out[i], norm_ffn[i], w_router_group[i], b_router_group[i], w_router_expert[i],
            b_router_expert[i], w_gate[i], w_up[i], w_down[i], w_ple[i], norm_ple[i], norm_pg[i],
            w_pg[i])
        convs.append(c_i)
        ssms.append(s_i)
        vs.append(v_i)
    y = rms_norm(h, norm_final)
    return y, jnp.stack(convs), jnp.stack(ssms), jnp.stack(vs)

def setup_inputs(seed: int = 0) -> dict:
    key = jax.random.key(seed)
    ks = jax.random.split(key, 40)
    f32 = jnp.float32
    nrm = lambda k, shape, scale: jax.random.normal(k, shape, f32) * scale
    gain = lambda k, shape: 1.0 + 0.05 * jax.random.normal(k, shape, f32)
    dt0 = jnp.exp(jax.random.uniform(ks[10], (DEPTH, SSD_HEADS), f32, math.log(1e-3), math.log(1e-1)))
    dt_bias = dt0 + jnp.log(-jnp.expm1(-dt0))
    a_log = jnp.log(jax.random.uniform(ks[11], (DEPTH, SSD_HEADS), f32, 1.0, 16.0))
    return {
        'x_prompt': nrm(ks[0], (BATCH, SEQ, D_MODEL), 1.0),
        'x_sample': nrm(ks[1], (DEC_BATCH, DEC_SEQ, D_MODEL), 1.0),
        'state_conv': nrm(ks[2], (DEPTH, DEC_BATCH, CONV_WIDTH - 1, CONV_DIM), 1.0),
        'state_ssm': nrm(ks[3], (DEPTH, DEC_BATCH, SSD_HEADS, SSD_HEAD_DIM, D_STATE), 0.1),
        'p_prompt': nrm(ks[4], (DEPTH, BATCH, SEQ, D_PLE), 1.0),
        'p_sample': nrm(ks[5], (DEPTH, DEC_BATCH, DEC_SEQ, D_PLE), 1.0),
        'norm_mix': gain(ks[6], (DEPTH, D_MODEL)),
        'w_in': nrm(ks[7], (DEPTH, D_MODEL, IN_DIM), D_MODEL ** -0.5),
        'conv_w': nrm(ks[8], (DEPTH, CONV_WIDTH, CONV_DIM), CONV_WIDTH ** -0.5),
        'conv_b': nrm(ks[9], (DEPTH, CONV_DIM), 0.02),
        'dt_bias': dt_bias,
        'a_log': a_log,
        'd_skip': gain(ks[12], (DEPTH, SSD_HEADS)),
        'ssd_norm': gain(ks[13], (DEPTH, D_SSD)),
        'gmlp_norm': gain(ks[14], (DEPTH, D_GMLP)),
        'w_spatial': nrm(ks[15], (DEPTH, GMLP_HEADS, GMLP_CHUNK, GMLP_CHUNK), GMLP_CHUNK ** -0.5),
        'b_spatial': 1.0 + nrm(ks[16], (DEPTH, GMLP_HEADS, GMLP_CHUNK), 0.02),
        'w_out': nrm(ks[17], (DEPTH, D_MIX, D_MODEL), D_MIX ** -0.5),
        'norm_ffn': gain(ks[18], (DEPTH, D_MODEL)),
        'w_router_group': nrm(ks[19], (DEPTH, D_MODEL, N_EXPERT_GROUPS), D_MODEL ** -0.5),
        'b_router_group': nrm(ks[20], (DEPTH, N_EXPERT_GROUPS), 0.01),
        'w_router_expert': nrm(ks[21], (DEPTH, D_MODEL, N_EXPERTS), D_MODEL ** -0.5),
        'b_router_expert': nrm(ks[22], (DEPTH, N_EXPERTS), 0.01),
        'w_gate': nrm(ks[23], (DEPTH, N_EXPERTS, D_MODEL, D_EXPERT), D_MODEL ** -0.5),
        'w_up': nrm(ks[24], (DEPTH, N_EXPERTS, D_MODEL, D_EXPERT), D_MODEL ** -0.5),
        'w_down': nrm(ks[25], (DEPTH, N_EXPERTS, D_EXPERT, D_MODEL), D_EXPERT ** -0.5),
        'w_ple': nrm(ks[26], (DEPTH, D_PLE, D_MODEL), D_PLE ** -0.5),
        'norm_ple': gain(ks[27], (DEPTH, D_MODEL)),
        'norm_pg': gain(ks[28], (DEPTH, D_MODEL)),
        'w_pg': nrm(ks[29], (DEPTH, D_MODEL, D_MODEL), D_MODEL ** -0.5),
        'norm_final': gain(ks[30], (D_MODEL,)),
    }

def reference(x_prompt, x_sample, state_conv, state_ssm, p_prompt, p_sample, norm_mix, w_in,
              conv_w, conv_b, dt_bias, a_log, d_skip, ssd_norm, gmlp_norm, w_spatial, b_spatial,
              w_out, norm_ffn, w_router_group, b_router_group, w_router_expert, b_router_expert,
              w_gate, w_up, w_down, w_ple, norm_ple, norm_pg, w_pg, norm_final):
    weights = (norm_mix, w_in, conv_w, conv_b, dt_bias, a_log, d_skip, ssd_norm, gmlp_norm,
               w_spatial, b_spatial, w_out, norm_ffn, w_router_group, b_router_group,
               w_router_expert, b_router_expert, w_gate, w_up, w_down, w_ple, norm_ple,
               norm_pg, w_pg, norm_final)
    n_prompt = x_prompt.shape[0]
    zero_conv = jnp.zeros((DEPTH, n_prompt, CONV_WIDTH - 1, CONV_DIM), x_prompt.dtype)
    zero_ssm = jnp.zeros((DEPTH, n_prompt) + state_ssm.shape[2:], state_ssm.dtype)
    y_prompt, new_conv_prompt, new_ssm_prompt, _ = trunk(x_prompt, p_prompt, zero_conv, zero_ssm, *weights)
    y_sample, new_conv_sample, new_ssm_sample, new_gmlp_v_sample = trunk(
        x_sample, p_sample, state_conv, state_ssm, *weights)
    return (y_prompt, y_sample, new_conv_prompt, new_ssm_prompt, new_conv_sample, new_ssm_sample, new_gmlp_v_sample)


_drawn_inputs = setup_inputs


def setup_inputs(seed=0):
    import zlib

    import numpy as np

    out = dict(_drawn_inputs(seed))
    spreads = {}
    factors = {'d_skip': 14.124,
     'b_spatial': 14.902,
     'b_router_group': 26.512,
     'b_router_expert': 25.342,
     'norm_ple': 17.588,
     'norm_pg': 33.806,
     'ssd_norm': 3.74,
     'norm_ffn': 3.383}
    for name, (base, spread) in spreads.items():
        noise = np.random.default_rng([zlib.crc32(name.encode()), seed]).standard_normal(out[name].shape)
        drawn = base * np.exp(spread * noise) if base else spread * noise
        out[name] = __import__('jax').numpy.asarray(drawn.astype(out[name].dtype))
    for name, factor in factors.items():
        out[name] = (out[name] * factor).astype(out[name].dtype)
    return out
```

```python
from contextlib import ExitStack

import concourse.bass as bass
from concourse import mybir

F32 = mybir.dt.float32
I32 = mybir.dt.int32
U32 = mybir.dt.uint32
F32R = mybir.dt.float32r
ACT = mybir.ActivationFunctionType
ALU = mybir.AluOpType
AX = mybir.AxisListType

P = 128
BANK = 512
BIG = 1.0e30
TINY = 1.0e-30
EPS = 1e-6


class Own:

    def __init__(self, eng, sem):
        self.eng, self.sem, self.n = eng, sem, 0

    def did(self, instruction):
        instruction.then_inc(self.sem, 1)
        self.n += 1
        return self.n

    def wait(self, n=None):
        self.eng.wait_ge(self.sem, self.n if n is None else n)

    def restart(self):
        self.wait()
        self.eng.sem_clear(self.sem)
        self.n = 0


def build(nc, i, o):
    D = i["x_prompt"].shape[2]
    SEQ = i["x_prompt"].shape[1]
    NSEQ, NTOK = i["x_sample"].shape[0], i["x_sample"].shape[1]
    S = NSEQ * NTOK
    KC = D // P
    NT = SEQ // P
    TILES = NT + 1
    IN = i["w_in"].shape[2]
    HEADS = i["dt_bias"].shape[1]
    SSD = i["ssd_norm"].shape[1]
    HP = SSD // HEADS
    N = i["state_ssm"].shape[4]
    CONV = i["conv_w"].shape[2]
    TAPS = i["conv_w"].shape[1]
    GROUPS = (CONV - SSD) // (2 * N)
    GW = SSD // GROUPS
    GH = HEADS // GROUPS
    GM = i["gmlp_norm"].shape[1]
    GMH = i["w_spatial"].shape[1]
    GMD = GM // GMH
    NG = i["w_router_group"].shape[2]
    NE = i["w_router_expert"].shape[2]
    EPG = NE // NG
    DE = i["w_gate"].shape[3]
    DC = DE // P
    PLE = i["w_ple"].shape[1]
    PC = PLE // P
    XC = SSD // P
    CC = CONV // P
    MAXB = -(-(SEQ + S) // P)
    ROUTED = 2 * (SEQ + S)
    BLOCKS = (ROUTED + NE * (P - 1)) // P
    assert (D, SSD, GM, DE) == (2 * BANK, BANK, BANK, BANK) and KC == CC == 8
    Z0, X0, DT0, U0, V0 = 0, SSD, SSD + CONV, SSD + CONV + HEADS, SSD + CONV + HEADS + GM

    with ExitStack() as ctx:
        def sb(name, shape, dt=F32):
            return ctx.enter_context(nc.sbuf_tensor(name, shape, dt))

        made = {}

        def s(name):
            if name not in made:
                made[name] = ctx.enter_context(nc.semaphore(name))
            return made[name]

        bank = [ctx.enter_context(nc.psum_tensor(f"bank{n}", [P, BANK], F32)) for n in range(8)]

        ident = sb("ident", [P, P])
        incl = sb("incl", [P, P])
        strict = sb("strict", [P, P])
        ones = sb("ones", [P, P])
        seq_cols = sb("seq_cols", [S, NSEQ])
        incl_s = sb("incl_s", [S, S])
        strict_s = sb("strict_s", [S, S])
        NROWS = KC * 3 + (TAPS + 1) * CC + XC + GMH
        cols = sb("cols", [P, NROWS])
        c_mix, c_ffn, c_pg, c_cw, c_cb = 0, KC, 2 * KC, 3 * KC, 3 * KC + TAPS * CC
        c_ssd = c_cb + CC
        c_bs = c_ssd + XC
        heads3 = sb("heads3", [P, 3, HEADS])
        bias_r = sb("bias_r", [P, NG + NE])
        bs_s = sb("bs_s", [S, GMH])
        logits = sb("logits", [P, TILES, NG + NE])
        small = sb("small", [P, 160])
        half_neg = sb("half_neg", [P, 4])
        norm_c = sb("norm_c", [P, 2])
        gates = sb("gates", [P, 2, TILES])
        slots_u = sb("slots_u", [P, 2, TILES], U32)
        TB = BLOCKS + MAXB
        token_u = sb("token_u", [P, TB], U32)
        plan_u = sb("plan_u", [P, 2 * NE + 1], U32)
        index_u = sb("index_u", [P, 2], U32)
        arena = -(-nc.sbuf_base // 32) * 32

        def placed(name, at, width, dt=F32):
            assert arena + at + 4 * width <= nc.sbuf_usable_end, (name, arena + at + 4 * width)
            return nc.alloc_sbuf_tensor_at(name, [P, width], dt, offset=arena + at)

        WORK = 12584
        h = placed("h", 0, TILES * D)
        A0 = 4 * TILES * D
        weights = placed("weights", A0, KC * IN + KC * D)
        work = placed("work", A0 + 4 * (KC * IN + KC * D), WORK)
        tail = A0 + 4 * (KC * IN + KC * D + WORK)
        gm_row = placed("gm_row", tail, GM)
        w_r = placed("w_r", tail + 4 * GM, KC * (NG + NE))[:, :].rearrange("p (k n) -> p k n", k=KC)
        tail += 4 * GM + 4 * KC * (NG + NE)
        conv_old = placed("conv_old", tail, CC * NSEQ * (TAPS - 1))[:, :].rearrange("p (c q) -> p c q", c=CC)
        tail += 4 * CC * NSEQ * (TAPS - 1)
        wsn = placed("wsn", tail + 4 * NSEQ * S, GMH * S)[0:S, :]
        seq_rows = placed("seq_rows", tail, NSEQ * S)[:, :].rearrange(
            "p (b l) -> p b l", b=NSEQ)
        GU, DN = KC * 2 * DE, DC * D
        HE = DE // 2
        raw_gu = [placed(f"raw_gu{q}", A0 + 2 * GU * q, GU // 2)[:, :].rearrange("p (k w n) -> p k w n", k=KC, w=2) for q in range(2)]
        B0 = A0 + 4 * GU
        w_hi, w_lo = placed("w_hi", B0, GU + DN, F32R), placed("w_lo", B0 + 4 * (GU + DN), GU + DN, F32R)
        B1 = B0 + 8 * (GU + DN)
        raw_d = placed("raw_d", B1, DN)[:, :].rearrange("p (k n) -> p k n", k=DC)
        B2 = B1 + 4 * DN
        xh = placed("xh", B2, D, F32R)[:, :].rearrange("p (k t) -> p k t", k=KC)
        xl = placed("xl", B2 + 4 * D, D, F32R)[:, :].rearrange("p (k t) -> p k t", k=KC)
        hid_hi = placed("hid_hi", B2 + 8 * D, DE, F32R)[:, :].rearrange("p (k t) -> p k t", k=DC)
        hid_lo = placed("hid_lo", B2 + 8 * D + 4 * DE, DE, F32R)[:, :].rearrange("p (k t) -> p k t", k=DC)
        B3 = B2 + 8 * D + 8 * DE
        xg = placed("xg", B3, D)[:, :]
        yb = placed("yb", B3 + 4 * D, D)[:, :]
        sg = placed("sg", B3 + 8 * D, DE)[:, :]
        R0 = B2
        CW = 10800
        work_r = placed("work_r", R0, 5632)
        work_c = placed("work_c", B0, CW)
        w_pg = placed("w_pg", A0, KC * D)[:, :].rearrange("p (k n) -> p k n", k=KC)
        w_ple = placed("w_ple", B1, PC * D)[:, :].rearrange("p (k n) -> p k n", k=PC)
        gu_hi, gu_lo = (w[:, 0:GU].rearrange("p (k w n) -> p k w n", k=KC, w=2) for w in (w_hi, w_lo))
        d_hi, d_lo = (w[:, GU:].rearrange("p (k n) -> p k n", k=DC) for w in (w_hi, w_lo))
        STEPS = 2 * KC + DC
        SPLITS = {"A0": range(KC // 2), "A1": range(KC // 2, KC), "B": range(KC, 2 * KC), "D0": range(2 * KC, 2 * KC + DC // 2),
                  "D1": range(2 * KC + DC // 2, STEPS)}

        m_rows = nc.dram_tensor("m_rows", [SEQ + S, D], F32, kind="Internal").ap()
        y_rows = nc.dram_tensor("y_rows", [TB * P, D], F32, kind="Internal").ap()

        def carver(tensor, size):
            at = [0]

            def carve(width):
                at[0] += width
                assert at[0] <= size, at[0]
                return tensor[:, at[0] - width:at[0]]
            return carve

        carve = carver(work, WORK)
        xn = carve(D)
        aT = carve(D).rearrange("p (k t) -> p k t", k=KC)
        raw = carve(CONV)
        acc = raw.rearrange("p (c t) -> p c t", c=CC)
        convin = carve(CC * (P + TAPS - 1)).rearrange("p (c t) -> p c t", c=CC)
        xcT = carve(CONV).rearrange("p (c t) -> p c t", c=CC)
        mixA = carve(HEADS * P)
        dec = mixA.rearrange("p (h t) -> p h t", h=HEADS)
        mT = mixA.rearrange("p (k t) -> p k t", k=KC)
        cat = carve(D)
        catT = carve(D).rearrange("p (k t) -> p k t", k=KC)
        wsT = carve(GMH * P).rearrange("p (h t) -> p h t", h=GMH)
        bt = carve(GROUPS * N)
        vv, xdt, xwd, yy, state = (carve(SSD) for _ in range(5))
        zs, uu = cat[:, 0:SSD], cat[:, SSD:]
        cbm = carve(GROUPS * P).rearrange("p (g t) -> p g t", g=GROUPS)
        ws_s = carve(GMH * S).rearrange("p (h t) -> p h t", h=GMH)

        w_in = weights[:, 0:KC * IN].rearrange("p (k n) -> p k n", k=KC)
        w_out = weights[:, KC * IN:].rearrange("p (k n) -> p k n", k=KC)
        SN = XC * NSEQ * N
        carve = carver(weights, KC * IN)
        carve(GU)
        s_nat = carve(SN).rearrange("p (c b n) -> p c b n", c=XC, b=NSEQ)
        s_tr = carve(SN).rearrange("p (b m) -> p b m", b=NSEQ)
        ctm = carve(GROUPS * NSEQ * S).rearrange("p (g b t) -> p g b t", g=GROUPS, b=NSEQ)
        bmm = carve(GROUPS * NSEQ * N)[0:S, :].rearrange("p (g b n) -> p g b n", g=GROUPS, b=NSEQ)
        dax = carve(SSD)[0:S, :]
        final_sb = carve(SSD)
        conv_s = convin.rearrange("p c t -> p (c t)")[:, 0:CC * NSEQ * (NTOK + TAPS - 1)].rearrange(
            "p (c b t) -> p c b t", c=CC, b=NSEQ)

        ssx, ssh, ssv, ssy = small[:, 0:1], small[:, 1:2], small[:, 2:3], small[:, 4:6]
        vx, vh, vvv, vy = small[:, 6:7], small[:, 7:8], small[:, 8:9], small[:, 10:12]
        rx, rh, rv, ry = small[:, 12:13], small[:, 13:14], small[:, 14:15], small[:, 16:18]
        xsp, nab, ex, ln1, dd, rd, dtv, da = (small[:, 24 + 8 * n:32 + 8 * n] for n in range(8))
        ecum = small[:, 88:112]
        edcol = small[:, 112:144].rearrange("p (c b) -> p c b", c=XC)

        def bc(ap, *shape):
            while len(ap.shape) < len(shape):
                ap = ap.unsqueeze(len(ap.shape))
            return ap.to_broadcast(list(shape))

        def rows(t):
            return S if isinstance(t, int) and t == NT else P

        def hrow(t):
            return h[0:rows(t), bass.ds(t * D, D)]

        def hhalf(t, half):
            return h[0:rows(t), bass.ds(t * D + half * BANK, BANK)]

        carve = carver(work_c, CW)
        ya, y2 = carve(D), carve(D)
        p_in, pT = carve(PLE), carve(PLE).rearrange("p (k t) -> p k t", k=PC)
        en, an, gate, yout, ple_row, fin_row = (carve(D) for _ in range(6))
        anT = carve(D).rearrange("p (k t) -> p k t", k=KC)

        carve = carver(work_r, 5632)
        R = {}
        for name, w in (("eg", TILES * NG), ("og", TILES * NG), ("leg", TILES * EPG), ("tmp", TILES * NE), ("o1", TILES * EPG),
                        ("o2", TILES * EPG), ("h1", TILES * NE), ("h2", TILES * NE), ("h12", TILES * NE), ("rank", TILES * NE),
                        ("vec", 16 * TILES), ("cnt", NE), ("base", NE), ("end", NE), ("run", NE), ("big", max(NE * MAXB, BLOCKS * NE, TILES * BLOCKS)),
                        ("iota", P), ("tok", TILES), ("blk", 2 * TILES), ("mod", 2 * TILES), ("pos", 2 * TILES),
                        ("hs0", P), ("hs1", P), ("hb0", BLOCKS), ("hb1", BLOCKS), ("valid", TILES)):
            R[name] = carve(w)
        oh12 = R["h12"]
        hot_slot, hot_block = [R["hs0"], R["hs1"]], [R["hb0"], R["hb1"]]

        sse = small[:, 144:146]
        ssc, ssf = small[:, 146:147], small[:, 147:148]
        vc, ve, vf = small[:, 148:149], small[:, 149:150], small[:, 150:151]
        rc, re_, rf = small[:, 151:152], small[:, 152:153], small[:, 153:154]

        def blocks_in_all(eng):
            first = eng.value_load(plan_u[0:1, NE - 1:NE], min_val=0, max_val=BLOCKS - 1)
            return eng.snap(first + eng.value_load(plan_u[0:1, 2 * NE - 1:2 * NE], min_val=1, max_val=MAXB))

        def each_block(eng, one_block):
            eng.wait_ge(s("plan_ready"), 1)

            def expert(e, more):
                first = eng.value_load(plan_u[0:1, bass.ds(e, 1)], min_val=0, max_val=BLOCKS - 1)
                count = eng.value_load(plan_u[0:1, bass.ds(e + NE, 1)], min_val=1, max_val=MAXB)
                with eng.If(count > 1):
                    with eng.Fori(0, eng.snap(count - 1)) as j:
                        one_block(eng.snap(first + j), e, False, True)
                one_block(eng.snap(first + count - 1), e, more, more)

            with eng.Fori(0, NE - 1) as e:
                expert(e, True)
            expert(NE - 1, False)

        block = ctx.enter_context(nc.Block())

        @block.sync
        def _(sp):
            sp.dma_start(h[:, 0:D], i["x_prompt"][0, 0:P, :]).then_inc(s("x0_loaded"), 16)
            rowsT = work[0:NROWS, 0:P]
            for at, src in ((c_mix, i["norm_mix"].rearrange("o (c p) -> (o c) p", p=P)),
                            (c_ffn, i["norm_ffn"].rearrange("o (c p) -> (o c) p", p=P)),
                            (c_pg, i["norm_pg"].rearrange("o (c p) -> (o c) p", p=P)),
                            (c_cw, i["conv_w"].rearrange("o j (c p) -> (o j c) p", p=P)),
                            (c_cb, i["conv_b"].rearrange("o (c p) -> (o c) p", p=P)),
                            (c_ssd, i["ssd_norm"].rearrange("o (c p) -> (o c) p", p=P)),
                            (c_bs, i["b_spatial"][0])):
                sp.dma_start(rowsT[at:at + src.shape[0], :], src).then_inc(s("rows_loaded"), 16)
            w_src = i["w_in"][0].rearrange("(k p) n -> p k n", p=P)
            sp.dma_start(w_in[:, :, Z0:X0], w_src[:, :, Z0:X0]).then_inc(s("w_z_loaded"), 16)
            sp.dma_start(w_in[:, :, X0:X0 + BANK], w_src[:, :, X0:X0 + BANK]).then_inc(s("w_x_loaded"), 16)
            sp.dma_start(w_in[:, :, X0 + BANK:DT0], w_src[:, :, X0 + BANK:DT0]).then_inc(s("w_bc_loaded"), 16)
            sp.dma_start(w_in[:, :, DT0:U0], w_src[:, :, DT0:U0]).then_inc(s("w_dt_loaded"), 16)
            sp.dma_start(w_in[:, :, U0:IN], w_src[:, :, U0:IN]).then_inc(s("w_uv_loaded"), 16)
            sp.dma_start(h[:, D:NT * D].rearrange("p (t n) -> p t n", n=D),
                         i["x_prompt"][0, P:SEQ, :].rearrange("(t p) n -> p t n", p=P)).then_inc(s("x_loaded"), 16)
            sp.dma_start(h[0:S, NT * D:], i["x_sample"].rearrange("b t n -> (b t) n")).then_inc(s("x_loaded"), 16)
            sp.dma_start(w_out[:, :, :], i["w_out"][0].rearrange("(k p) n -> p k n", p=P)).then_inc(s("w_out_loaded"), 16)

            def m_store(t, n):
                sp.wait_ge(s("m_ready"), n)
                sp.dma_start(m_rows[bass.ds(t * P, rows(t)), :], xn[0:rows(t), :]).then_inc(s("m_stored"), 16)

            with sp.Fori(1, NT - 1) as t:
                m_store(t - 1, t)
            sp.wait_ge(s("raw0_ready"), NT)
            sp.wait_ge(s("raw1_ready"), NT)
            sp.dma_start(o["conv_p"][0, 0], raw[P - TAPS + 1:P, :]).then_inc(s("conv_stored"), 16)
            m_store(NT - 2, NT - 1)
            sp.wait_ge(s("raw0_ready"), TILES)
            sp.wait_ge(s("raw1_ready"), TILES)
            for b in range(NSEQ):
                lo = b * NTOK + NTOK - TAPS + 1
                sp.dma_start(o["conv_s"][0, b], raw[lo:b * NTOK + NTOK, :]).then_inc(s("conv_stored"), 16)
            def gate_up(e, q, done):
                if done is not None:
                    sp.wait_ge(s("w_split"), done)
                for w, name in enumerate(("w_gate", "w_up")):
                    sp.dma_start(raw_gu[q][:, :, w, :], i[name][0, bass.ds(e, 1), :, q * HE:(q + 1) * HE].rearrange(
                        "o (k p) n -> p (o k) n", p=P)).then_inc(s(f"gu{q}_loaded"), 16)

            def down(e, done):
                if done is not None:
                    sp.wait_ge(s("w_split"), done)
                sp.dma_start(raw_d, i["w_down"][0, bass.ds(e, 1)].rearrange("o (k p) n -> p (o k) n", p=P)).then_inc(s("d_loaded"), 16)

            sp.wait_ge(s("v_done"), TILES)
            for c in range(XC):
                sp.dma_start(s_nat[:, c], i["state_ssm"][0].rearrange("b (c a) p n -> (a p) c b n", c=XC)[:, c]
                             ).then_inc(s("states_loaded"), 16)
            gate_up(0, 0, None)
            gate_up(0, 1, None)
            m_store(NT - 1, NT)
            sp.wait_ge(s("vn_ready"), TILES)
            sp.dma_start(o["v_s"].rearrange("o b t n -> (o b t) n"), vv[0:S, :]).then_inc(s("out_stored"), 16)
            sp.wait_ge(s("final_ready"), 1)
            sp.dma_start(o["ssm_p"][0, 0].rearrange("(c a) p n -> (a p) c n", c=XC),
                         final_sb.rearrange("p (c n) -> p c n", c=XC)).then_inc(s("out_stored"), 16)
            for c in range(XC):
                sp.wait_ge(s("s_new"), 2 * (c + 1))
                sp.dma_start(o["ssm_s"][0].rearrange("b (c a) p n -> (a p) c b n", c=XC)[:, c], s_nat[:, c]
                             ).then_inc(s("ssm_stored"), 16)
            m_store(NT, TILES)

            sp.wait_ge(s("out_done"), TILES)
            sp.wait_ge(s("ssm_stored"), 16 * XC)
            sp.wait_ge(s("lg_done"), TILES)
            down(0, None)
            sp.wait_ge(s("plan_ready"), 1)
            total = blocks_in_all(sp)
            unused = sp.value_load(plan_u[0:1, 2 * NE:], min_val=0, max_val=BLOCKS - NE)
            sp.sem_inc(s("unused_filled"), 16)
            with sp.If(unused > 0):
                with sp.Fori(0, unused) as j:
                    sp.dma_start(y_rows[bass.ds((BLOCKS - 1 - j) * P, P), :].rearrange("p (k n) -> p k n", n=P),
                                 ones[:, :].unsqueeze(1).to_broadcast([P, KC, P])).then_inc(s("unused_filled"), 16)
            with sp.Fori(1, NE) as e:
                done = sp.snap(STEPS * e)
                gate_up(e, 0, sp.snap(done - KC - DC))
                gate_up(e, 1, sp.snap(done - DC))
                down(e, done)
            sp.wait_ge(s("w_split"), STEPS * NE)
            sp.dma_start(w_pg, i["w_pg"][0].rearrange("(k p) n -> p k n", p=P)).then_inc(s("w_pg_loaded"), 16)
            sp.dma_start(w_ple, i["w_ple"][0].rearrange("(k p) n -> p k n", p=P)).then_inc(s("w_ple_loaded"), 16)
            sp.wait_ge(s("unused_filled"), sp.snap(16 * unused + 16))
            sp.sem_inc(s("blocks_over"), 1)
            sp.wait_ge(s("y_stored"), sp.snap(16 * total + 16))
            sp.sem_inc(s("blocks_over"), 1)
            sp.wait_ge(s("down_done"), total)
            sp.dma_start(ple_row, i["norm_ple"].partition_broadcast(P).rearrange("q o n -> q (o n)")).then_inc(s("c_rows_loaded"), 16)
            sp.dma_start(fin_row, i["norm_final"].partition_broadcast(P)).then_inc(s("c_rows_loaded"), 16)

            def p_load(t, n, prev):
                if prev is not None:
                    sp.wait_ge(s("pTp_done"), prev)
                src = i["p_sample"][0].rearrange("b t n -> (b t) n") if rows(t) == S else i["p_prompt"][0, 0, bass.ds(t * P, P), :]
                sp.dma_start(p_in[0:rows(t), :], src).then_inc(s("p_loaded"), 16)

            def out_store(t, n):
                sp.wait_ge(s("yout_ready"), n)
                dst = o["y_s"].rearrange("b t n -> (b t) n") if rows(t) == S else o["y_p"][0, bass.ds(t * P, P), :]
                sp.dma_start(dst, yout[0:rows(t), :]).then_inc(s("y_out_stored"), 16)

            p_load(0, 1, None)
            p_load(1, 2, 1)
            with sp.Fori(1, NT - 1) as t:
                n = sp.snap(t + 1)
                p_load(n, t, n)
                out_store(t - 1, t)
            p_load(NT, TILES, NT)
            out_store(NT - 2, NT - 1)
            out_store(NT - 1, NT)
            out_store(NT, TILES)
            sp.wait_ge(s("y_out_stored"), 16 * TILES)
            sp.wait_ge(s("out_stored"), 32)
            sp.wait_ge(s("conv_stored"), 16 * (1 + NSEQ))
            sp.wait_ge(s("m_stored"), 16 * TILES)

        @block.tensor
        def _(pe):
            def product(out, lhs, rhs, ks):
                for k in ks:
                    last = nc.tensor.matmul(out, lhs(k), rhs(k), start=(k == ks[0]), stop=(k == ks[-1]))
                return last

            def transposes(src, T, lo, hi, out, w=P):
                for c in range(lo, hi):
                    last = nc.tensor.transpose(out[:, (c - lo) * P:(c - lo) * P + T], src[0:T, c * P:c * P + w], ident[0:T, 0:T])
                return last

            pe.wait_ge(s("ident_ready"), 1)
            pe.wait_ge(s("rows_loaded"), 16 * 7)
            nc.tensor.transpose(bank[0][:, 0:NROWS], work[0:NROWS, 0:P], ident[0:NROWS, 0:NROWS]).then_inc(s("cols_done"), 1)
            Q = NSEQ * (TAPS - 1)
            pe.wait_ge(s("conv_old_loaded"), 16)
            for c in range(CC):
                last = nc.tensor.transpose(bank[1][:, c * Q:(c + 1) * Q], h[32:32 + Q, NT * D + c * P:NT * D + (c + 1) * P],
                                           ident[32:32 + Q, 32:32 + Q])
            last.then_inc(s("conv_old_done"), 1)
            pe.wait_ge(s("ws_loaded"), 16)
            wn = cat.rearrange("p (h t) -> p h t", h=GMH)
            for hh in range(GMH):
                last = nc.tensor.transpose(bank[2 + hh // 4][:, (hh % 4) * P:(hh % 4 + 1) * P], wn[:, hh, :], ident[:, :])
                if hh % 4 == 3:
                    last.then_inc(s("wsT_done"), 1)

            def x_transposes(t, n):
                T = rows(t)
                pe.wait_ge(s("xn_ready"), n)
                transposes(xn, T, 0, 4, bank[5])
                transposes(xn, T, 4, 8, bank[6]).then_inc(s("aTp_done"), 1)

            def cat_transposes(t, n):
                T = rows(t)
                pe.wait_ge(s("cat_ready"), n)
                transposes(cat, T, 0, 4, bank[4]).then_inc(s("catTp0_done"), 1)
                transposes(cat, T, 4, 8, bank[5]).then_inc(s("catTp1_done"), 1)

            def out_product(t, n, bank7_free):
                T = rows(t)
                pe.wait_ge(s("catT0_ready"), n)
                pe.wait_ge(s("catT1_ready"), n)
                pe.wait_ge(*bank7_free)
                for half in range(2):
                    last = product(bank[6 + half][0:T, :], lambda k: catT[:, k, 0:T],
                                   lambda k: w_out[:, k, half * BANK:(half + 1) * BANK], range(KC))
                last.then_inc(s("out_done"), 1)

            def m_transposes(t, n):
                T = rows(t)
                pe.wait_ge(s("m_ready"), n)
                transposes(xn, T, 0, 4, bank[0])
                transposes(xn, T, 4, 8, bank[1]).then_inc(s("mTp_done"), 1)

            def router(t, n):
                T = rows(t)
                pe.wait_ge(s("mT_ready"), n)
                product(bank[3][0:T, 0:NG + NE], lambda k: mT[:, k, 0:T], lambda k: w_r[:, k, :], range(KC)).then_inc(s("lg_done"), 1)

            def z_product(t, n):
                T = rows(t)
                pe.wait_ge(s("aT_ready"), n)
                product(bank[2][0:T, :], lambda k: aT[:, k, 0:T], lambda k: w_in[:, k, Z0:Z0 + BANK], range(KC)).then_inc(s("z_done"), 1)

            def tile(t, n, p):
                T = rows(t)
                sample = T == S
                first = isinstance(t, int) and t == 0
                proj = lambda out, c0, w: product(out, lambda k: aT[:, k, 0:T], lambda k: w_in[:, k, c0:c0 + w], range(KC))
                if first:
                    pe.wait_ge(s("w_x_loaded"), 16)
                    pe.wait_ge(s("cols_ready"), 1)
                    pe.wait_ge(s("conv_old_ready"), 1)
                else:
                    pe.wait_ge(s("decay_ready"), p)
                proj(bank[0][0:T, :], X0, BANK).then_inc(s("xb_done"), 1)
                if first:
                    pe.wait_ge(s("w_bc_loaded"), 16)
                proj(bank[1][0:T, :], X0 + BANK, BANK).then_inc(s("bc_done"), 1)
                if not first:
                    cat_transposes(t - 1, p)
                pe.wait_ge(s("raw0_ready"), n)
                pe.wait_ge(s("raw1_ready"), n)
                transposes(raw, T, 0, 4, bank[0])
                transposes(raw, T, 4, 8, bank[1]).then_inc(s("rawT_done"), 1)
                if first:
                    pe.wait_ge(s("w_dt_loaded"), 16)
                else:
                    pe.wait_ge(s("bt_ready"), p)
                proj(bank[3][0:T, 0:HEADS], DT0, HEADS).then_inc(s("dt_done"), 1)
                if not first:
                    out_product(t - 1, p, (s("state_ready"), n))
                else:
                    pe.wait_ge(s("w_uv_loaded"), 16)
                pe.wait_ge(s("z_ready"), n)
                proj(bank[2][0:T, :], U0, BANK).then_inc(s("u_done"), 1)
                proj(bank[4][0:T, :], V0, BANK).then_inc(s("v_done"), 1)
                if not first:
                    pe.wait_ge(s("h_ready"), p)
                else:
                    pe.wait_ge(s("w_out_loaded"), 16)
                if not sample:
                    x_transposes(t + 1, (t + 2) if isinstance(t, int) else n + 1)
                mk_i, mk_s = (incl_s, strict_s) if sample else (incl, strict)
                pe.wait_ge(s("dam_ready"), n)
                pe.wait_ge(s("convin_ready"), n)
                for half in range(2):
                    last = nc.tensor.matmul(bank[half].rearrange("p (h t) -> p h t", h=4)[0:T, :, 0:T], mk_s[0:T, 0:T],
                                            dec[0:T, 4 * half:4 * half + 4, 0:T], start=True, stop=True)
                last.then_inc(s("seg_done"), 1)
                nc.tensor.matmul(bank[3][0:T, 0:HEADS], mk_i[0:T, 0:T], da[0:T, :], start=True, stop=True)
                last = nc.tensor.matmul(bank[3][0:T, HEADS:2 * HEADS], mk_s[0:T, 0:T], da[0:T, :], start=True, stop=True)
                if not sample:
                    last = nc.tensor.matmul(bank[3][0:T, 2 * HEADS:3 * HEADS], ones[0:T, 0:T], da[0:T, :], start=True, stop=True)
                else:
                    for c in range(XC):
                        last = nc.tensor.matmul(bank[3][:, 32 + NSEQ * c:32 + NSEQ * (c + 1)], dax[0:T, c * P:(c + 1) * P],
                                                seq_cols[:, :], start=True, stop=True)
                last.then_inc(s("cum_done"), 1)
                pe.wait_ge(s("xc_ready"), n)
                for c in range(XC):
                    last = nc.tensor.transpose(bank[7][0:T, c * P:(c + 1) * P], xcT[:, c, 0:T], ident[:, :])
                last.then_inc(s("xtok_done"), 1)
                pe.wait_ge(s("u_ready"), n)
                for g in range(GROUPS):
                    last = nc.tensor.matmul(bank[2][0:T, g * P:g * P + T], xcT[:, XC + g, 0:T], xcT[:, XC + GROUPS + g, 0:T],
                                            start=True, stop=True)
                last.then_inc(s("cb_done"), 1)
                pe.wait_ge(s("ecum_ready"), n)
                for g in range(GROUPS):
                    last = nc.tensor.transpose(bank[3][0:T, g * N:(g + 1) * N], xcT[:, XC + g, 0:T], ident[:, :])
                last.then_inc(s("bt_done"), 1)
                if not sample:
                    pe.wait_ge(s("aT_ready"), (t + 2) if isinstance(t, int) else n + 1)
                pe.wait_ge(s("vn_ready"), n)
                if sample:
                    pe.wait_ge(s("ws_s_ready"), 1)
                for hh in range(GMH):
                    last = nc.tensor.matmul(bank[6][0:T, hh * GMD:(hh + 1) * GMD], (ws_s[0:S, hh, :] if sample else wsT[:, hh, :]),
                                            vv[0:T, hh * GMD:(hh + 1) * GMD], start=True, stop=True)
                last.then_inc(s("gm_done"), 1)
                if sample:
                    pe.wait_ge(s("states_loaded"), 16 * XC)
                    pe.wait_ge(s("xw_ready"), n)
                    for b in range(NSEQ):
                        if b >= 2:
                            pe.wait_ge(s("s_tr_ready"), b - 1)
                        for c in range(XC):
                            last = nc.tensor.transpose(bank[5 + 2 * (b % 2)][:, c * P:(c + 1) * P], s_nat[:, c, b, :], ident[:, :])
                        last.then_inc(s("s_trp_done"), 1)
                    pe.wait_ge(s("s_tr_ready"), NSEQ)
                    pe.wait_ge(s("ctm_ready"), 1)
                    for g in range(GROUPS):
                        last = product(bank[5][0:T, g * GW:(g + 1) * GW], lambda b: ctm[:, g, b, :],
                                       lambda b: s_tr[:, b, g * GW:(g + 1) * GW], range(NSEQ))
                else:
                    pe.wait_ge(s("state_ready"), n)
                    for g in range(GROUPS):
                        last = nc.tensor.matmul(bank[5][0:T, g * GW:(g + 1) * GW], xcT[:, XC + GROUPS + g, 0:T],
                                                state[:, g * GW:(g + 1) * GW], start=True, stop=True)
                last.then_inc(s("yoff_done"), 1)
                pe.wait_ge(s("wts_ready"), n)
                pe.wait_ge(s("v_ready"), n)
                pe.wait_ge(s("xw_ready"), n)
                for hh in range(HEADS):
                    last = nc.tensor.matmul(bank[4][0:T, hh * HP:(hh + 1) * HP], dec[0:T, hh, 0:T], xdt[0:T, hh * HP:(hh + 1) * HP],
                                            start=True, stop=True)
                last.then_inc(s("ydiag_done"), 1)
                pe.wait_ge(s("bt_ready"), n)
                if not sample:
                    for g in range(GROUPS):
                        last = nc.tensor.matmul(bank[7][:, g * GW:(g + 1) * GW], bt[0:T, g * N:(g + 1) * N], xwd[0:T, g * GW:(g + 1) * GW],
                                                start=True, stop=True)
                    last.then_inc(s("cs_done"), 1)
                else:
                    pe.wait_ge(s("bmm_ready"), 1)
                    for j in range(2 * XC):
                        c, q = j // 2, j % 2
                        if j >= 2:
                            pe.wait_ge(s("s_new"), j - 1)
                        else:
                            pe.wait_ge(s("cbm_ready"), n)
                        nc.tensor.matmul(bank[7 if q else 2][:, :], xwd[0:T, c * P:(c + 1) * P],
                                         bmm[:, c * P // GW, 4 * q:4 * q + 4, :].rearrange("p b n -> p (b n)"), start=True, stop=True
                                         ).then_inc(s("cs_s_done"), 1)
                    pe.wait_ge(s("s_new"), 2 * XC)
                    for c in range(XC):
                        last = nc.tensor.transpose(bank[2][:, c * P:(c + 1) * P], state[:, c * P:(c + 1) * P], ident[:, :])
                    last.then_inc(s("finalp_done"), 1)
                if not first:
                    pe.wait_ge(s("decay_ready"), n)
                    m_transposes(t - 1, p)
                if not sample:
                    pe.wait_ge(s("cbm_ready"), n)
                    z_product(t + 1, t + 2 if isinstance(t, int) else pe.snap(n + 1))
                if not first:
                    router(t - 1, p)

            x_transposes(0, 1)
            pe.wait_ge(s("w_z_loaded"), 16)
            pe.wait_ge(s("wsT_ready"), 2)
            z_product(0, 1)
            tile(0, 1, 0)
            pe.wait_ge(s("w_r_ready"), 1)
            with pe.Fori(1, NT - 1) as t:
                tile(t, pe.snap(t + 1), t)
            tile(NT - 1, NT, NT - 1)
            tile(NT, TILES, NT)
            cat_transposes(NT, TILES)
            out_product(NT, TILES, (s("s_new"), 2 * XC))
            m_transposes(NT, TILES)
            pe.wait_ge(s("lg_ready"), NT)
            router(NT, TILES)

            E = TILES * NE
            pe.wait_ge(s("onehot_ready"), 1)
            nc.tensor.matmul(bank[0][:, 0:E], incl[:, :], oh12, start=True, stop=True)
            nc.tensor.matmul(bank[1][:, 0:E], ones[:, :], oh12, start=True, stop=True).then_inc(s("ranks_done"), 1)
            for j in range(2 * TILES):
                pe.wait_ge(s("hot_ready"), j + 1)
                T = rows(j // 2)
                nc.tensor.matmul(bank[2][:, 0:BLOCKS], hot_slot[j % 2][0:T, :], hot_block[j % 2][0:T, :], start=(j == 0),
                                 stop=(j == 2 * TILES - 1)).then_inc(s("hot_used"), 1)

            def product3(out, lh, ll, rh, rl, ks):
                for k in ks:
                    nc.tensor.matmul(out, lh(k), rh(k), start=(k == ks[0]), stop=False)
                    nc.tensor.matmul(out, lh(k), rl(k), start=False, stop=False)
                    last = nc.tensor.matmul(out, ll(k), rh(k), start=False, stop=(k == ks[-1]))
                return last

            def b_rows(gathered):
                pe.wait_ge(s("gathered"), gathered)
                transposes(xg, P, 0, 4, bank[0])
                transposes(xg, P, 4, 8, bank[1]).then_inc(s("xTp_done"), 1)

            def one_block(b, e, splits, more):
                n = pe.snap(b + 1)
                pe.wait_ge(s("xT_ready"), n)
                steps = STEPS * e if isinstance(e, int) else pe.snap(STEPS * e)
                for half in range(2):
                    cols_ = slice(half * HE, (half + 1) * HE)
                    pe.wait_ge(s("w_split"), steps + (half + 1) * KC)
                    for w, name in ((0, "gate_done"), (1, "up_done")):
                        product3(bank[2 + 2 * half + w][:, 0:HE], lambda k: xh[:, k, :], lambda k: xl[:, k, :],
                                 lambda k: gu_hi[:, k, w, cols_], lambda k: gu_lo[:, k, w, cols_], range(KC)).then_inc(s(name), 1)
                pe.wait_ge(s("hid_ready"), pe.snap(2 * n))
                transposes(sg, P, 0, DC, bank[2]).then_inc(s("hTp_done"), 1)
                b_rows(pe.snap(16 * n + 16))
                pe.wait_ge(s("w_split"), steps + STEPS)
                pe.wait_ge(s("bank6_free"), n)
                pe.wait_ge(s("bank7_free"), n)
                pe.wait_ge(s("hidT_ready"), n)
                for half in range(2):
                    done = product3(bank[6 + half][:, :], lambda k: hid_hi[:, k, :], lambda k: hid_lo[:, k, :],
                                    lambda k: d_hi[:, k, half * BANK:(half + 1) * BANK],
                                    lambda k: d_lo[:, k, half * BANK:(half + 1) * BANK], range(DC))
                done.then_inc(s("down_done"), 1)

            b_rows(16)
            each_block(pe, one_block)

            def c_embed(t, n):
                T = rows(t)
                pe.wait_ge(s("p_loaded"), 16 * n if isinstance(n, int) else pe.snap(16 * n))
                transposes(p_in, T, 0, PC, bank[0]).then_inc(s("pTp_done"), 1)
                pe.wait_ge(s("pT_ready"), n)
                for half in range(2):
                    last = product(bank[1 + half][0:T, :], lambda k: pT[:, k, 0:T], lambda k: w_ple[:, k, half * BANK:(half + 1) * BANK],
                                   range(PC))
                last.then_inc(s("ple_done"), 1)

            def c_rows(t, n):
                T = rows(t)
                pe.wait_ge(s("an_ready"), n)
                transposes(an, T, 0, 4, bank[3])
                transposes(an, T, 4, 8, bank[4]).then_inc(s("anTp_done"), 1)

            def c_gate(t, n, p):
                T = rows(t)
                pe.wait_ge(s("anT_ready"), n)
                if p is not None:
                    pe.wait_ge(s("sig_ready"), p)
                for half in range(2):
                    last = product(bank[5 + half][0:T, :], lambda k: anT[:, k, 0:T], lambda k: w_pg[:, k, half * BANK:(half + 1) * BANK],
                                   range(KC))
                last.then_inc(s("pg_done"), 1)

            total1 = pe.snap(blocks_in_all(pe) + 1)
            pe.wait_ge(s("xT_ready"), total1)
            pe.wait_ge(s("bank6_free"), total1)
            pe.wait_ge(s("bank7_free"), total1)
            pe.wait_ge(s("w_pg_loaded"), 16)
            pe.wait_ge(s("w_ple_loaded"), 16)
            c_rows(0, 1)
            c_embed(0, 1)

            def c_tile(t, n, p):
                c_gate(t, n, p)
                if rows(t) != S:
                    n2 = n + 1 if isinstance(n, int) else pe.snap(n + 1)
                    c_rows(t + 1, n2)
                    pe.wait_ge(s("en_ready"), n)
                    c_embed(t + 1, n2)

            c_tile(0, 1, None)
            with pe.Fori(1, NT - 1) as t:
                c_tile(t, pe.snap(t + 1), t)
            c_tile(NT - 1, NT, NT - 1)
            c_tile(NT, TILES, NT)

        @block.vector
        def _(dve):
            V = nc.vector
            own = Own(dve, s("dve_own"))

            dve.wait_ge(s("cols_done"), 1)
            V.tensor_copy(cols[:, :], bank[0][:, 0:NROWS]).then_inc(s("cols_ready"), 1)
            dve.wait_ge(s("conv_old_done"), 1)
            V.tensor_copy(conv_old.rearrange("p c q -> p (c q)"), bank[1][:, 0:CC * NSEQ * (TAPS - 1)]).then_inc(s("conv_old_ready"), 1)
            dve.wait_ge(s("incl_ready"), 1)
            for half in range(2):
                dve.wait_ge(s("wsT_done"), half + 1)
                V.tensor_tensor(wsT[:, 4 * half:4 * half + 4, :], bank[2 + half].rearrange("p (h t) -> p h t", h=4),
                                incl[:, :].unsqueeze(1).to_broadcast([P, 4, P]), ALU.mult).then_inc(s("wsT_ready"), 1)
            own.did(V.memset(state, 0.0))
            dve.wait_ge(s("heads_loaded"), 16 * 3)
            dve.wait_ge(s("ealog_ready"), 1)
            own.did(V.tensor_scalar(heads3[:, 1, :], heads3[:, 1, :], -1.0, None, ALU.mult))
            own.wait()
            V.memset(convin[:, :, 0:TAPS - 1], 0.0).then_inc(s("state_ready"), 1)

            def gain_evict(dst, src_bank, T, c0):
                return V.tensor_tensor(dst[:, :, 0:T], src_bank.rearrange("p (c t) -> p c t", c=4)[:, :, 0:T],
                                       bc(cols[:, c0:c0 + 4], P, 4, T), ALU.mult)

            def aT_evict(t, n):
                dve.wait_ge(s("aTp_done"), n)
                T = rows(t)
                own.did(gain_evict(aT[:, 0:4], bank[5], T, c_mix))
                gain_evict(aT[:, 4:8], bank[6], T, c_mix + 4).then_inc(s("aT_ready"), 1)

            def h_add(t, n):
                T = rows(t)
                dve.wait_ge(s("out_done"), n)
                own.did(V.tensor_tensor(hhalf(t, 0), bank[6][0:T, :], hhalf(t, 0), ALU.add))
                own.wait()
                V.tensor_tensor(hhalf(t, 1), bank[7][0:T, :], hhalf(t, 1), ALU.add).then_inc(s("h_ready"), 1)

            def catT0(t, n):
                T = rows(t)
                dve.wait_ge(s("catTp0_done"), n)
                gain_evict(catT[:, 0:4], bank[4], T, c_ssd).then_inc(s("catT0_ready"), 1)

            def lg_evict(t, n):
                T = rows(t)
                dve.wait_ge(s("lg_done"), n)
                dst = logits[0:T, bass.ds(t, 1), :].rearrange("p o e -> p (o e)")
                V.tensor_tensor(dst, bank[3][0:T, 0:NG + NE], bias_r[0:T, :], ALU.add).then_inc(s("lg_ready"), 1)

            def tile(t, n, p):
                T = rows(t)
                sample = T == S
                first = isinstance(t, int) and t == 0
                last_two = isinstance(t, int) and t >= NT - 1
                dve.wait_ge(s("bc_done"), n)
                V.tensor_copy(raw[0:T, BANK:], bank[1][0:T, :]).then_inc(s("raw1_ready"), 1)
                if not first:
                    catT0(t - 1, p)
                dve.wait_ge(s("rawT_done"), n)
                if sample:
                    own.did(V.tensor_copy(conv_s[:, :, :, 0:TAPS - 1], conv_old.rearrange("p c (b j) -> p c b j", b=NSEQ)))
                elif not first:
                    own.did(V.tensor_copy(convin[:, :, 0:TAPS - 1], convin[:, :, P:P + TAPS - 1]))
                    own.wait()
                for half in range(2):
                    cs = slice(4 * half, 4 * half + 4)
                    if sample:
                        dst = conv_s[:, cs, :, TAPS - 1:]
                        src = bank[half].rearrange("p (c t) -> p c t", c=4)[:, :, 0:T].rearrange("p c (b t) -> p c b t", b=NSEQ)
                    else:
                        dst, src = convin[:, cs, TAPS - 1:], bank[half].rearrange("p (c t) -> p c t", c=4)
                    ins = V.tensor_copy(dst, src)
                    if half == 0:
                        own.did(ins)
                    else:
                        ins.then_inc(s("convin_ready"), 1)
                own.wait()
                dve.wait_ge(s("convin_ready"), n)
                if last_two:
                    dve.wait_ge(s("conv_stored"), 16 if t == NT - 1 else 16 * (1 + NSEQ))
                dve.wait_ge(s("dt_done"), n)
                own.did(V.tensor_tensor(xsp[0:T], bank[3][0:T, 0:HEADS], heads3[0:T, 0, :], ALU.add))
                own.wait()
                V.scalar_tensor_tensor(out=nab[0:T], in0=xsp[0:T], scalar=-1.0, in1=xsp[0:T], op0=ALU.mult, op1=ALU.min).then_inc(s("nab_ready"), 1)
                tap = {}
                for j in range(TAPS):
                    for c in range(CC):
                        w = cols[:, c_cw + j * CC + c:c_cw + j * CC + c + 1]
                        if sample:
                            src = conv_s[:, c, :, j:j + NTOK]
                            dst = acc[:, c, 0:T].rearrange("p (b t) -> p b t", b=NSEQ)
                        else:
                            src, dst = convin[:, c, j:j + P], acc[:, c, :]
                        if j == 0:
                            tap[c] = own.did(V.tensor_scalar(dst, src, w, cols[:, c_cb + c:c_cb + c + 1], ALU.mult, ALU.add))
                        else:
                            own.wait(tap[c])
                            ins = V.scalar_tensor_tensor(out=dst, in0=src, scalar=w, in1=dst, op0=ALU.mult, op1=ALU.add)
                            if j == TAPS - 1 and c % 4 == 3:
                                ins.then_inc(s("conv_ready"), 1)
                            else:
                                tap[c] = own.did(ins)
                dve.wait_ge(s("sp_ready"), n)
                own.did(V.tensor_scalar(dd[0:T], ex[0:T], 1.0, -1.0, ALU.add, ALU.add))
                own.wait()
                own.did(V.tensor_scalar(dd[0:T], dd[0:T], TINY, None, ALU.add))
                own.did(V.scalar_tensor_tensor(out=rd[0:T], in0=ln1[0:T], scalar=TINY, in1=ex[0:T], op0=ALU.add, op1=ALU.mult))
                own.wait()
                own.did(V.reciprocal(dd[0:T], dd[0:T]))
                own.wait()
                own.did(V.tensor_tensor(rd[0:T], rd[0:T], dd[0:T], ALU.mult))
                own.wait()
                own.did(V.scalar_tensor_tensor(out=dtv[0:T], in0=xsp[0:T], scalar=0.0, in1=rd[0:T], op0=ALU.max, op1=ALU.add))
                own.wait()
                own.did(V.tensor_tensor(da[0:T], dtv[0:T], heads3[0:T, 1, :], ALU.mult))
                own.wait()
                if sample:
                    dve.wait_ge(s("v_done"), n)
                    own.did(V.tensor_copy(dax.rearrange("p (h q) -> p h q", h=HEADS), bc(da[0:T], T, HEADS, HP)))
                mk_i = incl_s if sample else incl
                V.tensor_tensor(dec[0:T, :, 0:T], bc(da[0:T], T, HEADS, T), mk_i[0:T, 0:T].unsqueeze(1).to_broadcast([T, HEADS, T]),
                                ALU.mult).then_inc(s("dam_ready"), 1)
                if sample:
                    own.wait()
                if not first:
                    h_add(t - 1, p)
                if not sample:
                    aT_evict(t + 1, (n + 1))
                dve.wait_ge(s("rv_ready"), n)
                V.scalar_tensor_tensor(out=vv[0:T, :], in0=vv[0:T, :], scalar=rv[0:T, :], in1=gm_row[0:T, :], op0=ALU.mult,
                                       op1=ALU.mult).then_inc(s("vn_ready"), 1)
                dve.wait_ge(s("ecum_ready"), n)
                dve.wait_ge(s("xtok_done"), n)
                xt = bank[7][0:T, :].rearrange("p (h q) -> p h q", h=HEADS)
                v3 = lambda ap: ap[0:T, :].rearrange("p (h q) -> p h q", h=HEADS)
                own.did(V.tensor_tensor(v3(xdt), xt, bc(dtv[0:T], T, HEADS, HP), ALU.mult))
                own.did(V.tensor_tensor(v3(yy), xt, bc(heads3[0:T, 2, :], T, HEADS, HP), ALU.mult))
                own.wait()
                V.tensor_tensor(v3(xwd), v3(xdt), bc(ecum[0:T, HEADS:2 * HEADS], T, HEADS, HP), ALU.mult).then_inc(s("xw_ready"), 1)
                dve.wait_ge(s("cb_done"), n)
                V.tensor_tensor(cbm[0:T, :, 0:T], bank[2][0:T, 0:GROUPS * P].rearrange("p (g t) -> p g t", g=GROUPS)[:, :, 0:T],
                                mk_i[0:T, 0:T].unsqueeze(1).to_broadcast([T, GROUPS, T]), ALU.mult).then_inc(s("cbm_ready"), 1)
                dve.wait_ge(s("cbm_ready"), n)
                dve.wait_ge(s("decay_ready"), n)
                for g in range(GROUPS):
                    hs = slice(g * GH, (g + 1) * GH)
                    ins = V.tensor_tensor(dec[0:T, hs, 0:T], dec[0:T, hs, 0:T], cbm[0:T, g, 0:T].unsqueeze(1).to_broadcast([T, GH, T]), ALU.mult)
                    if g == GROUPS - 1:
                        ins.then_inc(s("wts_ready"), 1)
                    else:
                        own.did(ins)
                        own.wait()
                if sample:
                    for g in range(GROUPS):
                        ins = V.tensor_tensor(ctm[:, g, :, :], xcT[:, XC + GROUPS + g, 0:S].unsqueeze(1).to_broadcast([P, NSEQ, S]),
                                              seq_rows[:, :, :], ALU.mult)
                        if g == GROUPS - 1:
                            own.wait()
                            ins.then_inc(s("ctm_ready"), 1)
                        else:
                            own.did(ins)
                    dve.wait_ge(s("bt_ready"), n)
                    for g in range(GROUPS):
                        ins = V.tensor_tensor(bmm[:, g, :, :], bt[0:S, g * N:(g + 1) * N].unsqueeze(1).to_broadcast([S, NSEQ, N]),
                                              bc(seq_cols[:, :], S, NSEQ, N), ALU.mult)
                        if g == GROUPS - 1:
                            ins.then_inc(s("bmm_ready"), 1)
                        else:
                            own.did(ins)
                dve.wait_ge(s("gm_done"), n)
                if not first:
                    dve.wait_ge(s("catTp1_done"), p)
                bcol = bs_s[:, :] if sample else cols[:, c_bs:c_bs + GMH]
                c3 = bank[6][0:T, :].rearrange("p (h q) -> p h q", h=GMH)
                own.did(V.tensor_tensor(c3, c3, bc(bcol[0:T], T, GMH, GMD), ALU.add))
                own.wait()
                own.did(V.tensor_tensor(uu[0:T, :], bank[6][0:T, :], uu[0:T, :], ALU.mult))
                dve.wait_ge(s("yoff_done"), n)
                c3 = bank[5][0:T, :].rearrange("p (h q) -> p h q", h=HEADS)
                own.did(V.tensor_tensor(c3, c3, bc(ecum[0:T, 0:HEADS], T, HEADS, HP), ALU.mult))
                own.wait()
                own.did(V.tensor_tensor(yy[0:T, :], bank[5][0:T, :], yy[0:T, :], ALU.add))
                own.wait()
                dve.wait_ge(s("ydiag_done"), n)
                own.did(V.tensor_tensor(yy[0:T, :], bank[4][0:T, :], yy[0:T, :], ALU.add))
                own.wait()
                own.did(V.tensor_tensor(yy[0:T, :], yy[0:T, :], zs[0:T, :], ALU.mult))
                own.wait()
                for g in range(GROUPS):
                    seg = yy[0:T, g * GW:(g + 1) * GW]
                    ins = V.tensor_tensor_reduce(out=bank[5][0:T, g * GW:(g + 1) * GW], in0=seg, in1=seg, scale=1.0, scalar=0.0, op0=ALU.mult,
                                                 op1=ALU.add, accum_out=ssy[0:T, g:g + 1])
                    own.did(ins)
                own.wait()
                V.tensor_scalar(vy[0:T], ssy[0:T], 1.0 / GW, EPS, ALU.mult, ALU.add).then_inc(s("vy_ready"), 1)
                if not sample:
                    dve.wait_ge(s("cs_done"), n)
                    own.did(V.tensor_tensor(state.rearrange("p (h q) -> p h q", h=HEADS), state.rearrange("p (h q) -> p h q", h=HEADS),
                                            bc(ecum[:, 2 * HEADS:3 * HEADS], P, HEADS, HP), ALU.mult))
                    own.wait()
                    V.tensor_tensor(state, bank[7][:, :], state, ALU.add).then_inc(s("state_ready"), 1)
                else:
                    for j in range(2 * XC):
                        c, q = j // 2, j % 2
                        dst = s_nat[:, c, 4 * q:4 * q + 4, :]
                        dve.wait_ge(s("cs_s_done"), j + 1)
                        own.did(V.tensor_tensor(dst, dst, bc(edcol[:, c, 4 * q:4 * q + 4], P, 4, N), ALU.mult))
                        own.wait()
                        V.tensor_tensor(dst, bank[7 if q else 2].rearrange("p (b n) -> p b n", b=4), dst, ALU.add).then_inc(s("s_new"), 1)
                dve.wait_ge(s("ry_ready"), n)
                V.tensor_tensor(cat[0:T, 0:SSD].rearrange("p (g q) -> p g q", g=GROUPS), yy[0:T, :].rearrange("p (g q) -> p g q", g=GROUPS),
                                bc(ry[0:T], T, GROUPS, GW), ALU.mult).then_inc(s("cat_ready"), 1)
                if not first:
                    lg_evict(t - 1, p)
                own.restart()

            dve.wait_ge(s("gm_row_loaded"), 16)
            aT_evict(0, 1)
            dve.wait_ge(s("w_r_loaded"), 64)
            V.tensor_tensor(w_r, w_r, bc(cols[:, c_ffn:c_ffn + KC], P, KC, NG + NE), ALU.mult).then_inc(s("w_r_ready"), 1)
            tile(0, 1, 0)
            with dve.Fori(1, NT - 1) as t:
                tile(t, dve.snap(t + 1), t)
            tile(NT - 1, NT, NT - 1)
            dve.wait_ge(s("ws_s_loaded"), 16 * NSEQ)
            own.did(V.transpose(ws_s[0:S, :, :].rearrange("p h t -> p (h t)"), wsn))
            own.wait()
            dve.wait_ge(s("seq_ready"), 1)
            own.did(V.tensor_tensor(ws_s[0:S, :, :], ws_s[0:S, :, :], incl_s[:, :].unsqueeze(1).to_broadcast([S, GMH, S]), ALU.mult))
            own.wait()
            dve.wait_ge(s("bs_s_loaded"), 16 * NSEQ)
            V.memset(logits[:, NT, :], 0.0).then_inc(s("ws_s_ready"), 1)
            tile(NT, TILES, NT)
            dve.wait_ge(s("finalp_done"), 1)
            V.tensor_copy(final_sb, bank[2][:, :]).then_inc(s("final_ready"), 1)
            catT0(NT, TILES)
            h_add(NT, TILES)
            lg_evict(NT, TILES)

            dve.wait_ge(s("lg_ready"), TILES)
            dve.wait_ge(s("out_done"), TILES)
            def step(ins):
                own.did(ins)
                own.wait()
            g3 = lambda k, e: R[k].rearrange("p (t e) -> p t e", t=TILES)
            vec = [R["vec"][:, n * TILES:(n + 1) * TILES] for n in range(16)]
            lgr, ler = logits[:, :, 0:NG], logits[:, :, NG:]
            eg, og, leg, o1, o2 = (g3(k, 0) for k in ("eg", "og", "leg", "o1", "o2"))
            h1, h2, h12 = (R[k].rearrange("p (t g e) -> p t g e", t=TILES, g=NG) for k in ("h1", "h2", "h12"))

            def pick(values, out, W):
                step(V.tensor_reduce(vec[0], values, AX.X, ALU.max))
                step(V.tensor_tensor(out, values, bc(vec[0], P, TILES, W), ALU.is_equal))
                step(V.memset(vec[1], 1.0))
                for j in range(W):
                    col = out[:, :, j:j + 1].rearrange("p t o -> p (t o)")
                    step(V.tensor_tensor(col, col, vec[1], ALU.mult))
                    step(V.tensor_tensor(vec[1], vec[1], col, ALU.subtract))

            dve.wait_ge(s("iota_ready"), 1)
            pick(lgr, og, NG)
            step(V.tensor_tensor(eg, lgr, bc(vec[0], P, TILES, NG), ALU.subtract))
            V.tensor_copy(eg, eg).then_inc(s("eg_ready"), 1)
            tmp = R["tmp"].rearrange("p (t g e) -> p t g e", t=TILES, g=NG)
            step(V.tensor_tensor(tmp, ler.rearrange("p t (g e) -> p t g e", g=NG), bc(og, P, TILES, NG, EPG), ALU.mult))
            step(V.tensor_reduce(leg, tmp.rearrange("p t g e -> p t e g"), AX.X, ALU.add))
            pick(leg, o1, EPG)
            step(V.tensor_copy(vec[2], vec[0]))
            step(V.scalar_tensor_tensor(out=leg, in0=o1, scalar=-BIG, in1=leg, op0=ALU.mult, op1=ALU.add))
            pick(leg, o2, EPG)
            V.tensor_tensor(vec[3], vec[0], vec[2], ALU.subtract).then_inc(s("dtop_ready"), 1)
            for hot, oo in ((h1, o1), (h2, o2)):
                step(V.tensor_tensor(hot, bc(og, P, TILES, NG, EPG), oo.unsqueeze(2).to_broadcast([P, TILES, NG, EPG]), ALU.mult))
                step(V.tensor_tensor(hot, hot, bc(R["valid"], P, TILES, NG, EPG), ALU.mult))
            V.tensor_tensor(R["h12"], R["h1"], R["h2"], ALU.add).then_inc(s("onehot_ready"), 1)
            dve.wait_ge(s("eg_exp"), 1)
            step(V.tensor_reduce(vec[4], eg, AX.X, ALU.add))
            dve.wait_ge(s("dtop_exp"), 1)
            step(V.scalar_tensor_tensor(out=vec[4], in0=vec[5], scalar=1.0, in1=vec[4], op0=ALU.add, op1=ALU.mult))
            step(V.reciprocal(gates[:, 0, :], vec[4]))
            step(V.tensor_tensor(gates[:, 1, :], gates[:, 0, :], vec[5], ALU.mult))
            dve.wait_ge(s("ranks_done"), 1)
            rank = R["rank"].rearrange("p (t e) -> p t e", t=TILES)
            tot = bank[1][:, 0:TILES * NE].rearrange("p (t e) -> p t e", t=TILES)
            step(V.tensor_scalar(R["rank"], bank[0][:, 0:TILES * NE], -1.0, None, ALU.add))
            step(V.memset(R["run"], 0.0))
            for t in range(TILES):
                step(V.tensor_tensor(rank[:, t, :], rank[:, t, :], R["run"], ALU.add))
                step(V.tensor_tensor(R["run"], tot[:, t, :], R["run"], ALU.add))
            bige = R["big"][:, 0:NE * MAXB].rearrange("p (e j) -> p e j", e=NE)
            iota_r = R["iota"]
            step(V.tensor_scalar(R["cnt"], R["run"], 1.0 / P, None, ALU.mult))
            step(V.tensor_tensor(bige, bc(R["cnt"], P, NE, MAXB), iota_r[:, 0:MAXB].unsqueeze(1).to_broadcast([P, NE, MAXB]), ALU.is_gt))
            step(V.tensor_reduce(R["cnt"], bige, AX.X, ALU.add))
            step(V.tensor_scalar(R["cnt"], R["cnt"], 1.0, None, ALU.max))
            step(V.tensor_copy(R["end"], R["cnt"]))
            for e in range(1, NE):
                step(V.tensor_tensor(R["end"][:, e:e + 1], R["end"][:, e:e + 1], R["end"][:, e - 1:e], ALU.add))
            step(V.tensor_tensor(R["base"], R["end"], R["cnt"], ALU.subtract))
            step(V.tensor_copy(plan_u[:, 0:NE], R["base"]))
            step(V.tensor_scalar(R["blk"][:, 0:1], R["end"][:, NE - 1:NE], -1.0, float(BLOCKS), ALU.mult, ALU.add))
            step(V.tensor_copy(plan_u[:, 2 * NE:], R["blk"][:, 0:1]))
            V.tensor_copy(plan_u[:, NE:2 * NE], R["cnt"]).then_inc(s("plan_ready"), 1)
            step(V.tensor_scalar(R["base"], R["base"], float(P), None, ALU.mult))
            step(V.tensor_tensor(rank, rank, R["base"].unsqueeze(1).to_broadcast([P, TILES, NE]), ALU.add))
            for q, hot in enumerate(("h1", "h2")):
                step(V.tensor_tensor(R["tmp"], R[hot], R["rank"], ALU.mult))
                step(V.tensor_reduce(R["pos"][:, q * TILES:(q + 1) * TILES], R["tmp"].rearrange("p (t e) -> p t e", t=TILES), AX.X, ALU.add))
            step(V.tensor_copy(slots_u.rearrange("p q t -> p (q t)"), R["pos"]))
            for q in range(2):
                bigt = R["big"][:, 0:TILES * (BLOCKS - 1)].rearrange("p (t b) -> p t b", t=TILES)
                pos = R["pos"][:, q * TILES:(q + 1) * TILES]
                step(V.tensor_scalar(vec[6], pos, 1.0 / P, None, ALU.mult))
                step(V.tensor_tensor(bigt, bc(vec[6], P, TILES, BLOCKS - 1), iota_r[:, 1:BLOCKS].unsqueeze(1).to_broadcast([P, TILES, BLOCKS - 1]), ALU.is_ge))
                step(V.tensor_reduce(R["blk"][:, q * TILES:(q + 1) * TILES], bigt, AX.X, ALU.add))
            step(V.scalar_tensor_tensor(out=R["mod"], in0=R["blk"], scalar=-float(P), in1=R["pos"], op0=ALU.mult, op1=ALU.add))
            for j in range(2 * TILES):
                t, q = j // 2, j % 2
                if j >= 2:
                    dve.wait_ge(s("hot_used"), j - 1)
                c = q * TILES + t
                own.did(V.tensor_scalar(hot_slot[q], iota_r, R["mod"][:, c:c + 1], None, ALU.is_equal))
                own.wait()
                V.tensor_scalar(hot_block[q], iota_r[:, 0:BLOCKS], R["blk"][:, c:c + 1], R["tok"][:, t:t + 1], ALU.is_equal, ALU.mult
                                ).then_inc(s("hot_ready"), 1)
            dve.wait_ge(s("hot_used"), 2 * TILES)
            step(V.memset(token_u[:, BLOCKS:], 0))
            V.tensor_copy(token_u[:, 0:BLOCKS], bank[2][:, 0:BLOCKS]).then_inc(s("tokens_ready"), 1)
            dve.wait_ge(s("tokens_ready"), 1)
            own.restart()

            def lo(out, x, hi):
                return V.tensor_tensor(out, x, hi.bitcast(F32), ALU.subtract)

            def split(e, at):
                done = STEPS * e if isinstance(e, int) else dve.snap(STEPS * e)
                steps = SPLITS[at]
                for q in steps:
                    dve.wait_ge(s("w_high"), done + q + 1)
                    if q < 2 * KC:
                        k, cols_ = q % KC, slice(q // KC * HE, (q // KC + 1) * HE)
                        ins = V.scalar_tensor_tensor(out=gu_lo[:, k, :, cols_], in0=raw_gu[q // KC][:, k, :, :], scalar=cols[:, c_ffn + k:c_ffn + k + 1],
                                                     in1=gu_hi[:, k, :, cols_].bitcast(F32), op0=ALU.mult, op1=ALU.subtract)
                    else:
                        ks = q - 2 * KC
                        ins = lo(d_lo[:, ks, :], raw_d[:, ks, :], d_hi[:, ks, :])
                    ins.then_inc(s("w_split"), 1)

            def b_xT(n):
                dve.wait_ge(s("xh_ready"), n)
                own.did(lo(xl[:, 0:4].rearrange("p k t -> p (k t)"), bank[0][:, :], xh[:, 0:4].rearrange("p k t -> p (k t)")))
                lo(xl[:, 4:8].rearrange("p k t -> p (k t)"), bank[1][:, :], xh[:, 4:8].rearrange("p k t -> p (k t)")).then_inc(s("xT_ready"), 1)

            def b_hid(n, half):
                dve.wait_ge(s("silu_ready"), dve.snap(2 * n - 1 + half))
                dve.wait_ge(s("up_done"), dve.snap(2 * n - 1 + half))
                part = sg[:, half * HE:(half + 1) * HE]
                V.tensor_tensor(part, bank[3 + 2 * half][:, 0:HE], part, ALU.mult).then_inc(s("hid_ready"), 1)

            def one_block(b, e, splits, more):
                n = dve.snap(b + 1)
                if splits:
                    split(e + 1, "A0")
                b_hid(n, 1)
                dve.wait_ge(s("hh_ready"), n)
                lo(hid_lo.rearrange("p k t -> p (k t)"), bank[2][:, :], hid_hi.rearrange("p k t -> p (k t)")).then_inc(s("hidT_ready"), 1)
                b_xT(dve.snap(n + 1))
                if splits:
                    split(e + 1, "A1")
                    split(e + 1, "B")
                dve.wait_ge(s("down_done"), n)
                dve.wait_ge(s("y_stored"), dve.snap(16 * n))
                V.tensor_copy(yb[:, BANK:], bank[7][:, :]).then_inc(s("bank7_free"), 1)
                if splits:
                    split(e + 1, "D0")
                    split(e + 1, "D1")
                if more:
                    b_hid(dve.snap(n + 1), 0)
                own.restart()

            dve.sem_inc(s("bank7_free"), 1)
            for part in SPLITS:
                split(0, part)
            b_xT(1)
            b_hid(1, 0)
            own.restart()
            each_block(dve, one_block)

            def c_head(t, n):
                T = rows(t)
                dve.wait_ge(s("ya_loaded"), 16 * n if isinstance(n, int) else dve.snap(16 * n))
                dve.wait_ge(s("y2_loaded"), 16 * n if isinstance(n, int) else dve.snap(16 * n))
                g = lambda q: gates[0:T, q, bass.ds(t, 1)]
                own.did(V.scalar_tensor_tensor(out=hrow(t), in0=ya[0:T, :], scalar=g(0), in1=hrow(t), op0=ALU.mult, op1=ALU.add))
                own.wait()
                V.scalar_tensor_tensor(out=hrow(t), in0=y2[0:T, :], scalar=g(1), in1=hrow(t), op0=ALU.mult, op1=ALU.add).then_inc(s("hc_ready"), 1)

            def c_anT(t, n):
                T = rows(t)
                dve.wait_ge(s("anTp_done"), n)
                own.did(gain_evict(anT[:, 0:4], bank[3], T, c_pg))
                gain_evict(anT[:, 4:8], bank[4], T, c_pg + 4).then_inc(s("anT_ready"), 1)

            def c_en(t, n):
                T = rows(t)
                dve.wait_ge(s("re_ready"), n)
                own.did(V.scalar_tensor_tensor(out=en[0:T, 0:BANK], in0=bank[1][0:T, :], scalar=re_[0:T, :], in1=ple_row[0:T, 0:BANK],
                                               op0=ALU.mult, op1=ALU.mult))
                own.wait()
                V.scalar_tensor_tensor(out=en[0:T, BANK:], in0=bank[2][0:T, :], scalar=re_[0:T, :], in1=ple_row[0:T, BANK:],
                                       op0=ALU.mult, op1=ALU.mult).then_inc(s("en_ready"), 1)

            def c_blend(t, n):
                T = rows(t)
                dve.wait_ge(s("sig_ready"), n)
                dve.wait_ge(s("en_ready"), n)
                own.did(V.tensor_tensor(gate[0:T, :], gate[0:T, :], en[0:T, :], ALU.mult))
                own.wait()
                V.tensor_tensor(hrow(t), hrow(t), gate[0:T, :], ALU.add).then_inc(s("hf_ready"), 1)

            def c_out(t, n, p):
                T = rows(t)
                dve.wait_ge(s("rf_ready"), n)
                if p is not None:
                    dve.wait_ge(s("y_out_stored"), 16 * p if isinstance(p, int) else dve.snap(16 * p))
                V.scalar_tensor_tensor(out=yout[0:T, :], in0=hrow(t), scalar=rf[0:T, :], in1=fin_row[0:T, :], op0=ALU.mult,
                                       op1=ALU.mult).then_inc(s("yout_ready"), 1)

            dve.wait_ge(s("c_rows_loaded"), 32)
            c_head(0, 1)
            c_anT(0, 1)
            c_en(0, 1)

            def c_tile(t, n, p, pp):
                if rows(t) != S:
                    n2 = n + 1 if isinstance(n, int) else dve.snap(n + 1)
                    c_head(t + 1, n2)
                c_blend(t, n)
                if rows(t) != S:
                    c_anT(t + 1, n2)
                    c_en(t + 1, n2)
                c_out(t, n, p)
                own.restart()

            c_tile(0, 1, None, None)
            with dve.Fori(1, NT - 1) as t:
                c_tile(t, dve.snap(t + 1), t, None)
            c_tile(NT - 1, NT, NT - 1, None)
            c_tile(NT, TILES, NT, None)

        @block.scalar
        def _(act):
            A = nc.scalar
            own = Own(act, s("act_own"))
            for j, src in enumerate((i["dt_bias"], i["a_log"], i["d_skip"])):
                act.dma_start(heads3[:, j, :], src.partition_broadcast(P).rearrange("q o n -> q (o n)")).then_inc(s("heads_loaded"), 16)
            act.dma_start(h[32:32 + NSEQ * (TAPS - 1), NT * D:], i["state_conv"][0].rearrange("b j n -> (b j) n")).then_inc(s("conv_old_loaded"), 16)
            act.dma_start(cat.rearrange("p (h t) -> p h t", h=GMH), i["w_spatial"][0].rearrange("h t s -> t h s")).then_inc(s("ws_loaded"), 16)
            act.dma_start(gm_row[:, :], i["gmlp_norm"].partition_broadcast(P).rearrange("q o n -> q (o n)")).then_inc(s("gm_row_loaded"), 16)
            act.dma_start(w_r[:, :, 0:NG], i["w_router_group"][0].rearrange("(k p) n -> p k n", p=P)).then_inc(s("w_r_loaded"), 16)
            act.dma_start(w_r[:, :, NG:], i["w_router_expert"][0].rearrange("(k p) n -> p k n", p=P)).then_inc(s("w_r_loaded"), 16)
            act.dma_start(bias_r[:, 0:NG], i["b_router_group"].partition_broadcast(P).rearrange("q o n -> q (o n)")).then_inc(s("w_r_loaded"), 16)
            act.dma_start(bias_r[:, NG:], i["b_router_expert"].partition_broadcast(P).rearrange("q o n -> q (o n)")).then_inc(s("w_r_loaded"), 16)
            act.wait_ge(s("heads_loaded"), 16 * 3)
            A.activation(heads3[:, 1, :], heads3[:, 1, :], ACT.Exp).then_inc(s("ealog_ready"), 1)

            def x_square(t, n, free):
                T = rows(t)
                if isinstance(t, int) and t == 0:
                    act.wait_ge(s("x0_loaded"), 16)
                    act.wait_ge(s("cols_ready"), 1)
                else:
                    act.wait_ge(s("x_loaded"), 32)
                A.activation(xn[0:T, :], hrow(t), ACT.Square, accum_out=ssx[0:T, :]).then_inc(s("ssx_ready"), 1)

            def h_square(t, n):
                T = rows(t)
                act.wait_ge(s("h_ready"), n)
                A.activation(xn[0:T, :], hrow(t), ACT.Square, accum_out=ssh[0:T, :]).then_inc(s("ssh_ready"), 1)

            def mT_evict(t, n):
                T = rows(t)
                act.wait_ge(s("mTp_done"), n)
                own.did(A.activation(mT[:, 0:4, 0:T], bank[0].rearrange("p (c t) -> p c t", c=4)[:, :, 0:T], ACT.Copy))
                own.wait()
                A.activation(mT[:, 4:8, 0:T], bank[1].rearrange("p (c t) -> p c t", c=4)[:, :, 0:T], ACT.Copy).then_inc(s("mT_ready"), 1)

            def catT1(t, n):
                T = rows(t)
                act.wait_ge(s("catTp1_done"), n)
                A.activation(catT[:, 4:8, 0:T], bank[5].rearrange("p (c t) -> p c t", c=4)[:, :, 0:T], ACT.Copy).then_inc(s("catT1_ready"), 1)

            def tile(t, n, p):
                T = rows(t)
                sample = T == S
                first = isinstance(t, int) and t == 0
                act.wait_ge(s("xb_done"), n)
                A.activation(raw[0:T, 0:BANK], bank[0][0:T, :], ACT.Copy).then_inc(s("raw0_ready"), 1)
                if not sample:
                    if not first:
                        act.wait_ge(s("ry_ready"), p)
                    x_square(t + 1, n, p)
                if not first:
                    catT1(t - 1, p)
                act.wait_ge(s("nab_ready"), n)
                own.did(A.activation(ex[0:T], nab[0:T], ACT.Exp))
                own.wait()
                A.activation(ln1[0:T], ex[0:T], ACT.Ln, bias=1.0).then_inc(s("sp_ready"), 1)
                act.wait_ge(s("z_done"), n)
                A.activation(zs[0:T, :], bank[2][0:T, :], ACT.Silu).then_inc(s("z_ready"), 1)
                act.wait_ge(s("conv_ready"), 2 * n if isinstance(n, int) else act.snap(2 * n))
                A.activation(xcT[:, :, 0:T], acc[:, :, 0:T], ACT.Silu).then_inc(s("xc_ready"), 1)
                act.wait_ge(s("u_done"), n)
                A.activation(uu[0:T, :], bank[2][0:T, :], ACT.Gelu).then_inc(s("u_ready"), 1)
                act.wait_ge(s("v_done"), n)
                A.activation(vv[0:T, :], bank[4][0:T, :], ACT.Gelu).then_inc(s("v_ready"), 1)
                act.wait_ge(s("v_ready"), n)
                A.activation(yy[0:T, :], vv[0:T, :], ACT.Square, accum_out=ssv[0:T, :]).then_inc(s("ssv_ready"), 1)
                act.wait_ge(s("seg_done"), n)
                for half in range(2):
                    b3 = bank[half].rearrange("p (h t) -> p h t", h=4)[0:T, :, 0:T]
                    ins = A.activation(dec[0:T, 4 * half:4 * half + 4, 0:T], b3, ACT.Exp)
                    if half:
                        own.wait()
                        ins.then_inc(s("decay_ready"), 1)
                    else:
                        own.did(ins)
                act.wait_ge(s("cum_done"), n)
                if sample:
                    own.did(A.activation(edcol[:, :, :].rearrange("p c b -> p (c b)"), bank[3][:, 32:32 + NSEQ * XC], ACT.Exp))
                    own.wait()
                w = (2 if sample else 3) * HEADS
                A.activation(ecum[0:T, 0:w], bank[3][0:T, 0:w], ACT.Exp).then_inc(s("ecum_ready"), 1)
                if not first:
                    if not sample:
                        act.wait_ge(s("aTp_done"), (n + 1) if isinstance(n, int) else act.snap(n + 1))
                    h_square(t - 1, p)
                act.wait_ge(s("bt_done"), n)
                A.activation(bt[0:T, :], bank[3][0:T, 0:GROUPS * N], ACT.Copy).then_inc(s("bt_ready"), 1)
                if sample:
                    for b in range(NSEQ):
                        act.wait_ge(s("s_trp_done"), b + 1)
                        A.activation(s_tr[:, b, :], bank[5 + 2 * (b % 2)][:, :], ACT.Copy).then_inc(s("s_tr_ready"), 1)
                if not first:
                    mT_evict(t - 1, p)
                own.restart()

            x_square(0, 1, None)
            act.wait_ge(s("gm_row_loaded"), 16)
            act.wait_ge(s("aTp_done"), 1)
            tile(0, 1, 0)
            with act.Fori(1, NT - 1) as t:
                tile(t, act.snap(t + 1), t)
            tile(NT - 1, NT, NT - 1)
            tile(NT, TILES, NT)
            catT1(NT, TILES)
            h_square(NT, TILES)
            mT_evict(NT, TILES)
            act.wait_ge(s("eg_ready"), 1)
            eg = R["eg"]
            A.activation(eg, eg, ACT.Exp).then_inc(s("eg_exp"), 1)
            act.wait_ge(s("dtop_ready"), 1)
            A.activation(R["vec"][:, 5 * TILES:6 * TILES], R["vec"][:, 3 * TILES:4 * TILES], ACT.Exp).then_inc(s("dtop_exp"), 1)

            def split(e, at):
                x2 = isinstance(e, int)
                if at[0] != "D":
                    act.wait_ge(s(f"gu{int(at[0] == 'B')}_loaded"), 32 * (e + 1) if x2 else act.snap(32 * e + 32))
                steps = SPLITS[at]
                for q in steps:
                    if q < 2 * KC:
                        k, cols_ = q % KC, slice(q // KC * HE, (q // KC + 1) * HE)
                        ins = A.activation(gu_hi[:, k, :, cols_], raw_gu[q // KC][:, k, :, :], ACT.Copy, scale=cols[:, c_ffn + k:c_ffn + k + 1])
                    else:
                        if q == 2 * KC:
                            act.wait_ge(s("d_loaded"), 16 * (e + 1) if x2 else act.snap(16 * e + 16))
                        ks = q - 2 * KC
                        ins = A.activation(d_hi[:, ks, :], raw_d[:, ks, :], ACT.Copy)
                    ins.then_inc(s("w_high"), 1)

            def b_xT(n):
                act.wait_ge(s("xTp_done"), n)
                own.did(A.activation(xh[:, 0:4].rearrange("p k t -> p (k t)"), bank[0][:, :], ACT.Copy))
                own.wait()
                A.activation(xh[:, 4:8].rearrange("p k t -> p (k t)"), bank[1][:, :], ACT.Copy).then_inc(s("xh_ready"), 1)

            def b_silu(n, half):
                act.wait_ge(s("gate_done"), act.snap(2 * n - 1 + half))
                A.activation(sg[:, half * HE:(half + 1) * HE], bank[2 + 2 * half][:, 0:HE], ACT.Silu).then_inc(s("silu_ready"), 1)

            def one_block(b, e, splits, more):
                n = act.snap(b + 1)
                if splits:
                    split(e + 1, "A0")
                b_silu(n, 1)
                act.wait_ge(s("hTp_done"), n)
                A.activation(hid_hi.rearrange("p k t -> p (k t)"), bank[2][:, :], ACT.Copy).then_inc(s("hh_ready"), 1)
                b_xT(act.snap(n + 1))
                if splits:
                    split(e + 1, "A1")
                    split(e + 1, "B")
                act.wait_ge(s("down_done"), n)
                act.wait_ge(s("y_stored"), act.snap(16 * n))
                A.activation(yb[:, 0:BANK], bank[6][:, :], ACT.Copy).then_inc(s("bank6_free"), 1)
                if splits:
                    split(e + 1, "D0")
                if more:
                    b_silu(act.snap(n + 1), 0)
                act.wait_ge(s("bank6_free"), act.snap(n + 1))
                act.wait_ge(s("bank7_free"), act.snap(n + 1))
                act.dma_start(y_rows[bass.ds(b * P, P), :], yb).then_inc(s("y_stored"), 16)
                if splits:
                    split(e + 1, "D1")
                own.restart()
                if more:
                    act.wait_ge(s("up_done"), act.snap(2 * n + 1))

            act.sem_inc(s("bank6_free"), 1)
            act.sem_inc(s("y_stored"), 16)
            act.wait_ge(s("out_done"), TILES)
            act.wait_ge(s("mTp_done"), TILES)
            act.wait_ge(s("lg_done"), TILES)
            act.wait_ge(s("ssm_stored"), 16 * XC)
            act.wait_ge(s("out_stored"), 32)
            for part in SPLITS:
                split(0, part)
            b_xT(1)
            b_silu(1, 0)
            own.restart()
            act.wait_ge(s("up_done"), 1)
            each_block(act, one_block)

            def c_pT(t, n):
                T = rows(t)
                act.wait_ge(s("pTp_done"), n)
                A.activation(pT[:, :, 0:T], bank[0][:, 0:PC * P].rearrange("p (c t) -> p c t", c=PC)[:, :, 0:T], ACT.Copy).then_inc(s("pT_ready"), 1)

            def c_hsq(t, n):
                T = rows(t)
                act.wait_ge(s("hc_ready"), n)
                A.activation(an[0:T, :], hrow(t), ACT.Square, accum_out=ssc[0:T, :]).then_inc(s("ssc_ready"), 1)

            def c_esq(t, n):
                T = rows(t)
                act.wait_ge(s("ple_done"), n)
                own.did(A.activation(en[0:T, 0:BANK], bank[1][0:T, :], ACT.Square, accum_out=sse[0:T, 0:1]))
                A.activation(en[0:T, BANK:], bank[2][0:T, :], ACT.Square, accum_out=sse[0:T, 1:2]).then_inc(s("sse_ready"), 1)

            def c_sig(t, n):
                T = rows(t)
                act.wait_ge(s("pg_done"), n)
                own.did(A.activation(gate[0:T, 0:BANK], bank[5][0:T, :], ACT.Sigmoid))
                own.wait()
                A.activation(gate[0:T, BANK:], bank[6][0:T, :], ACT.Sigmoid).then_inc(s("sig_ready"), 1)

            def c_fsq(t, n, p):
                T = rows(t)
                act.wait_ge(s("hf_ready"), n)
                A.activation(gate[0:T, :], hrow(t), ACT.Square, accum_out=ssf[0:T, :]).then_inc(s("ssf_ready"), 1)

            c_hsq(0, 1)
            c_pT(0, 1)
            c_esq(0, 1)

            def c_tile(t, n, p):
                if rows(t) != S:
                    n2 = n + 1 if isinstance(n, int) else act.snap(n + 1)
                    act.wait_ge(s("anTp_done"), n)
                    c_hsq(t + 1, n2)
                if p is not None:
                    act.wait_ge(s("ssf_ready"), p)
                c_sig(t, n)
                if rows(t) != S:
                    c_pT(t + 1, n2)
                c_fsq(t, n, p)
                if rows(t) != S:
                    c_esq(t + 1, n2)
                own.restart()

            c_tile(0, 1, None)
            with act.Fori(1, NT - 1) as t:
                c_tile(t, act.snap(t + 1), t)
            c_tile(NT - 1, NT, NT - 1)
            c_tile(NT, TILES, NT)

        @block.gpsimd
        def _(pool):
            G = nc.gpsimd
            own = Own(pool, s("pool_own"))
            own.did(G.memset(ident[:, :], 0.0))
            own.did(G.memset(ones[:, :], 1.0))
            own.did(G.memset(half_neg[:, :], -0.5))
            norm_eps = {D: norm_c[:, 0:1], GM: norm_c[:, 1:2]}
            own.did(G.memset(norm_c[:, 0:1], D * EPS))
            own.did(G.memset(norm_c[:, 1:2], GM * EPS))
            own.did(G.memset(wsn, 0.0))
            own.wait()
            G.affine_select(out=ident[:, :], in_=ident[:, :], compare_op=ALU.not_equal, fill=1.0, base=0, pattern=[[-1, P]],
                            channel_multiplier=1).then_inc(s("ident_ready"), 1)
            own.did(G.affine_select(out=incl[:, :], in_=ones[:, :], compare_op=ALU.is_ge, fill=0.0, base=0, pattern=[[1, P]], channel_multiplier=-1))
            own.wait()
            G.affine_select(out=strict[:, :], in_=ones[:, :], compare_op=ALU.is_gt, fill=0.0, base=0, pattern=[[-1, P]],
                            channel_multiplier=1).then_inc(s("incl_ready"), 1)
            def rstd(sum_, var, out, T, count):
                own.did(G.tensor_tensor(var[0:T], sum_[0:T], norm_eps[count][0:T, :], ALU.add))
                own.wait()
                own.did(G.tensor_tensor(var[0:T], var[0:T], half_neg[0:T, 0:1], ALU.pow))
                own.wait()
                return G.tensor_scalar(out[0:T], var[0:T], float(count) ** 0.5, None, ALU.mult)

            def x_norm(t, n):
                T = rows(t)
                pool.wait_ge(s("ssx_ready"), n)
                own.did(rstd(ssx, vx, rx, T, D))
                own.wait()
                G.tensor_tensor(xn[0:T, :], hrow(t), rx[0:T, :].to_broadcast([T, D]), ALU.mult).then_inc(s("xn_ready"), 1)

            def m_norm(t, n):
                T = rows(t)
                pool.wait_ge(s("ssh_ready"), n)
                own.did(rstd(ssh, vh, rh, T, D))
                own.wait()
                G.tensor_tensor(xn[0:T, :], hrow(t), rh[0:T, :].to_broadcast([T, D]), ALU.mult).then_inc(s("m_ready"), 1)

            def tile(t, n, p):
                T = rows(t)
                if T != S:
                    x_norm(t + 1, n + 1 if isinstance(n, int) else pool.snap(n + 1))
                pool.wait_ge(s("ssv_ready"), n)
                rstd(ssv, vvv, rv, T, GM).then_inc(s("rv_ready"), 1)
                if not (isinstance(t, int) and t == 0):
                    m_norm(t - 1, p)
                if not (isinstance(t, int) and t == 0):
                    pool.wait_ge(s("m_stored"), 16 * p if isinstance(p, int) else pool.snap(16 * p))
                pool.wait_ge(s("vy_ready"), n)
                G.tensor_tensor(ry[0:T], vy[0:T], half_neg[0:T, 0:GROUPS], ALU.pow).then_inc(s("ry_ready"), 1)
                own.restart()

            x_norm(0, 1)
            wsn3 = wsn.rearrange("p (h t) -> p h t", h=GMH)
            for b in range(NSEQ):
                pool.dma_start(wsn3[b * NTOK:(b + 1) * NTOK, :, b * NTOK:(b + 1) * NTOK],
                               i["w_spatial"][0, :, 0:NTOK, 0:NTOK].rearrange("h t s -> t h s")).then_inc(s("ws_s_loaded"), 16)
                pool.dma_start(bs_s[b * NTOK:(b + 1) * NTOK, :], i["b_spatial"][0, :, 0:NTOK].rearrange("h t -> t h"),
                               allow_slow_non_contiguous=True).then_inc(s("bs_s_loaded"), 16)
            own.did(G.affine_select(out=seq_cols[:, :], in_=ones[0:S, 0:NSEQ], compare_op=ALU.is_ge, fill=0.0, base=0, pattern=[[-NTOK, NSEQ]], channel_multiplier=1))
            own.wait()
            own.did(G.affine_select(out=seq_cols[:, :], in_=seq_cols[:, :], compare_op=ALU.is_ge, fill=0.0, base=NTOK - 1, pattern=[[NTOK, NSEQ]], channel_multiplier=-1))
            own.wait()
            own.did(G.tensor_tensor(incl_s.rearrange("p (b t) -> p b t", b=NSEQ), bc(seq_cols[:, :], S, NSEQ, NTOK), incl[0:S, 0:S].rearrange("p (b t) -> p b t", b=NSEQ), ALU.mult))
            pool.wait_ge(s("incl_ready"), 1)
            own.did(G.tensor_tensor(strict_s.rearrange("p (b t) -> p b t", b=NSEQ), bc(seq_cols[:, :], S, NSEQ, NTOK), strict[0:S, 0:S].rearrange("p (b t) -> p b t", b=NSEQ), ALU.mult))
            own.did(G.memset(seq_rows[:, :, :], 1.0))
            own.wait()
            own.did(G.affine_select(out=seq_rows[:, :, :], in_=seq_rows[:, :, :], compare_op=ALU.is_ge, fill=0.0, base=0, pattern=[[-NTOK, NSEQ], [1, S]], channel_multiplier=0))
            own.wait()
            G.affine_select(out=seq_rows[:, :, :], in_=seq_rows[:, :, :], compare_op=ALU.is_ge, fill=0.0, base=NTOK - 1, pattern=[[NTOK, NSEQ], [-1, S]],
                            channel_multiplier=0).then_inc(s("seq_ready"), 1)

            tile(0, 1, 0)
            with pool.Fori(1, NT - 1) as t:
                tile(t, pool.snap(t + 1), t)
            tile(NT - 1, NT, NT - 1)
            tile(NT, TILES, NT)
            m_norm(NT, TILES)
            pool.wait_ge(s("m_stored"), 16 * TILES)
            pool.wait_ge(s("mTp_done"), TILES)
            pool.wait_ge(s("out_done"), TILES)
            pool.wait_ge(s("lg_ready"), TILES)
            own.did(G.iota(R["iota"], [[1, P]], base=0, channel_multiplier=0, allow_small_or_imprecise_dtypes=True))
            own.did(G.iota(R["tok"], [[P, TILES]], base=0, channel_multiplier=1, allow_small_or_imprecise_dtypes=True))
            own.did(G.memset(R["valid"], 1.0))
            own.wait()
            G.affine_select(out=R["valid"], in_=R["valid"], compare_op=ALU.is_ge, fill=0.0, base=SEQ + S - 1, pattern=[[-P, TILES]],
                            channel_multiplier=-1).then_inc(s("iota_ready"), 1)

            def gather(b, rows_used, before):
                if rows_used is not None:
                    pool.wait_ge(s("xTp_done"), rows_used)
                    pool.wait_ge(s("gathered"), before)
                pool.wait_ge(s("tokens_ready"), 1)
                own.did(G.tensor_copy(index_u[:, 0:1], token_u[:, bass.ds(b, 1)]))
                own.wait()
                pool.indirect_dma_start(xg, None, m_rows, bass.IndirectOffsetOnAxis(ap=index_u[:, 0:1], axis=0)).then_inc(s("gathered"), 16)
                own.restart()

            gather(0, None, None)
            total = blocks_in_all(pool)
            with pool.Fori(0, total) as b:
                n = pool.snap(b + 1)
                gather(n, n, pool.snap(16 * n))

            def c_gather(t, n, p):
                T = rows(t)
                for q, dst, name in ((0, ya, "ya_loaded"), (1, y2, "y2_loaded")):
                    if p is not None:
                        pool.wait_ge(s("hc_ready"), p)
                    own.did(G.tensor_copy(index_u[0:T, q:q + 1], slots_u[0:T, q, bass.ds(t, 1)]))
                    own.wait()
                    pool.indirect_dma_start(dst[0:T, :], None, y_rows[0:BLOCKS * P, :], bass.IndirectOffsetOnAxis(ap=index_u[0:T, q:q + 1], axis=0)
                                            ).then_inc(s(name), 16)

            def c_an(t, n):
                T = rows(t)
                pool.wait_ge(s("ssc_ready"), n)
                own.did(rstd(ssc, vc, rc, T, D))
                own.wait()
                G.tensor_tensor(an[0:T, :], hrow(t), rc[0:T, :].to_broadcast([T, D]), ALU.mult).then_inc(s("an_ready"), 1)

            def c_re(t, n):
                T = rows(t)
                pool.wait_ge(s("sse_ready"), n)
                own.did(G.tensor_tensor(ve[0:T], sse[0:T, 0:1], sse[0:T, 1:2], ALU.add))
                own.wait()
                rstd(ve, ve, re_, T, D).then_inc(s("re_ready"), 1)

            def c_rf(t, n):
                T = rows(t)
                pool.wait_ge(s("ssf_ready"), n)
                rstd(ssf, vf, rf, T, D).then_inc(s("rf_ready"), 1)

            pool.wait_ge(s("blocks_over"), 2)
            c_gather(0, 1, None)
            c_gather(1, 2, 1)
            c_an(0, 1)
            c_re(0, 1)

            def c_tile(t, n, p):
                n2 = n + 1 if isinstance(n, int) else pool.snap(n + 1)
                if rows(t) != S:
                    if not (isinstance(t, int) and t == NT - 1):
                        c_gather(t + 2, None, n2)
                    c_an(t + 1, n2)
                c_rf(t, n)
                if rows(t) != S:
                    c_re(t + 1, n2)
                own.restart()

            c_tile(0, 1, None)
            with pool.Fori(1, NT - 2) as t:
                c_tile(t, pool.snap(t + 1), t)
            c_tile(NT - 2, NT - 1, None)
            c_tile(NT - 1, NT, None)
            c_tile(NT, TILES, None)


_OUTS = ("y_p", "y_s", "conv_p", "ssm_p", "conv_s", "ssm_s", "v_s")


def declare(nc, arrays, mybir_):
    ins = {name: nc.dram_tensor(f"in_{name}", a.shape, F32, kind="ExternalInput").ap() for name, a in arrays.items()}
    depth, nseq, taps, conv = arrays["state_conv"].shape
    _, _, heads, hp, n = arrays["state_ssm"].shape
    batch = arrays["x_prompt"].shape[0]
    ntok = arrays["x_sample"].shape[1]
    shapes = dict(y_p=arrays["x_prompt"].shape, y_s=arrays["x_sample"].shape, conv_p=(depth, batch, taps, conv),
                  ssm_p=(depth, batch, heads, hp, n), conv_s=(depth, nseq, taps, conv), ssm_s=(depth, nseq, heads, hp, n),
                  v_s=(depth, nseq, ntok, arrays["gmlp_norm"].shape[1]))
    outs = {name: nc.dram_tensor(f"out_{name}", shapes[name], F32, kind="ExternalOutput").ap() for name in _OUTS}
    return ins, outs


def kernel(**inputs):
    import numpy as np
    import concourse.bacc as bacc
    from concourse.bass_utils import run_bass_kernel_spmd

    nc = bacc.Bacc("TRN2", target_bir_lowering=False, num_devices=1)
    arrays = {name: np.ascontiguousarray(a) for name, a in inputs.items()}
    i, o = declare(nc, arrays, mybir)
    build(nc, i, o)
    r = run_bass_kernel_spmd(nc, [{f"in_{name}": a for name, a in arrays.items()}], core_ids=[0])
    return tuple(r.results[0][f"out_{name}"] for name in _OUTS)
```

```python
from contextlib import ExitStack

import concourse.bass as bass
from concourse import mybir

F32 = mybir.dt.float32
I32 = mybir.dt.int32
U32 = mybir.dt.uint32
F32R = mybir.dt.float32r
ACT = mybir.ActivationFunctionType
ALU = mybir.AluOpType
AX = mybir.AxisListType

P = 128
BANK = 512
BIG = 1.0e30
TINY = 1.0e-30
EPS = 1e-6


class Own:

    def __init__(self, eng, sem):
        self.eng, self.sem, self.n = eng, sem, 0

    def did(self, instruction):
        instruction.then_inc(self.sem, 1)
        self.n += 1
        return self.n

    def wait(self, n=None):
        self.eng.wait_ge(self.sem, self.n if n is None else n)

    def restart(self):
        self.wait()
        self.eng.sem_clear(self.sem)
        self.n = 0


def build(nc, i, o):
    D = i["x_prompt"].shape[2]
    SEQ = i["x_prompt"].shape[1]
    NSEQ, NTOK = i["x_sample"].shape[0], i["x_sample"].shape[1]
    S = NSEQ * NTOK
    KC = D // P
    NT = SEQ // P
    TILES = NT + 1
    IN = i["w_in"].shape[2]
    HEADS = i["dt_bias"].shape[1]
    SSD = i["ssd_norm"].shape[1]
    HP = SSD // HEADS
    N = i["state_ssm"].shape[4]
    CONV = i["conv_w"].shape[2]
    TAPS = i["conv_w"].shape[1]
    GROUPS = (CONV - SSD) // (2 * N)
    GW = SSD // GROUPS
    GH = HEADS // GROUPS
    GM = i["gmlp_norm"].shape[1]
    GMH = i["w_spatial"].shape[1]
    GMD = GM // GMH
    NG = i["w_router_group"].shape[2]
    NE = i["w_router_expert"].shape[2]
    EPG = NE // NG
    DE = i["w_gate"].shape[3]
    DC = DE // P
    PLE = i["w_ple"].shape[1]
    PC = PLE // P
    XC = SSD // P
    CC = CONV // P
    MAXB = -(-(SEQ + S) // P)
    ROUTED = 2 * (SEQ + S)
    BLOCKS = (ROUTED + NE * (P - 1)) // P
    assert (D, SSD, GM, DE) == (2 * BANK, BANK, BANK, BANK) and KC == CC == 8
    Z0, X0, DT0, U0, V0 = 0, SSD, SSD + CONV, SSD + CONV + HEADS, SSD + CONV + HEADS + GM

    with ExitStack() as ctx:
        def sb(name, shape, dt=F32):
            return ctx.enter_context(nc.sbuf_tensor(name, shape, dt))

        made = {}

        def s(name):
            if name not in made:
                made[name] = ctx.enter_context(nc.semaphore(name))
            return made[name]

        bank = [ctx.enter_context(nc.psum_tensor(f"bank{n}", [P, BANK], F32)) for n in range(8)]

        ident = sb("ident", [P, P])
        incl = sb("incl", [P, P])
        strict = sb("strict", [P, P])
        ones = sb("ones", [P, P])
        seq_cols = sb("seq_cols", [S, NSEQ])
        incl_s = sb("incl_s", [S, S])
        strict_s = sb("strict_s", [S, S])
        NROWS = KC * 3 + (TAPS + 1) * CC + XC + GMH
        cols = sb("cols", [P, NROWS])
        c_mix, c_ffn, c_pg, c_cw, c_cb = 0, KC, 2 * KC, 3 * KC, 3 * KC + TAPS * CC
        c_ssd = c_cb + CC
        c_bs = c_ssd + XC
        heads3 = sb("heads3", [P, 3, HEADS])
        bias_r = sb("bias_r", [P, NG + NE])
        bs_s = sb("bs_s", [S, GMH])
        logits = sb("logits", [P, TILES, NG + NE])
        small = sb("small", [P, 160])
        half_neg = sb("half_neg", [P, 4])
        norm_c = sb("norm_c", [P, 2])
        gates = sb("gates", [P, 2, TILES])
        slots_u = sb("slots_u", [P, 2, TILES], U32)
        TB = BLOCKS + MAXB
        token_u = sb("token_u", [P, TB], U32)
        plan_u = sb("plan_u", [P, 2 * NE + 1], U32)
        index_u = sb("index_u", [P, 2], U32)
        arena = -(-nc.sbuf_base // 32) * 32

        def placed(name, at, width, dt=F32):
            assert arena + at + 4 * width <= nc.sbuf_usable_end, (name, arena + at + 4 * width)
            return nc.alloc_sbuf_tensor_at(name, [P, width], dt, offset=arena + at)

        WORK = 12584
        h = placed("h", 0, TILES * D)
        A0 = 4 * TILES * D
        weights = placed("weights", A0, KC * IN + KC * D)
        work = placed("work", A0 + 4 * (KC * IN + KC * D), WORK)
        tail = A0 + 4 * (KC * IN + KC * D + WORK)
        gm_row = placed("gm_row", tail, GM)
        w_r = placed("w_r", tail + 4 * GM, KC * (NG + NE))[:, :].rearrange("p (k n) -> p k n", k=KC)
        tail += 4 * GM + 4 * KC * (NG + NE)
        conv_old = placed("conv_old", tail, CC * NSEQ * (TAPS - 1))[:, :].rearrange("p (c q) -> p c q", c=CC)
        tail += 4 * CC * NSEQ * (TAPS - 1)
        wsn = placed("wsn", tail + 4 * NSEQ * S, GMH * S)[0:S, :]
        seq_rows = placed("seq_rows", tail, NSEQ * S)[:, :].rearrange(
            "p (b l) -> p b l", b=NSEQ)
        GU, DN = KC * 2 * DE, DC * D
        HE = DE // 2
        raw_gu = [placed(f"raw_gu{q}", A0 + 2 * GU * q, GU // 2)[:, :].rearrange("p (k w n) -> p k w n", k=KC, w=2) for q in range(2)]
        B0 = A0 + 4 * GU
        w_hi, w_lo = placed("w_hi", B0, GU + DN, F32R), placed("w_lo", B0 + 4 * (GU + DN), GU + DN, F32R)
        B1 = B0 + 8 * (GU + DN)
        raw_d = placed("raw_d", B1, DN)[:, :].rearrange("p (k n) -> p k n", k=DC)
        B2 = B1 + 4 * DN
        xh = placed("xh", B2, D, F32R)[:, :].rearrange("p (k t) -> p k t", k=KC)
        xl = placed("xl", B2 + 4 * D, D, F32R)[:, :].rearrange("p (k t) -> p k t", k=KC)
        hid_hi = placed("hid_hi", B2 + 8 * D, DE, F32R)[:, :].rearrange("p (k t) -> p k t", k=DC)
        hid_lo = placed("hid_lo", B2 + 8 * D + 4 * DE, DE, F32R)[:, :].rearrange("p (k t) -> p k t", k=DC)
        B3 = B2 + 8 * D + 8 * DE
        xg = placed("xg", B3, D)[:, :]
        yb = placed("yb", B3 + 4 * D, D)[:, :]
        sg = placed("sg", B3 + 8 * D, DE)[:, :]
        R0 = B2
        RF = TILES * NE + 2 * P + 2 * TILES * (P + BLOCKS)
        WR = (B3 + 8 * D + 4 * DE - R0) // 4 - RF
        work_r = placed("work_r", R0, WR)
        work_f = placed("work_f", R0 + 4 * WR, RF, F32R)
        work_c = placed("work_c", A0, 3 * D)
        a_hi, a_lo = (placed(f"a_{q}", B1 + 4 * D * n, D, F32R)[:, :].rearrange("p (k t) -> p k t", k=KC)
                      for n, q in enumerate(("hi", "lo")))
        C0 = B1 + 2 * DN
        p_hi, p_lo = (placed(f"p_{q}", C0 + 4 * PLE * n, PLE, F32R)[:, :].rearrange("p (k t) -> p k t", k=PC)
                      for n, q in enumerate(("hi", "lo")))
        p_in = placed("p_in", C0 + 8 * PLE, PLE)[:, :]
        ple_row = placed("ple_row", C0 + 12 * PLE, D)[:, :]
        ya, y2, yout, junk, fin_row = (placed(f"rows{n}", B2 + 4 * D * n, D)[:, :] for n in range(5))
        gu_hi, gu_lo = (w[:, 0:GU].rearrange("p (k w n) -> p k w n", k=KC, w=2) for w in (w_hi, w_lo))
        d_hi, d_lo = (w[:, GU:].rearrange("p (k n) -> p k n", k=DC) for w in (w_hi, w_lo))
        STEPS = 2 * KC + DC
        SPLITS = {"A0": range(KC // 2), "A1": range(KC // 2, KC), "B": range(KC, 2 * KC), "D0": range(2 * KC, 2 * KC + DC // 2),
                  "D1": range(2 * KC + DC // 2, STEPS)}

        m_rows = nc.dram_tensor("m_rows", [SEQ + S, D], F32, kind="Internal").ap()
        y_rows = nc.dram_tensor("y_rows", [TB * P, D], F32, kind="Internal").ap()

        def carver(tensor, size):
            at = [0]

            def carve(width):
                at[0] += width
                assert at[0] <= size, at[0]
                return tensor[:, at[0] - width:at[0]]
            return carve

        carve = carver(work, WORK)
        xn = carve(D)
        aT = carve(D).rearrange("p (k t) -> p k t", k=KC)
        raw = carve(CONV)
        acc = raw.rearrange("p (c t) -> p c t", c=CC)
        convin = carve(CC * (P + TAPS - 1)).rearrange("p (c t) -> p c t", c=CC)
        xcT = carve(CONV).rearrange("p (c t) -> p c t", c=CC)
        mixA = carve(HEADS * P)
        dec = mixA.rearrange("p (h t) -> p h t", h=HEADS)
        mT = mixA.rearrange("p (k t) -> p k t", k=KC)
        cat = carve(D)
        catT = carve(D).rearrange("p (k t) -> p k t", k=KC)
        wsT = carve(GMH * P).rearrange("p (h t) -> p h t", h=GMH)
        bt = carve(GROUPS * N)
        vv, xdt, xwd, yy, state = (carve(SSD) for _ in range(5))
        zs, uu = cat[:, 0:SSD], cat[:, SSD:]
        cbm = carve(GROUPS * P).rearrange("p (g t) -> p g t", g=GROUPS)
        rowsT = catT[0:NROWS, 0, :]
        ws_s = carve(GMH * S).rearrange("p (h t) -> p h t", h=GMH)

        w_in = weights[:, 0:KC * IN].rearrange("p (k n) -> p k n", k=KC)
        w_out = weights[:, KC * IN:].rearrange("p (k n) -> p k n", k=KC)
        SN = XC * NSEQ * N
        carve = carver(weights, KC * IN)
        carve(GU)
        s_nat = carve(SN).rearrange("p (c b n) -> p c b n", c=XC, b=NSEQ)
        s_tr = carve(SN).rearrange("p (b m) -> p b m", b=NSEQ)
        ctm = carve(GROUPS * NSEQ * S).rearrange("p (g b t) -> p g b t", g=GROUPS, b=NSEQ)
        bmm = carve(GROUPS * NSEQ * N)[0:S, :].rearrange("p (g b n) -> p g b n", g=GROUPS, b=NSEQ)
        dax = carve(SSD)[0:S, :]
        final_sb = carve(SSD)
        conv_s = convin.rearrange("p c t -> p (c t)")[:, 0:CC * NSEQ * (NTOK + TAPS - 1)].rearrange(
            "p (c b t) -> p c b t", c=CC, b=NSEQ)

        ssx, ssh, ssv, ssy = small[:, 0:1], small[:, 1:2], small[:, 2:3], small[:, 4:6]
        vx, vh, vvv, vy = small[:, 6:7], small[:, 7:8], small[:, 8:9], small[:, 10:12]
        rx, rh, rv, ry = small[:, 12:13], small[:, 13:14], small[:, 14:15], small[:, 16:18]
        xsp, nab, ex, ln1, dd, rd, dtv, da = (small[:, 24 + 8 * n:32 + 8 * n] for n in range(8))
        ecum = small[:, 88:112]
        edcol = small[:, 112:144].rearrange("p (c b) -> p c b", c=XC)

        def bc(ap, *shape):
            while len(ap.shape) < len(shape):
                ap = ap.unsqueeze(len(ap.shape))
            return ap.to_broadcast(list(shape))

        def rows(t):
            return S if isinstance(t, int) and t == NT else P

        def hrow(t):
            return h[0:rows(t), bass.ds(t * D, D)]

        def hhalf(t, half):
            return h[0:rows(t), bass.ds(t * D + half * BANK, BANK)]

        carve = carver(work_c, 3 * D)
        en, an, gate = carve(D), carve(D), carve(D)

        carve = carver(work_r, WR)
        R = {}
        for name, w in (("eg", TILES * NG), ("og", TILES * NG), ("leg", TILES * EPG), ("o1", TILES * EPG), ("o2", TILES * EPG),
                        ("hot", 2 * TILES * NE), ("tmp", 2 * TILES * NE), ("rank", TILES * NE), ("vec", 6 * TILES),
                        ("cnt", NE), ("base", NE), ("end", NE), ("big", max(NE * MAXB, 2 * TILES * (BLOCKS - 1))), ("upto", NE * NE),
                        ("iota", P), ("first", BLOCKS), ("order", NG), ("tok", TILES), ("blk", 2 * TILES), ("mod", 2 * TILES),
                        ("pos", 2 * TILES), ("valid", TILES)):
            R[name] = carve(w)
        carve = carver(work_f, RF)
        for name, w in (("hot12", TILES * NE), ("incl", P), ("ones", P), ("hot_slot", 2 * TILES * P), ("hot_block", 2 * TILES * BLOCKS)):
            R[name] = carve(w)
        assert NG == EPG

        sse = small[:, 144:146]
        ssc, ssf = small[:, 146:147], small[:, 147:148]
        vc, ve, vf = small[:, 148:149], small[:, 149:150], small[:, 150:151]
        rc, re_, rf = small[:, 151:152], small[:, 152:153], small[:, 153:154]

        def gain(e, k):
            at = (c_pg if isinstance(e, int) and e == NE else c_ffn) + k
            return cols[:, at:at + 1]

        def update_bank(j):
            return 2 if j % 2 == 0 else 1 if j == 1 else 5

        def blocks_in_all(eng):
            first = eng.value_load(plan_u[0:1, NE - 1:NE], min_val=0, max_val=BLOCKS - 1)
            return eng.snap(first + eng.value_load(plan_u[0:1, 2 * NE - 1:2 * NE], min_val=1, max_val=MAXB))

        def each_block(eng, one_block):
            eng.wait_ge(s("plan_ready"), 1)

            def expert(e, more):
                first = eng.value_load(plan_u[0:1, bass.ds(e, 1)], min_val=0, max_val=BLOCKS - 1)
                count = eng.value_load(plan_u[0:1, bass.ds(e + NE, 1)], min_val=1, max_val=MAXB)
                with eng.If(count > 1):
                    with eng.Fori(0, eng.snap(count - 1)) as j:
                        one_block(eng.snap(first + j), e, False, True)
                one_block(eng.snap(first + count - 1), e, True, more)

            with eng.Fori(0, NE - 1) as e:
                expert(e, True)
            expert(NE - 1, False)

        block = ctx.enter_context(nc.Block())

        @block.sync
        def _(sp):
            sp.dma_start(h[:, 0:D], i["x_prompt"][0, 0:P, :]).then_inc(s("x0_loaded"), 16)
            w_src = i["w_in"][0].rearrange("(k p) n -> p k n", p=P)
            sp.dma_start(w_in[:, :, Z0:X0], w_src[:, :, Z0:X0]).then_inc(s("w_z_loaded"), 16)
            for at, src in ((c_mix, i["norm_mix"].rearrange("o (c p) -> (o c) p", p=P)),
                            (c_ffn, i["norm_ffn"].rearrange("o (c p) -> (o c) p", p=P)),
                            (c_pg, i["norm_pg"].rearrange("o (c p) -> (o c) p", p=P)),
                            (c_cw, i["conv_w"].rearrange("o j (c p) -> (o j c) p", p=P)),
                            (c_cb, i["conv_b"].rearrange("o (c p) -> (o c) p", p=P)),
                            (c_ssd, i["ssd_norm"].rearrange("o (c p) -> (o c) p", p=P)),
                            (c_bs, i["b_spatial"][0])):
                sp.dma_start(rowsT[at:at + src.shape[0], :], src).then_inc(s("rows_loaded"), 16)
            sp.dma_start(w_in[:, :, X0:X0 + BANK], w_src[:, :, X0:X0 + BANK]).then_inc(s("w_x_loaded"), 16)
            sp.dma_start(w_in[:, :, X0 + BANK:DT0], w_src[:, :, X0 + BANK:DT0]).then_inc(s("w_bc_loaded"), 16)
            sp.dma_start(w_in[:, :, DT0:U0], w_src[:, :, DT0:U0]).then_inc(s("w_dt_loaded"), 16)
            sp.dma_start(w_in[:, :, U0:IN], w_src[:, :, U0:IN]).then_inc(s("w_uv_loaded"), 16)
            sp.dma_start(h[:, D:NT * D].rearrange("p (t n) -> p t n", n=D),
                         i["x_prompt"][0, P:SEQ, :].rearrange("(t p) n -> p t n", p=P)).then_inc(s("x_loaded"), 16)
            sp.dma_start(h[0:S, NT * D:], i["x_sample"].rearrange("b t n -> (b t) n")).then_inc(s("x_loaded"), 16)
            sp.dma_start(w_out[:, :, :], i["w_out"][0].rearrange("(k p) n -> p k n", p=P)).then_inc(s("w_out_loaded"), 16)

            def m_store(t, n):
                sp.wait_ge(s("m_ready"), n)
                sp.dma_start(m_rows[bass.ds(t * P, rows(t)), :], xn[0:rows(t), :]).then_inc(s("m_stored"), 16)

            with sp.Fori(1, NT - 1) as t:
                m_store(t - 1, t)
            sp.wait_ge(s("raw0_ready"), NT)
            sp.wait_ge(s("raw1_ready"), NT)
            sp.dma_start(o["conv_p"][0, 0], raw[P - TAPS + 1:P, :]).then_inc(s("conv_stored"), 16)
            m_store(NT - 2, NT - 1)
            sp.wait_ge(s("raw0_ready"), TILES)
            sp.wait_ge(s("raw1_ready"), TILES)
            for b in range(NSEQ):
                lo = b * NTOK + NTOK - TAPS + 1
                sp.dma_start(o["conv_s"][0, b], raw[lo:b * NTOK + NTOK, :]).then_inc(s("conv_stored"), 16)
            def gate_up(e, q, done):
                if done is not None:
                    sp.wait_ge(s("w_split"), done)
                for w, name in enumerate(("w_gate", "w_up")):
                    sp.dma_start(raw_gu[q][:, :, w, :], i[name][0, bass.ds(e, 1), :, q * HE:(q + 1) * HE].rearrange(
                        "o (k p) n -> p (o k) n", p=P)).then_inc(s(f"gu{q}_loaded"), 16)

            def down(e, done):
                if done is not None:
                    sp.wait_ge(s("w_split"), done)
                sp.dma_start(raw_d, i["w_down"][0, bass.ds(e, 1)].rearrange("o (k p) n -> p (o k) n", p=P)).then_inc(s("d_loaded"), 16)

            sp.wait_ge(s("v_done"), TILES)
            for c in range(XC):
                sp.dma_start(s_nat[:, c], i["state_ssm"][0].rearrange("b (c a) p n -> (a p) c b n", c=XC)[:, c]
                             ).then_inc(s("states_loaded"), 16)
            gate_up(0, 0, None)
            gate_up(0, 1, None)
            m_store(NT - 1, NT)
            sp.wait_ge(s("vn_ready"), TILES)
            sp.dma_start(o["v_s"].rearrange("o b t n -> (o b t) n"), vv[0:S, :]).then_inc(s("out_stored"), 16)
            def states_store(c):
                sp.wait_ge(s("s_new"), 2 * (c + 1))
                sp.dma_start(o["ssm_s"][0].rearrange("b (c a) p n -> (a p) c b n", c=XC)[:, c], s_nat[:, c]
                             ).then_inc(s("ssm_stored"), 16)

            for c in range(XC - 1):
                states_store(c)
            m_store(NT, TILES)
            states_store(XC - 1)
            sp.wait_ge(s("final_ready"), 1)
            sp.dma_start(o["ssm_p"][0, 0].rearrange("(c a) p n -> (a p) c n", c=XC),
                         final_sb.rearrange("p (c n) -> p c n", c=XC)).then_inc(s("out_stored"), 16)

            sp.wait_ge(s("out_done"), TILES)
            sp.wait_ge(s("ssm_stored"), 16 * XC)
            sp.wait_ge(s("lg_done"), TILES)
            down(0, None)
            sp.wait_ge(s("plan_ready"), 1)
            total = blocks_in_all(sp)
            unused = sp.value_load(plan_u[0:1, 2 * NE:], min_val=0, max_val=BLOCKS - NE)
            sp.sem_inc(s("unused_filled"), 16)
            with sp.If(unused > 0):
                with sp.Fori(0, unused) as j:
                    sp.dma_start(y_rows[bass.ds((BLOCKS - 1 - j) * P, P), :].rearrange("p (k n) -> p k n", n=P),
                                 ones[:, :].unsqueeze(1).to_broadcast([P, KC, P])).then_inc(s("unused_filled"), 16)
            with sp.Fori(1, NE) as e:
                done = sp.snap(STEPS * e)
                gate_up(e, 0, sp.snap(done - KC - DC))
                gate_up(e, 1, sp.snap(done - DC))
                down(e, done)
            for q in range(2):
                sp.wait_ge(s("w_split"), STEPS * NE - DC - (1 - q) * KC)
                for w in range(2):
                    sp.dma_start(raw_gu[q][:, :, w, :], i["w_pg"][0, :, w * BANK + q * HE:w * BANK + (q + 1) * HE].rearrange(
                        "(k p) n -> p k n", p=P)).then_inc(s(f"gu{q}_loaded"), 16)
            sp.wait_ge(s("w_split"), STEPS * NE)
            sp.dma_start(raw_d[:, 0:PC, :], i["w_ple"][0].rearrange("(k p) n -> p k n", p=P)).then_inc(s("d_loaded"), 16)
            sp.dma_start(ple_row, i["norm_ple"].partition_broadcast(P).rearrange("q o n -> q (o n)")).then_inc(s("c_rows_loaded"), 16)

            def p_load(t, n, prev):
                if prev is not None:
                    sp.wait_ge(s("pTp_done"), prev)
                src = i["p_sample"][0].rearrange("b t n -> (b t) n") if rows(t) == S else i["p_prompt"][0, 0, bass.ds(t * P, P), :]
                sp.dma_start(p_in[0:rows(t), :], src).then_inc(s("p_loaded"), 16)

            def out_store(t, n):
                sp.wait_ge(s("yout_ready"), n)
                dst = o["y_s"].rearrange("b t n -> (b t) n") if rows(t) == S else o["y_p"][0, bass.ds(t * P, P), :]
                sp.dma_start(dst, yout[0:rows(t), :]).then_inc(s("y_out_stored"), 16)

            p_load(0, 1, None)
            sp.wait_ge(s("unused_filled"), sp.snap(16 * unused + 16))
            sp.sem_inc(s("blocks_over"), 1)
            sp.wait_ge(s("y_stored"), sp.snap(16 * total + 16))
            sp.sem_inc(s("blocks_over"), 1)
            sp.dma_start(fin_row, i["norm_final"].partition_broadcast(P)).then_inc(s("c_rows_loaded"), 16)
            p_load(1, 2, 1)
            with sp.Fori(1, NT - 1) as t:
                n = sp.snap(t + 1)
                p_load(n, t, n)
                out_store(t - 1, t)
            p_load(NT, TILES, NT)
            out_store(NT - 2, NT - 1)
            out_store(NT - 1, NT)
            out_store(NT, TILES)
            sp.wait_ge(s("y_out_stored"), 16 * TILES)
            sp.wait_ge(s("out_stored"), 32)
            sp.wait_ge(s("conv_stored"), 16 * (1 + NSEQ))
            sp.wait_ge(s("m_stored"), 16 * TILES)

        @block.tensor
        def _(pe):
            def product(out, lhs, rhs, ks):
                for k in ks:
                    last = nc.tensor.matmul(out, lhs(k), rhs(k), start=(k == ks[0]), stop=(k == ks[-1]))
                return last

            def transposes(src, T, lo, hi, out, w=P):
                for c in range(lo, hi):
                    last = nc.tensor.transpose(out[:, (c - lo) * P:(c - lo) * P + T], src[0:T, c * P:c * P + w], ident[0:T, 0:T])
                return last

            pe.wait_ge(s("ident_ready"), 1)
            pe.wait_ge(s("rows_loaded"), 16 * 7)
            nc.tensor.transpose(bank[0][:, 0:NROWS], rowsT, ident[0:NROWS, 0:NROWS]).then_inc(s("cols_done"), 1)
            Q = NSEQ * (TAPS - 1)
            pe.wait_ge(s("conv_old_loaded"), 16)
            for c in range(CC):
                last = nc.tensor.transpose(bank[1][:, c * Q:(c + 1) * Q], h[32:32 + Q, NT * D + c * P:NT * D + (c + 1) * P],
                                           ident[32:32 + Q, 32:32 + Q])
            last.then_inc(s("conv_old_done"), 1)
            pe.wait_ge(s("ws_loaded"), 16)
            wn = cat.rearrange("p (h t) -> p h t", h=GMH)
            for hh in range(GMH):
                last = nc.tensor.transpose(bank[2 + hh // 4][:, (hh % 4) * P:(hh % 4 + 1) * P], wn[:, hh, :], ident[:, :])
                if hh % 4 == 3:
                    last.then_inc(s("wsT_done"), 1)

            def x_transposes(t, n):
                T = rows(t)
                pe.wait_ge(s("xn_ready"), n)
                transposes(xn, T, 0, 4, bank[5])
                transposes(xn, T, 4, 8, bank[6]).then_inc(s("aTp_done"), 1)

            def cat_transposes(t, n):
                T = rows(t)
                pe.wait_ge(s("cat_ready"), n)
                transposes(cat, T, 0, 4, bank[4]).then_inc(s("catTp0_done"), 1)
                transposes(cat, T, 4, 8, bank[5]).then_inc(s("catTp1_done"), 1)

            def out_half(T, half):
                return product(bank[6 + half][0:T, :], lambda k: catT[:, k, 0:T], lambda k: w_out[:, k, half * BANK:(half + 1) * BANK],
                               range(KC))

            def out_product(t, n, bank7_free):
                T = rows(t)
                pe.wait_ge(s("catT0_ready"), n)
                pe.wait_ge(s("catT1_ready"), n)
                pe.wait_ge(*bank7_free)
                for half in range(2):
                    last = out_half(T, half)
                last.then_inc(s("out_done"), 1)
            def m_transposes(t, n):
                T = rows(t)
                pe.wait_ge(s("m_ready"), n)
                transposes(xn, T, 0, 4, bank[0])
                transposes(xn, T, 4, 8, bank[1]).then_inc(s("mTp_done"), 1)

            def router(t, n):
                T = rows(t)
                pe.wait_ge(s("mT_ready"), n)
                product(bank[3][0:T, 0:NG + NE], lambda k: mT[:, k, 0:T], lambda k: w_r[:, k, :], range(KC)).then_inc(s("lg_done"), 1)

            def z_product(t, n):
                T = rows(t)
                pe.wait_ge(s("aT_ready"), n)
                product(bank[2][0:T, :], lambda k: aT[:, k, 0:T], lambda k: w_in[:, k, Z0:Z0 + BANK], range(KC)).then_inc(s("z_done"), 1)

            def tile(t, n, p):
                T = rows(t)
                sample = T == S
                first = isinstance(t, int) and t == 0
                proj = lambda out, c0, w: product(out, lambda k: aT[:, k, 0:T], lambda k: w_in[:, k, c0:c0 + w], range(KC))
                if first:
                    pe.wait_ge(s("w_x_loaded"), 16)
                    pe.wait_ge(s("cols_ready"), 1)
                    pe.wait_ge(s("conv_old_ready"), 1)
                else:
                    pe.wait_ge(s("decay_ready"), p)
                proj(bank[0][0:T, :], X0, BANK).then_inc(s("xb_done"), 1)
                if first:
                    pe.wait_ge(s("w_bc_loaded"), 16)
                proj(bank[1][0:T, :], X0 + BANK, BANK).then_inc(s("bc_done"), 1)
                if not first:
                    cat_transposes(t - 1, p)
                pe.wait_ge(s("raw0_ready"), n)
                pe.wait_ge(s("raw1_ready"), n)
                transposes(raw, T, 0, 4, bank[0])
                transposes(raw, T, 4, 8, bank[1]).then_inc(s("rawT_done"), 1)
                if first:
                    pe.wait_ge(s("w_dt_loaded"), 16)
                else:
                    pe.wait_ge(s("bt_ready"), p)
                proj(bank[3][0:T, 0:HEADS], DT0, HEADS).then_inc(s("dt_done"), 1)
                if not first:
                    out_product(t - 1, p, (s("state_ready"), n))
                else:
                    pe.wait_ge(s("w_uv_loaded"), 16)
                pe.wait_ge(s("z_ready"), n)
                proj(bank[2][0:T, :], U0, BANK).then_inc(s("u_done"), 1)
                proj(bank[4][0:T, :], V0, BANK).then_inc(s("v_done"), 1)
                if not first:
                    pe.wait_ge(s("h_ready"), p)
                else:
                    pe.wait_ge(s("w_out_loaded"), 16)
                if not sample:
                    x_transposes(t + 1, (t + 2) if isinstance(t, int) else n + 1)
                mk_i, mk_s = (incl_s, strict_s) if sample else (incl, strict)
                pe.wait_ge(s("dam_ready"), n)
                pe.wait_ge(s("convin_ready"), n)
                for half in range(2):
                    last = nc.tensor.matmul(bank[half].rearrange("p (h t) -> p h t", h=4)[0:T, :, 0:T], mk_s[0:T, 0:T],
                                            dec[0:T, 4 * half:4 * half + 4, 0:T], start=True, stop=True)
                last.then_inc(s("seg_done"), 1)
                nc.tensor.matmul(bank[3][0:T, 0:HEADS], mk_i[0:T, 0:T], da[0:T, :], start=True, stop=True)
                last = nc.tensor.matmul(bank[3][0:T, HEADS:2 * HEADS], mk_s[0:T, 0:T], da[0:T, :], start=True, stop=True)
                if not sample:
                    last = nc.tensor.matmul(bank[3][0:T, 2 * HEADS:3 * HEADS], ones[0:T, 0:T], da[0:T, :], start=True, stop=True)
                else:
                    for c in range(XC):
                        last = nc.tensor.matmul(bank[3][:, 32 + NSEQ * c:32 + NSEQ * (c + 1)], dax[0:T, c * P:(c + 1) * P],
                                                seq_cols[:, :], start=True, stop=True)
                last.then_inc(s("cum_done"), 1)
                pe.wait_ge(s("xc_ready"), n)
                for c in range(XC):
                    last = nc.tensor.transpose(bank[7][0:T, c * P:(c + 1) * P], xcT[:, c, 0:T], ident[:, :])
                last.then_inc(s("xtok_done"), 1)
                pe.wait_ge(s("u_ready"), n)
                for g in range(GROUPS):
                    last = nc.tensor.matmul(bank[2][0:T, g * P:g * P + T], xcT[:, XC + g, 0:T], xcT[:, XC + GROUPS + g, 0:T],
                                            start=True, stop=True)
                last.then_inc(s("cb_done"), 1)
                pe.wait_ge(s("ecum_ready"), n)
                for g in range(GROUPS):
                    last = nc.tensor.transpose(bank[3][0:T, g * N:(g + 1) * N], xcT[:, XC + g, 0:T], ident[:, :])
                last.then_inc(s("bt_done"), 1)
                if not sample:
                    pe.wait_ge(s("aT_ready"), (t + 2) if isinstance(t, int) else n + 1)
                pe.wait_ge(s("vn_ready"), n)
                if sample:
                    pe.wait_ge(s("ws_s_ready"), 1)
                for hh in range(GMH):
                    last = nc.tensor.matmul(bank[6][0:T, hh * GMD:(hh + 1) * GMD], (ws_s[0:S, hh, :] if sample else wsT[:, hh, :]),
                                            vv[0:T, hh * GMD:(hh + 1) * GMD], start=True, stop=True)
                last.then_inc(s("gm_done"), 1)
                if sample:
                    pe.wait_ge(s("states_loaded"), 16 * XC)
                    pe.wait_ge(s("xw_ready"), n)
                    for b in range(NSEQ):
                        if b >= 2:
                            pe.wait_ge(s("s_tr_ready"), b - 1)
                        for c in range(XC):
                            last = nc.tensor.transpose(bank[5 + 2 * (b % 2)][:, c * P:(c + 1) * P], s_nat[:, c, b, :], ident[:, :])
                        last.then_inc(s("s_trp_done"), 1)
                    pe.wait_ge(s("s_tr_ready"), NSEQ)
                    pe.wait_ge(s("ctm_ready"), 1)
                    for g in range(GROUPS):
                        last = product(bank[5][0:T, g * GW:(g + 1) * GW], lambda b: ctm[:, g, b, :],
                                       lambda b: s_tr[:, b, g * GW:(g + 1) * GW], range(NSEQ))
                else:
                    pe.wait_ge(s("state_ready"), n)
                    for g in range(GROUPS):
                        last = nc.tensor.matmul(bank[5][0:T, g * GW:(g + 1) * GW], xcT[:, XC + GROUPS + g, 0:T],
                                                state[:, g * GW:(g + 1) * GW], start=True, stop=True)
                last.then_inc(s("yoff_done"), 1)
                pe.wait_ge(s("wts_ready"), n)
                pe.wait_ge(s("v_ready"), n)
                pe.wait_ge(s("xw_ready"), n)
                for hh in range(HEADS):
                    last = nc.tensor.matmul(bank[4][0:T, hh * HP:(hh + 1) * HP], dec[0:T, hh, 0:T], xdt[0:T, hh * HP:(hh + 1) * HP],
                                            start=True, stop=True)
                last.then_inc(s("ydiag_done"), 1)
                if not sample:
                    pe.wait_ge(s("bt_ready"), n)
                    for g in range(GROUPS):
                        last = nc.tensor.matmul(bank[7][:, g * GW:(g + 1) * GW], bt[0:T, g * N:(g + 1) * N], xwd[0:T, g * GW:(g + 1) * GW],
                                                start=True, stop=True)
                    last.then_inc(s("cs_done"), 1)
                pe.wait_ge(s("decay_ready"), n)
                if not first:
                    m_transposes(t - 1, p)
                if not sample:
                    pe.wait_ge(s("cbm_ready"), n)
                    z_product(t + 1, t + 2 if isinstance(t, int) else pe.snap(n + 1))
                    if not first:
                        router(t - 1, p)

            def state_update(j, free):
                c, q = j // 2, j % 2
                if free is not None:
                    pe.wait_ge(s("s_new"), free)
                nc.tensor.matmul(bank[update_bank(j)][:, :], xwd[0:S, c * P:(c + 1) * P],
                                 bmm[:, c * P // GW, 4 * q:4 * q + 4, :].rearrange("p b n -> p (b n)"), start=True, stop=True
                                 ).then_inc(s("cs_s_done"), 1)

            x_transposes(0, 1)
            pe.wait_ge(s("w_z_loaded"), 16)
            pe.wait_ge(s("wsT_ready"), 2)
            z_product(0, 1)
            tile(0, 1, 0)
            pe.wait_ge(s("w_r_ready"), 1)
            with pe.Fori(1, NT - 1) as t:
                tile(t, pe.snap(t + 1), t)
            tile(NT - 1, NT, NT - 1)
            tile(NT, TILES, NT)
            pe.wait_ge(s("cbm_ready"), TILES)
            pe.wait_ge(s("bmm_ready"), 1)
            state_update(0, None)
            router(NT - 1, NT)
            state_update(1, None)
            cat_transposes(NT, TILES)
            pe.wait_ge(s("catT0_ready"), TILES)
            pe.wait_ge(s("catT1_ready"), TILES)
            out_half(S, 0)
            state_update(2, 1)
            state_update(3, 1)
            out_half(S, 1).then_inc(s("out_done"), 1)
            state_update(4, 3)
            state_update(5, 4)
            state_update(6, 5)
            state_update(7, 6)
            m_transposes(NT, TILES)
            pe.wait_ge(s("lg_ready"), NT)
            router(NT, TILES)
            pe.wait_ge(s("s_new"), 2 * XC)
            for c in range(XC):
                last = nc.tensor.transpose(bank[2][:, c * P:(c + 1) * P], state[:, c * P:(c + 1) * P], ident[:, :])
            last.then_inc(s("finalp_done"), 1)

            pe.wait_ge(s("onehot_ready"), 1)
            for t in range(TILES):
                last = nc.tensor.matmul(bank[1][:, 0:NE], R["ones"], R["hot12"][:, t * NE:(t + 1) * NE], start=(t == 0), stop=(t == TILES - 1))
            last.then_inc(s("counts_done"), 1)
            nc.tensor.matmul(bank[0][:, 0:TILES * NE], R["incl"], R["hot12"], start=True, stop=False)
            for d in range(1, TILES):
                last = nc.tensor.matmul(bank[0][:, d * NE:TILES * NE], R["ones"], R["hot12"][:, 0:(TILES - d) * NE], start=False,
                                        stop=(d == TILES - 1))
            last.then_inc(s("ranks_done"), 1)
            pe.wait_ge(s("final_ready"), 1)
            for c in range(2 * TILES):
                if c % TILES == 0:
                    pe.wait_ge(s("hot_ready"), c // TILES + 1)
                T = rows(c % TILES)
                last = nc.tensor.matmul(bank[2][:, 0:BLOCKS], R["hot_slot"][0:T, c * P:(c + 1) * P],
                                        R["hot_block"][0:T, c * BLOCKS:(c + 1) * BLOCKS], start=(c == 0), stop=(c == 2 * TILES - 1))
            last.then_inc(s("tokens_done"), 1)

            def product3(out, lh, ll, rh, rl, ks, K=None):
                for k in ks:
                    nc.tensor.matmul(out, lh(k), rh(k), start=(k == 0), stop=False)
                    nc.tensor.matmul(out, lh(k), rl(k), start=False, stop=False)
                    last = nc.tensor.matmul(out, ll(k), rh(k), start=False, stop=(k == (K or len(ks)) - 1))
                return last

            def hid_transposes(half, ready):
                pe.wait_ge(s("hid_ready"), ready)
                transposes(sg, P, half * DC // 2, (half + 1) * DC // 2, bank[2][:, half * HE:]).then_inc(s("hTp_done"), 1)

            def b_rows(gathered):
                pe.wait_ge(s("gathered"), gathered)
                transposes(xg, P, 0, 4, bank[0])
                transposes(xg, P, 4, 8, bank[1]).then_inc(s("xTp_done"), 1)

            def one_block(b, e, splits, more):
                n = pe.snap(b + 1)
                pe.wait_ge(s("xT_ready"), n)
                steps = STEPS * e if isinstance(e, int) else pe.snap(STEPS * e)
                n2 = pe.snap(2 * n)
                for half in range(2):
                    cols_ = slice(half * HE, (half + 1) * HE)
                    pe.wait_ge(s("w_split"), steps + (half + 1) * KC)
                    for w, name in ((0, "gate_done"), (1, "up_done")):
                        product3(bank[2 + 2 * half + w][:, 0:HE], lambda k: xh[:, k, :], lambda k: xl[:, k, :],
                                 lambda k: gu_hi[:, k, w, cols_], lambda k: gu_lo[:, k, w, cols_], range(KC)).then_inc(s(name), 1)
                        if half and w == 0:
                            hid_transposes(0, n2)
                b_rows(pe.snap(16 * n + 16))
                hid_transposes(1, pe.snap(2 * n + 1))
                pe.wait_ge(s("w_split"), steps + STEPS)
                pe.wait_ge(s("bank6_free"), n)
                pe.wait_ge(s("bank7_free"), n)
                for quarter in range(4):
                    part, half = quarter // 2, quarter % 2
                    if half == 0:
                        pe.wait_ge(s("hidT_ready"), n2 if part == 0 else pe.snap(2 * n + 1))
                    done = product3(bank[6 + half][:, :], lambda k: hid_hi[:, k, :], lambda k: hid_lo[:, k, :],
                                    lambda k: d_hi[:, k, half * BANK:(half + 1) * BANK],
                                    lambda k: d_lo[:, k, half * BANK:(half + 1) * BANK],
                                    range(part * DC // 2, (part + 1) * DC // 2), DC)
                done.then_inc(s("down_done"), 1)

            b_rows(16)
            each_block(pe, one_block)

            SPLIT_PG = STEPS * NE + 2 * KC
            SPLIT_ALL = SPLIT_PG + PC

            def c_embed(t, n):
                pe.wait_ge(s("p_loaded"), 16 * n if isinstance(n, int) else pe.snap(16 * n))
                transposes(p_in, rows(t), 0, PC, bank[0]).then_inc(s("pTp_done"), 1)

            def c_rows(t, n):
                T = rows(t)
                pe.wait_ge(s("an_ready"), n)
                transposes(an, T, 0, 4, bank[3])
                transposes(an, T, 4, 8, bank[4]).then_inc(s("anTp_done"), 1)

            def c_ple(t, n):
                T = rows(t)
                pe.wait_ge(s("pT_ready"), n)
                if not (isinstance(t, int) and t == 0):
                    pe.wait_ge(s("en_ready"), t)
                for half in range(2):
                    last = product3(bank[1 + half][0:T, :], lambda k: p_hi[:, k, 0:T], lambda k: p_lo[:, k, 0:T],
                                    lambda k: d_hi[:, k, half * BANK:(half + 1) * BANK],
                                    lambda k: d_lo[:, k, half * BANK:(half + 1) * BANK], range(PC))
                last.then_inc(s("ple_done"), 1)

            def c_gate(t, n, half):
                T = rows(t)
                pe.wait_ge(s("anT_ready"), n)
                if not (isinstance(t, int) and t == 0):
                    pe.wait_ge(s(f"sig{half}_ready"), t)
                product3(bank[5 + half][0:T, :], lambda k: a_hi[:, k, 0:T], lambda k: a_lo[:, k, 0:T],
                         lambda k: gu_hi[:, k, half, :], lambda k: gu_lo[:, k, half, :], range(KC)).then_inc(s(f"pg{half}_done"), 1)

            total1 = pe.snap(blocks_in_all(pe) + 1)
            pe.wait_ge(s("xT_ready"), total1)
            c_embed(0, 1)
            pe.wait_ge(s("w_split"), SPLIT_ALL)
            c_ple(0, 1)
            c_rows(0, 1)
            pe.wait_ge(s("bank6_free"), total1)
            pe.wait_ge(s("bank7_free"), total1)

            def c_tile(t, n):
                more = rows(t) != S
                n2 = n + 1 if isinstance(n, int) else pe.snap(n + 1)
                c_gate(t, n, 0)
                if more:
                    c_embed(t + 1, n2)
                c_gate(t, n, 1)
                if more:
                    c_rows(t + 1, n2)
                    c_ple(t + 1, n2)

            c_tile(0, 1)
            with pe.Fori(1, NT - 1) as t:
                c_tile(t, pe.snap(t + 1))
            c_tile(NT - 1, NT)
            c_tile(NT, TILES)

        @block.vector
        def _(dve):
            V = nc.vector
            own = Own(dve, s("dve_own"))

            dve.wait_ge(s("cols_done"), 1)
            V.tensor_copy(cols[:, :], bank[0][:, 0:NROWS]).then_inc(s("cols_ready"), 1)
            dve.wait_ge(s("conv_old_done"), 1)
            V.tensor_copy(conv_old.rearrange("p c q -> p (c q)"), bank[1][:, 0:CC * NSEQ * (TAPS - 1)]).then_inc(s("conv_old_ready"), 1)
            dve.wait_ge(s("incl_ready"), 1)
            for half in range(2):
                dve.wait_ge(s("wsT_done"), half + 1)
                V.tensor_tensor(wsT[:, 4 * half:4 * half + 4, :], bank[2 + half].rearrange("p (h t) -> p h t", h=4),
                                incl[:, :].unsqueeze(1).to_broadcast([P, 4, P]), ALU.mult).then_inc(s("wsT_ready"), 1)
            own.did(V.memset(state, 0.0))
            dve.wait_ge(s("heads_loaded"), 16 * 3)
            dve.wait_ge(s("ealog_ready"), 1)
            own.did(V.tensor_scalar(heads3[:, 1, :], heads3[:, 1, :], -1.0, None, ALU.mult))
            own.wait()
            V.memset(convin[:, :, 0:TAPS - 1], 0.0).then_inc(s("state_ready"), 1)

            def gain_evict(dst, src_bank, T, c0):
                return V.tensor_tensor(dst[:, :, 0:T], src_bank.rearrange("p (c t) -> p c t", c=4)[:, :, 0:T],
                                       bc(cols[:, c0:c0 + 4], P, 4, T), ALU.mult)

            def aT_evict(t, n):
                dve.wait_ge(s("aTp_done"), n)
                T = rows(t)
                own.did(gain_evict(aT[:, 0:4], bank[5], T, c_mix))
                gain_evict(aT[:, 4:8], bank[6], T, c_mix + 4).then_inc(s("aT_ready"), 1)

            def h_add(t, n):
                T = rows(t)
                dve.wait_ge(s("out_done"), n)
                own.did(V.tensor_tensor(hhalf(t, 0), bank[6][0:T, :], hhalf(t, 0), ALU.add))
                own.wait()
                V.tensor_tensor(hhalf(t, 1), bank[7][0:T, :], hhalf(t, 1), ALU.add).then_inc(s("h_ready"), 1)

            def catT0(t, n):
                T = rows(t)
                dve.wait_ge(s("catTp0_done"), n)
                gain_evict(catT[:, 0:4], bank[4], T, c_ssd).then_inc(s("catT0_ready"), 1)

            def lg_evict(t, n):
                T = rows(t)
                dve.wait_ge(s("lg_done"), n)
                dst = logits[0:T, bass.ds(t, 1), :].rearrange("p o e -> p (o e)")
                V.tensor_tensor(dst, bank[3][0:T, 0:NG + NE], bias_r[0:T, :], ALU.add).then_inc(s("lg_ready"), 1)

            def tile(t, n, p):
                T = rows(t)
                sample = T == S
                first = isinstance(t, int) and t == 0
                last_two = isinstance(t, int) and t >= NT - 1
                dve.wait_ge(s("bc_done"), n)
                V.tensor_copy(raw[0:T, BANK:], bank[1][0:T, :]).then_inc(s("raw1_ready"), 1)
                if not first:
                    catT0(t - 1, p)
                dve.wait_ge(s("rawT_done"), n)
                if sample:
                    own.did(V.tensor_copy(conv_s[:, :, :, 0:TAPS - 1], conv_old.rearrange("p c (b j) -> p c b j", b=NSEQ)))
                elif not first:
                    own.did(V.tensor_copy(convin[:, :, 0:TAPS - 1], convin[:, :, P:P + TAPS - 1]))
                    own.wait()
                for half in range(2):
                    cs = slice(4 * half, 4 * half + 4)
                    if sample:
                        dst = conv_s[:, cs, :, TAPS - 1:]
                        src = bank[half].rearrange("p (c t) -> p c t", c=4)[:, :, 0:T].rearrange("p c (b t) -> p c b t", b=NSEQ)
                    else:
                        dst, src = convin[:, cs, TAPS - 1:], bank[half].rearrange("p (c t) -> p c t", c=4)
                    ins = V.tensor_copy(dst, src)
                    if half == 0:
                        own.did(ins)
                    else:
                        ins.then_inc(s("convin_ready"), 1)
                own.wait()
                dve.wait_ge(s("convin_ready"), n)
                if last_two:
                    dve.wait_ge(s("conv_stored"), 16 if t == NT - 1 else 16 * (1 + NSEQ))
                dve.wait_ge(s("dt_done"), n)
                own.did(V.tensor_tensor(xsp[0:T], bank[3][0:T, 0:HEADS], heads3[0:T, 0, :], ALU.add))
                own.wait()
                V.scalar_tensor_tensor(out=nab[0:T], in0=xsp[0:T], scalar=-1.0, in1=xsp[0:T], op0=ALU.mult, op1=ALU.min).then_inc(s("nab_ready"), 1)
                tap = {}
                for j in range(TAPS):
                    for c in range(CC):
                        w = cols[:, c_cw + j * CC + c:c_cw + j * CC + c + 1]
                        if sample:
                            src = conv_s[:, c, :, j:j + NTOK]
                            dst = acc[:, c, 0:T].rearrange("p (b t) -> p b t", b=NSEQ)
                        else:
                            src, dst = convin[:, c, j:j + P], acc[:, c, :]
                        if j == 0:
                            tap[c] = own.did(V.tensor_scalar(dst, src, w, cols[:, c_cb + c:c_cb + c + 1], ALU.mult, ALU.add))
                        else:
                            own.wait(tap[c])
                            ins = V.scalar_tensor_tensor(out=dst, in0=src, scalar=w, in1=dst, op0=ALU.mult, op1=ALU.add)
                            if j == TAPS - 1 and c % 4 == 3:
                                ins.then_inc(s("conv_ready"), 1)
                            else:
                                tap[c] = own.did(ins)
                dve.wait_ge(s("sp_ready"), n)
                own.did(V.tensor_scalar(dd[0:T], ex[0:T], 1.0, -1.0, ALU.add, ALU.add))
                own.wait()
                own.did(V.tensor_scalar(dd[0:T], dd[0:T], TINY, None, ALU.add))
                own.did(V.scalar_tensor_tensor(out=rd[0:T], in0=ln1[0:T], scalar=TINY, in1=ex[0:T], op0=ALU.add, op1=ALU.mult))
                own.wait()
                own.did(V.reciprocal(dd[0:T], dd[0:T]))
                own.wait()
                own.did(V.tensor_tensor(rd[0:T], rd[0:T], dd[0:T], ALU.mult))
                own.wait()
                own.did(V.scalar_tensor_tensor(out=dtv[0:T], in0=xsp[0:T], scalar=0.0, in1=rd[0:T], op0=ALU.max, op1=ALU.add))
                own.wait()
                own.did(V.tensor_tensor(da[0:T], dtv[0:T], heads3[0:T, 1, :], ALU.mult))
                own.wait()
                if sample:
                    dve.wait_ge(s("v_done"), n)
                    own.did(V.tensor_copy(dax.rearrange("p (h q) -> p h q", h=HEADS), bc(da[0:T], T, HEADS, HP)))
                mk_i = incl_s if sample else incl
                V.tensor_tensor(dec[0:T, :, 0:T], bc(da[0:T], T, HEADS, T), mk_i[0:T, 0:T].unsqueeze(1).to_broadcast([T, HEADS, T]),
                                ALU.mult).then_inc(s("dam_ready"), 1)
                if sample:
                    own.wait()
                if not first:
                    h_add(t - 1, p)
                if not sample:
                    aT_evict(t + 1, (n + 1))
                dve.wait_ge(s("rv_ready"), n)
                V.scalar_tensor_tensor(out=vv[0:T, :], in0=vv[0:T, :], scalar=rv[0:T, :], in1=gm_row[0:T, :], op0=ALU.mult,
                                       op1=ALU.mult).then_inc(s("vn_ready"), 1)
                dve.wait_ge(s("ecum_ready"), n)
                dve.wait_ge(s("xtok_done"), n)
                xt = bank[7][0:T, :].rearrange("p (h q) -> p h q", h=HEADS)
                v3 = lambda ap: ap[0:T, :].rearrange("p (h q) -> p h q", h=HEADS)
                own.did(V.tensor_tensor(v3(xdt), xt, bc(dtv[0:T], T, HEADS, HP), ALU.mult))
                own.did(V.tensor_tensor(v3(yy), xt, bc(heads3[0:T, 2, :], T, HEADS, HP), ALU.mult))
                own.wait()
                V.tensor_tensor(v3(xwd), v3(xdt), bc(ecum[0:T, HEADS:2 * HEADS], T, HEADS, HP), ALU.mult).then_inc(s("xw_ready"), 1)
                dve.wait_ge(s("cb_done"), n)
                V.tensor_tensor(cbm[0:T, :, 0:T], bank[2][0:T, 0:GROUPS * P].rearrange("p (g t) -> p g t", g=GROUPS)[:, :, 0:T],
                                mk_i[0:T, 0:T].unsqueeze(1).to_broadcast([T, GROUPS, T]), ALU.mult).then_inc(s("cbm_ready"), 1)
                dve.wait_ge(s("cbm_ready"), n)
                dve.wait_ge(s("decay_ready"), n)
                for g in range(GROUPS):
                    hs = slice(g * GH, (g + 1) * GH)
                    ins = V.tensor_tensor(dec[0:T, hs, 0:T], dec[0:T, hs, 0:T], cbm[0:T, g, 0:T].unsqueeze(1).to_broadcast([T, GH, T]), ALU.mult)
                    if g == GROUPS - 1:
                        ins.then_inc(s("wts_ready"), 1)
                    else:
                        own.did(ins)
                        own.wait()
                if sample:
                    for g in range(GROUPS):
                        ins = V.tensor_tensor(ctm[:, g, :, :], xcT[:, XC + GROUPS + g, 0:S].unsqueeze(1).to_broadcast([P, NSEQ, S]),
                                              seq_rows[:, :, :], ALU.mult)
                        if g == GROUPS - 1:
                            own.wait()
                            ins.then_inc(s("ctm_ready"), 1)
                        else:
                            own.did(ins)
                    dve.wait_ge(s("bt_ready"), n)
                    for g in range(GROUPS):
                        ins = V.tensor_tensor(bmm[:, g, :, :], bt[0:S, g * N:(g + 1) * N].unsqueeze(1).to_broadcast([S, NSEQ, N]),
                                              bc(seq_cols[:, :], S, NSEQ, N), ALU.mult)
                        if g == GROUPS - 1:
                            ins.then_inc(s("bmm_ready"), 1)
                        else:
                            own.did(ins)
                dve.wait_ge(s("gm_done"), n)
                if not first:
                    dve.wait_ge(s("catTp1_done"), p)
                bcol = bs_s[:, :] if sample else cols[:, c_bs:c_bs + GMH]
                c3 = bank[6][0:T, :].rearrange("p (h q) -> p h q", h=GMH)
                own.did(V.tensor_tensor(c3, c3, bc(bcol[0:T], T, GMH, GMD), ALU.add))
                own.wait()
                own.did(V.tensor_tensor(uu[0:T, :], bank[6][0:T, :], uu[0:T, :], ALU.mult))
                dve.wait_ge(s("yoff_done"), n)
                c3 = bank[5][0:T, :].rearrange("p (h q) -> p h q", h=HEADS)
                own.did(V.tensor_tensor(c3, c3, bc(ecum[0:T, 0:HEADS], T, HEADS, HP), ALU.mult))
                own.wait()
                own.did(V.tensor_tensor(yy[0:T, :], bank[5][0:T, :], yy[0:T, :], ALU.add))
                own.wait()
                dve.wait_ge(s("ydiag_done"), n)
                own.did(V.tensor_tensor(yy[0:T, :], bank[4][0:T, :], yy[0:T, :], ALU.add))
                own.wait()
                own.did(V.tensor_tensor(yy[0:T, :], yy[0:T, :], zs[0:T, :], ALU.mult))
                own.wait()
                for g in range(GROUPS):
                    seg = yy[0:T, g * GW:(g + 1) * GW]
                    ins = V.tensor_tensor_reduce(out=bank[5][0:T, g * GW:(g + 1) * GW], in0=seg, in1=seg, scale=1.0, scalar=0.0, op0=ALU.mult,
                                                 op1=ALU.add, accum_out=ssy[0:T, g:g + 1])
                    own.did(ins)
                own.wait()
                V.tensor_scalar(vy[0:T], ssy[0:T], 1.0 / GW, EPS, ALU.mult, ALU.add).then_inc(s("vy_ready"), 1)
                if not sample:
                    dve.wait_ge(s("cs_done"), n)
                    own.did(V.tensor_tensor(state.rearrange("p (h q) -> p h q", h=HEADS), state.rearrange("p (h q) -> p h q", h=HEADS),
                                            bc(ecum[:, 2 * HEADS:3 * HEADS], P, HEADS, HP), ALU.mult))
                    own.wait()
                    V.tensor_tensor(state, bank[7][:, :], state, ALU.add).then_inc(s("state_ready"), 1)
                dve.wait_ge(s("ry_ready"), n)
                V.tensor_tensor(cat[0:T, 0:SSD].rearrange("p (g q) -> p g q", g=GROUPS), yy[0:T, :].rearrange("p (g q) -> p g q", g=GROUPS),
                                bc(ry[0:T], T, GROUPS, GW), ALU.mult).then_inc(s("cat_ready"), 1)
                if not first and not sample:
                    lg_evict(t - 1, p)
                own.restart()

            aT_evict(0, 1)
            dve.wait_ge(s("w_r_loaded"), 64)
            V.tensor_tensor(w_r, w_r, bc(cols[:, c_ffn:c_ffn + KC], P, KC, NG + NE), ALU.mult).then_inc(s("w_r_ready"), 1)
            dve.wait_ge(s("gm_row_loaded"), 16)
            tile(0, 1, 0)
            with dve.Fori(1, NT - 1) as t:
                tile(t, dve.snap(t + 1), t)
            tile(NT - 1, NT, NT - 1)
            dve.wait_ge(s("sample_w_loaded"), 32 * NSEQ)
            own.did(V.transpose(ws_s[0:S, :, :].rearrange("p h t -> p (h t)"), wsn))
            own.wait()
            dve.wait_ge(s("seq_ready"), 1)
            own.did(V.tensor_tensor(ws_s[0:S, :, :], ws_s[0:S, :, :], incl_s[:, :].unsqueeze(1).to_broadcast([S, GMH, S]), ALU.mult))
            own.wait()
            V.memset(logits[:, NT, :], 0.0).then_inc(s("ws_s_ready"), 1)
            tile(NT, TILES, NT)
            def state_add(j):
                c, q = j // 2, j % 2
                dst = s_nat[:, c, 4 * q:4 * q + 4, :]
                own.did(V.tensor_tensor(dst, dst, bc(edcol[:, c, 4 * q:4 * q + 4], P, 4, N), ALU.mult))
                own.wait()
                dve.wait_ge(s("cs_s_done"), j + 1)
                V.tensor_tensor(dst, bank[update_bank(j)].rearrange("p (b n) -> p b n", b=4), dst, ALU.add).then_inc(s("s_new"), 1)

            state_add(0)
            lg_evict(NT - 1, NT)
            catT0(NT, TILES)
            for j in range(1, 4):
                state_add(j)
            h_add(NT, TILES)
            for j in range(4, 2 * XC):
                state_add(j)
            dve.wait_ge(s("lg_ready"), NT)
            lg_evict(NT, TILES)
            own.did(V.tensor_copy(R["incl"], incl[:, :]))
            own.did(V.tensor_copy(R["ones"], ones[:, :]))

            dve.wait_ge(s("lg_ready"), TILES)
            dve.wait_ge(s("out_done"), TILES)
            def step(ins):
                own.did(ins)
                own.wait()
            g3 = lambda k: R[k].rearrange("p (t e) -> p t e", t=TILES)
            vec = [R["vec"][:, n * TILES:(n + 1) * TILES] for n in range(6)]
            lgr, ler = logits[:, :, 0:NG], logits[:, :, NG:]
            eg, og, leg, o1, o2 = (g3(k) for k in ("eg", "og", "leg", "o1", "o2"))

            def pick(values, out, W):
                step(V.tensor_reduce(vec[0], values, AX.X, ALU.max))
                step(V.tensor_tensor(out, values, bc(vec[0], P, TILES, W), ALU.is_equal))
                step(V.tensor_tensor(out, out, R["order"].unsqueeze(1).to_broadcast([P, TILES, W]), ALU.mult))
                step(V.tensor_reduce(vec[1], out, AX.X, ALU.max))
                step(V.tensor_tensor(out, out, bc(vec[1], P, TILES, W), ALU.is_equal))

            dve.wait_ge(s("iota_ready"), 1)
            step(V.tensor_scalar(R["order"], R["iota"][:, 0:NG], -1.0, float(NG), ALU.mult, ALU.add))
            pick(lgr, og, NG)
            step(V.tensor_tensor(eg, lgr, bc(vec[0], P, TILES, NG), ALU.subtract))
            V.tensor_copy(eg, eg).then_inc(s("exp_wanted"), 1)
            tmp = R["tmp"][:, 0:TILES * NE].rearrange("p (t g e) -> p t g e", t=TILES, g=NG)
            step(V.tensor_tensor(tmp, ler.rearrange("p t (g e) -> p t g e", g=NG), bc(og, P, TILES, NG, EPG), ALU.mult))
            own.did(V.tensor_reduce(leg, tmp.rearrange("p t g e -> p t e g"), AX.X, ALU.add))
            step(V.tensor_tensor(og, og, bc(R["valid"], P, TILES, NG), ALU.mult))
            pick(leg, o1, EPG)
            own.did(V.tensor_copy(vec[2], vec[0]))
            step(V.scalar_tensor_tensor(out=leg, in0=o1, scalar=-BIG, in1=leg, op0=ALU.mult, op1=ALU.add))
            pick(leg, o2, EPG)
            V.tensor_tensor(vec[3], vec[0], vec[2], ALU.subtract).then_inc(s("exp_wanted"), 1)
            hot = R["hot"].rearrange("p (q t g e) -> p q t g e", q=2, t=TILES, g=NG)
            for q, oo in enumerate((o1, o2)):
                own.did(V.tensor_tensor(hot[:, q], bc(og, P, TILES, NG, EPG), oo.unsqueeze(2).to_broadcast([P, TILES, NG, EPG]), ALU.mult))
            own.wait()
            V.tensor_tensor(R["hot12"], R["hot"][:, 0:TILES * NE], R["hot"][:, TILES * NE:], ALU.add).then_inc(s("onehot_ready"), 1)
            bige = R["big"][:, 0:NE * MAXB].rearrange("p (e j) -> p e j", e=NE)
            tri = R["upto"].rearrange("p (e j) -> p e j", e=NE)
            dve.wait_ge(s("counts_done"), 1)
            step(V.tensor_tensor(bige, bc(bank[1][:, 0:NE], P, NE, MAXB), R["first"][:, 0:MAXB].unsqueeze(1).to_broadcast([P, NE, MAXB]), ALU.is_gt))
            step(V.tensor_reduce(R["cnt"], bige, AX.X, ALU.add))
            step(V.tensor_scalar(R["cnt"], R["cnt"], 1.0, None, ALU.max))
            step(V.tensor_tensor(tri, tri, R["cnt"].unsqueeze(1).to_broadcast([P, NE, NE]), ALU.mult))
            step(V.tensor_reduce(R["end"], tri, AX.X, ALU.add))
            own.did(V.tensor_scalar(R["blk"][:, 0:1], R["end"][:, NE - 1:NE], -1.0, float(BLOCKS), ALU.mult, ALU.add))
            step(V.tensor_tensor(R["base"], R["end"], R["cnt"], ALU.subtract))
            own.did(V.tensor_copy(plan_u[:, 2 * NE:], R["blk"][:, 0:1]))
            own.did(V.tensor_copy(plan_u[:, 0:NE], R["base"]))
            step(V.tensor_scalar(R["base"], R["base"], float(P), -1.0, ALU.mult, ALU.add))
            V.tensor_copy(plan_u[:, NE:2 * NE], R["cnt"]).then_inc(s("plan_ready"), 1)
            dve.wait_ge(s("ranks_done"), 1)
            step(V.tensor_tensor(g3("rank"), bank[0][:, 0:TILES * NE].rearrange("p (t e) -> p t e", t=TILES),
                                 R["base"].unsqueeze(1).to_broadcast([P, TILES, NE]), ALU.add))
            step(V.tensor_tensor(R["tmp"].rearrange("p (q n) -> p q n", q=2), R["hot"].rearrange("p (q n) -> p q n", q=2),
                                 R["rank"].unsqueeze(1).to_broadcast([P, 2, TILES * NE]), ALU.mult))
            step(V.tensor_reduce(R["pos"], R["tmp"].rearrange("p (c e) -> p c e", e=NE), AX.X, ALU.add))
            own.did(V.tensor_copy(slots_u.rearrange("p q t -> p (q t)"), R["pos"]))
            C = 2 * TILES
            bigt = R["big"][:, 0:C * (BLOCKS - 1)].rearrange("p (c b) -> p c b", c=C)
            step(V.tensor_tensor(bigt, bc(R["pos"], P, C, BLOCKS - 1), R["first"][:, 1:BLOCKS].unsqueeze(1).to_broadcast([P, C, BLOCKS - 1]), ALU.is_ge))
            step(V.tensor_reduce(R["blk"], bigt, AX.X, ALU.add))
            own.did(V.scalar_tensor_tensor(out=R["mod"], in0=R["blk"], scalar=-float(P), in1=R["pos"], op0=ALU.mult, op1=ALU.add))
            hb = R["hot_block"].rearrange("p (c b) -> p c b", c=C)
            hs = R["hot_slot"].rearrange("p (c n) -> p c n", c=C)
            step(V.tensor_tensor(hb, bc(R["blk"], P, C, BLOCKS), R["iota"][:, 0:BLOCKS].unsqueeze(1).to_broadcast([P, C, BLOCKS]), ALU.is_equal))
            for q in range(2):
                own.did(V.tensor_tensor(hb[:, q * TILES:(q + 1) * TILES], hb[:, q * TILES:(q + 1) * TILES].bitcast(F32), bc(R["tok"], P, TILES, BLOCKS), ALU.mult))
            own.wait()
            for q in range(2):
                V.tensor_tensor(hs[:, q * TILES:(q + 1) * TILES], bc(R["mod"][:, q * TILES:(q + 1) * TILES], P, TILES, P),
                                R["iota"].unsqueeze(1).to_broadcast([P, TILES, P]), ALU.is_equal).then_inc(s("hot_ready"), 1)
            dve.wait_ge(s("exp_done"), 2)
            step(V.tensor_reduce(vec[4], eg, AX.X, ALU.add))
            step(V.scalar_tensor_tensor(out=vec[4], in0=vec[5], scalar=1.0, in1=vec[4], op0=ALU.add, op1=ALU.mult))
            step(V.reciprocal(gates[:, 0, :], vec[4]))
            step(V.tensor_tensor(gates[:, 1, :], gates[:, 0, :], vec[5], ALU.mult))
            step(V.memset(token_u[:, BLOCKS:], 0))
            dve.wait_ge(s("tokens_done"), 1)
            V.tensor_copy(token_u[:, 0:BLOCKS], bank[2][:, 0:BLOCKS]).then_inc(s("tokens_ready"), 1)
            dve.wait_ge(s("tokens_ready"), 1)
            own.restart()

            def lo(out, x, hi):
                return V.tensor_tensor(out, x, hi.bitcast(F32), ALU.subtract)

            def split(e, at):
                done = STEPS * e if isinstance(e, int) else dve.snap(STEPS * e)
                steps = SPLITS[at]
                for q in steps:
                    dve.wait_ge(s("w_high"), done + q + 1)
                    if q < 2 * KC:
                        k, cols_ = q % KC, slice(q // KC * HE, (q // KC + 1) * HE)
                        ins = V.scalar_tensor_tensor(out=gu_lo[:, k, :, cols_], in0=raw_gu[q // KC][:, k, :, :], scalar=gain(e, k),
                                                     in1=gu_hi[:, k, :, cols_].bitcast(F32), op0=ALU.mult, op1=ALU.subtract)
                    else:
                        ks = q - 2 * KC
                        ins = lo(d_lo[:, ks, :], raw_d[:, ks, :], d_hi[:, ks, :])
                    ins.then_inc(s("w_split"), 1)

            def b_xT(n):
                dve.wait_ge(s("xh_ready"), n)
                own.did(lo(xl[:, 0:4].rearrange("p k t -> p (k t)"), bank[0][:, :], xh[:, 0:4].rearrange("p k t -> p (k t)")))
                lo(xl[:, 4:8].rearrange("p k t -> p (k t)"), bank[1][:, :], xh[:, 4:8].rearrange("p k t -> p (k t)")).then_inc(s("xT_ready"), 1)

            def b_hidT(half, ready):
                dve.wait_ge(s("hh_ready"), ready)
                ks = slice(half * DC // 2, (half + 1) * DC // 2)
                lo(hid_lo[:, ks].rearrange("p k t -> p (k t)"), bank[2][:, half * HE:(half + 1) * HE],
                   hid_hi[:, ks].rearrange("p k t -> p (k t)")).then_inc(s("hidT_ready"), 1)

            def split_gu(splits, e):
                if splits:
                    split(e + 1, "A1")
                    split(e + 1, "B")

            def b_hid(n, half):
                dve.wait_ge(s("silu_ready"), dve.snap(2 * n - 1 + half))
                dve.wait_ge(s("up_done"), dve.snap(2 * n - 1 + half))
                part = sg[:, half * HE:(half + 1) * HE]
                V.tensor_tensor(part, bank[3 + 2 * half][:, 0:HE], part, ALU.mult).then_inc(s("hid_ready"), 1)

            def one_block(b, e, splits, more):
                n = dve.snap(b + 1)
                if splits:
                    split(e + 1, "A0")
                b_hidT(0, dve.snap(2 * n))
                b_hid(n, 1)
                b_xT(dve.snap(n + 1))
                b_hidT(1, dve.snap(2 * n + 1))
                if more:
                    split_gu(splits, e)
                else:
                    split(e + 1, "A1")
                dve.wait_ge(s("down_done"), n)
                dve.wait_ge(s("y_stored"), dve.snap(16 * n))
                V.tensor_copy(yb[:, BANK:], bank[7][:, :]).then_inc(s("bank7_free"), 1)
                if not more:
                    split(e + 1, "B")
                if more and splits:
                    split(e + 1, "D0")
                if more:
                    b_hid(dve.snap(n + 1), 0)
                if more and splits:
                    split(e + 1, "D1")
                own.restart()

            dve.sem_inc(s("bank7_free"), 1)
            for name in ("hid_ready", "hTp_done", "hh_ready", "hidT_ready"):
                dve.sem_inc(s(name), 1)
            for part in ("A0", "A1"):
                split(0, part)
            b_xT(1)
            for part in ("B", "D0", "D1"):
                split(0, part)
            b_hid(1, 0)
            own.restart()
            each_block(dve, one_block)

            def c_head(t, n):
                T = rows(t)
                dve.wait_ge(s("ya_loaded"), 16 * n if isinstance(n, int) else dve.snap(16 * n))
                dve.wait_ge(s("y2_loaded"), 16 * n if isinstance(n, int) else dve.snap(16 * n))
                g = lambda q: gates[0:T, q, bass.ds(t, 1)]
                own.did(V.scalar_tensor_tensor(out=hrow(t), in0=ya[0:T, :], scalar=g(0), in1=hrow(t), op0=ALU.mult, op1=ALU.add))
                own.wait()
                V.scalar_tensor_tensor(out=hrow(t), in0=y2[0:T, :], scalar=g(1), in1=hrow(t), op0=ALU.mult, op1=ALU.add).then_inc(s("hc_ready"), 1)

            def c_anT(t, n):
                T = rows(t)
                dve.wait_ge(s("ah_ready"), n)
                part = lambda b: bank[b].rearrange("p (c t) -> p c t", c=4)[:, :, 0:T]
                own.did(lo(a_lo[:, 0:4, 0:T], part(3), a_hi[:, 0:4, 0:T]))
                lo(a_lo[:, 4:8, 0:T], part(4), a_hi[:, 4:8, 0:T]).then_inc(s("anT_ready"), 1)

            def c_pT(t, n):
                T = rows(t)
                dve.wait_ge(s("ph_ready"), n)
                lo(p_lo[:, :, 0:T], bank[0][:, 0:PC * P].rearrange("p (c t) -> p c t", c=PC)[:, :, 0:T], p_hi[:, :, 0:T]
                   ).then_inc(s("pT_ready"), 1)

            def c_en(t, n):
                T = rows(t)
                dve.wait_ge(s("re_ready"), n)
                own.did(V.scalar_tensor_tensor(out=en[0:T, 0:BANK], in0=bank[1][0:T, :], scalar=re_[0:T, :], in1=ple_row[0:T, 0:BANK],
                                               op0=ALU.mult, op1=ALU.mult))
                own.wait()
                V.scalar_tensor_tensor(out=en[0:T, BANK:], in0=bank[2][0:T, :], scalar=re_[0:T, :], in1=ple_row[0:T, BANK:],
                                       op0=ALU.mult, op1=ALU.mult).then_inc(s("en_ready"), 1)

            def c_blend(t, n):
                T = rows(t)
                dve.wait_ge(s("sig0_ready"), n)
                dve.wait_ge(s("sig1_ready"), n)
                dve.wait_ge(s("en_ready"), n)
                own.did(V.tensor_tensor(gate[0:T, :], gate[0:T, :], en[0:T, :], ALU.mult))
                own.wait()
                V.tensor_tensor(hrow(t), hrow(t), gate[0:T, :], ALU.add).then_inc(s("hf_ready"), 1)

            def c_out(t, n, p):
                T = rows(t)
                dve.wait_ge(s("rf_ready"), n)
                if p is not None:
                    dve.wait_ge(s("y_out_stored"), 16 * p if isinstance(p, int) else dve.snap(16 * p))
                V.scalar_tensor_tensor(out=yout[0:T, :], in0=hrow(t), scalar=rf[0:T, :], in1=fin_row[0:T, :], op0=ALU.mult,
                                       op1=ALU.mult).then_inc(s("yout_ready"), 1)

            split(NE, "D0")
            c_head(0, 1)
            c_pT(0, 1)
            c_anT(0, 1)
            dve.wait_ge(s("c_rows_loaded"), 32)
            own.restart()

            def c_tile(t, n, p):
                more = rows(t) != S
                n2 = n + 1 if isinstance(n, int) else dve.snap(n + 1)
                if more:
                    c_head(t + 1, n2)
                if p is not None:
                    c_blend(t - 1, p)
                c_en(t, n)
                if p is not None:
                    c_out(t - 1, p, None if isinstance(t, int) and t == 1 else dve.snap(p - 1) if not isinstance(p, int) else p - 1)
                if more:
                    c_pT(t + 1, n2)
                    c_anT(t + 1, n2)
                own.restart()

            c_tile(0, 1, None)
            c_tile(1, 2, 1)
            with dve.Fori(2, NT - 1) as t:
                c_tile(t, dve.snap(t + 1), t)
            c_tile(NT - 1, NT, NT - 1)
            c_tile(NT, TILES, NT)
            c_blend(NT, TILES)
            c_out(NT, TILES, NT)

        @block.scalar
        def _(act):
            A = nc.scalar
            own = Own(act, s("act_own"))
            for j, src in enumerate((i["dt_bias"], i["a_log"], i["d_skip"])):
                act.dma_start(heads3[:, j, :], src.partition_broadcast(P).rearrange("q o n -> q (o n)")).then_inc(s("heads_loaded"), 16)
            act.dma_start(h[32:32 + NSEQ * (TAPS - 1), NT * D:], i["state_conv"][0].rearrange("b j n -> (b j) n")).then_inc(s("conv_old_loaded"), 16)
            act.dma_start(cat.rearrange("p (h t) -> p h t", h=GMH), i["w_spatial"][0].rearrange("h t s -> t h s")).then_inc(s("ws_loaded"), 16)
            act.dma_start(gm_row[:, :], i["gmlp_norm"].partition_broadcast(P).rearrange("q o n -> q (o n)")).then_inc(s("gm_row_loaded"), 16)
            act.dma_start(w_r[:, :, 0:NG], i["w_router_group"][0].rearrange("(k p) n -> p k n", p=P)).then_inc(s("w_r_loaded"), 16)
            act.dma_start(w_r[:, :, NG:], i["w_router_expert"][0].rearrange("(k p) n -> p k n", p=P)).then_inc(s("w_r_loaded"), 16)
            act.dma_start(bias_r[:, 0:NG], i["b_router_group"].partition_broadcast(P).rearrange("q o n -> q (o n)")).then_inc(s("w_r_loaded"), 16)
            act.dma_start(bias_r[:, NG:], i["b_router_expert"].partition_broadcast(P).rearrange("q o n -> q (o n)")).then_inc(s("w_r_loaded"), 16)
            act.wait_ge(s("heads_loaded"), 16 * 3)
            A.activation(heads3[:, 1, :], heads3[:, 1, :], ACT.Exp).then_inc(s("ealog_ready"), 1)

            def x_square(t, n, free):
                T = rows(t)
                if isinstance(t, int) and t == 0:
                    act.wait_ge(s("x0_loaded"), 16)
                else:
                    act.wait_ge(s("x_loaded"), 32)
                A.activation(xn[0:T, :], hrow(t), ACT.Square, accum_out=ssx[0:T, :]).then_inc(s("ssx_ready"), 1)

            def h_square(t, n):
                T = rows(t)
                act.wait_ge(s("h_ready"), n)
                A.activation(xn[0:T, :], hrow(t), ACT.Square, accum_out=ssh[0:T, :]).then_inc(s("ssh_ready"), 1)

            def mT_evict(t, n):
                T = rows(t)
                act.wait_ge(s("mTp_done"), n)
                own.did(A.activation(mT[:, 0:4, 0:T], bank[0].rearrange("p (c t) -> p c t", c=4)[:, :, 0:T], ACT.Copy))
                own.wait()
                A.activation(mT[:, 4:8, 0:T], bank[1].rearrange("p (c t) -> p c t", c=4)[:, :, 0:T], ACT.Copy).then_inc(s("mT_ready"), 1)

            def catT1(t, n):
                T = rows(t)
                act.wait_ge(s("catTp1_done"), n)
                A.activation(catT[:, 4:8, 0:T], bank[5].rearrange("p (c t) -> p c t", c=4)[:, :, 0:T], ACT.Copy).then_inc(s("catT1_ready"), 1)

            def tile(t, n, p):
                T = rows(t)
                sample = T == S
                first = isinstance(t, int) and t == 0
                act.wait_ge(s("xb_done"), n)
                A.activation(raw[0:T, 0:BANK], bank[0][0:T, :], ACT.Copy).then_inc(s("raw0_ready"), 1)
                if not sample and not first:
                    act.wait_ge(s("ry_ready"), p)
                    x_square(t + 1, n, p)
                if not first:
                    catT1(t - 1, p)
                if first:
                    act.wait_ge(s("z_done"), n)
                    A.activation(zs[0:T, :], bank[2][0:T, :], ACT.Silu).then_inc(s("z_ready"), 1)
                act.wait_ge(s("nab_ready"), n)
                own.did(A.activation(ex[0:T], nab[0:T], ACT.Exp))
                own.wait()
                A.activation(ln1[0:T], ex[0:T], ACT.Ln, bias=1.0).then_inc(s("sp_ready"), 1)
                if first:
                    x_square(t + 1, n, p)
                else:
                    act.wait_ge(s("z_done"), n)
                    A.activation(zs[0:T, :], bank[2][0:T, :], ACT.Silu).then_inc(s("z_ready"), 1)
                act.wait_ge(s("conv_ready"), 2 * n if isinstance(n, int) else act.snap(2 * n))
                A.activation(xcT[:, :, 0:T], acc[:, :, 0:T], ACT.Silu).then_inc(s("xc_ready"), 1)
                act.wait_ge(s("u_done"), n)
                A.activation(uu[0:T, :], bank[2][0:T, :], ACT.Gelu).then_inc(s("u_ready"), 1)
                act.wait_ge(s("v_done"), n)
                A.activation(vv[0:T, :], bank[4][0:T, :], ACT.Gelu).then_inc(s("v_ready"), 1)
                act.wait_ge(s("v_ready"), n)
                A.activation(yy[0:T, :], vv[0:T, :], ACT.Square, accum_out=ssv[0:T, :]).then_inc(s("ssv_ready"), 1)
                act.wait_ge(s("seg_done"), n)
                for half in range(2):
                    b3 = bank[half].rearrange("p (h t) -> p h t", h=4)[0:T, :, 0:T]
                    ins = A.activation(dec[0:T, 4 * half:4 * half + 4, 0:T], b3, ACT.Exp)
                    if half:
                        own.wait()
                        ins.then_inc(s("decay_ready"), 1)
                    else:
                        own.did(ins)
                act.wait_ge(s("cum_done"), n)
                if sample:
                    own.did(A.activation(edcol[:, :, :].rearrange("p c b -> p (c b)"), bank[3][:, 32:32 + NSEQ * XC], ACT.Exp))
                    own.wait()
                w = (2 if sample else 3) * HEADS
                A.activation(ecum[0:T, 0:w], bank[3][0:T, 0:w], ACT.Exp).then_inc(s("ecum_ready"), 1)
                if not first:
                    if not sample:
                        act.wait_ge(s("aTp_done"), (n + 1) if isinstance(n, int) else act.snap(n + 1))
                    h_square(t - 1, p)
                act.wait_ge(s("bt_done"), n)
                A.activation(bt[0:T, :], bank[3][0:T, 0:GROUPS * N], ACT.Copy).then_inc(s("bt_ready"), 1)
                if sample:
                    for b in range(NSEQ):
                        act.wait_ge(s("s_trp_done"), b + 1)
                        A.activation(s_tr[:, b, :], bank[5 + 2 * (b % 2)][:, :], ACT.Copy).then_inc(s("s_tr_ready"), 1)
                if not first:
                    mT_evict(t - 1, p)
                own.restart()

            x_square(0, 1, None)
            act.wait_ge(s("gm_row_loaded"), 16)
            act.wait_ge(s("aTp_done"), 1)
            tile(0, 1, 0)
            with act.Fori(1, NT - 1) as t:
                tile(t, act.snap(t + 1), t)
            tile(NT - 1, NT, NT - 1)
            tile(NT, TILES, NT)
            catT1(NT, TILES)
            h_square(NT, TILES)
            mT_evict(NT, TILES)
            act.wait_ge(s("finalp_done"), 1)
            A.activation(final_sb, bank[2][:, :], ACT.Copy).then_inc(s("final_ready"), 1)
            act.wait_ge(s("exp_wanted"), 1)
            eg = R["eg"]
            A.activation(eg, eg, ACT.Exp).then_inc(s("exp_done"), 1)
            act.wait_ge(s("exp_wanted"), 2)
            A.activation(R["vec"][:, 5 * TILES:6 * TILES], R["vec"][:, 3 * TILES:4 * TILES], ACT.Exp).then_inc(s("exp_done"), 1)

            def split(e, at):
                x2 = isinstance(e, int)
                if at[0] != "D":
                    act.wait_ge(s(f"gu{int(at[0] == 'B')}_loaded"), 32 * (e + 1) if x2 else act.snap(32 * e + 32))
                steps = SPLITS[at]
                for q in steps:
                    if q < 2 * KC:
                        k, cols_ = q % KC, slice(q // KC * HE, (q // KC + 1) * HE)
                        ins = A.activation(gu_hi[:, k, :, cols_], raw_gu[q // KC][:, k, :, :], ACT.Copy, scale=gain(e, k))
                    else:
                        if q == 2 * KC:
                            act.wait_ge(s("d_loaded"), 16 * (e + 1) if x2 else act.snap(16 * e + 16))
                        ks = q - 2 * KC
                        ins = A.activation(d_hi[:, ks, :], raw_d[:, ks, :], ACT.Copy)
                    ins.then_inc(s("w_high"), 1)

            def b_xT(n):
                act.wait_ge(s("xTp_done"), n)
                own.did(A.activation(xh[:, 0:4].rearrange("p k t -> p (k t)"), bank[0][:, :], ACT.Copy))
                own.wait()
                A.activation(xh[:, 4:8].rearrange("p k t -> p (k t)"), bank[1][:, :], ACT.Copy).then_inc(s("xh_ready"), 1)

            def b_hidT(half, ready):
                act.wait_ge(s("hTp_done"), ready)
                A.activation(hid_hi[:, half * DC // 2:(half + 1) * DC // 2].rearrange("p k t -> p (k t)"),
                             bank[2][:, half * HE:(half + 1) * HE], ACT.Copy).then_inc(s("hh_ready"), 1)

            def split_gu(splits, e):
                if splits:
                    split(e + 1, "A1")
                    split(e + 1, "B")

            def b_silu(n, half):
                act.wait_ge(s("gate_done"), act.snap(2 * n - 1 + half))
                A.activation(sg[:, half * HE:(half + 1) * HE], bank[2 + 2 * half][:, 0:HE], ACT.Silu).then_inc(s("silu_ready"), 1)

            def one_block(b, e, splits, more):
                n = act.snap(b + 1)
                if splits:
                    split(e + 1, "A0")
                b_hidT(0, act.snap(2 * n))
                b_silu(n, 1)
                b_xT(act.snap(n + 1))
                b_hidT(1, act.snap(2 * n + 1))
                if more:
                    split_gu(splits, e)
                else:
                    split(e + 1, "A1")
                act.wait_ge(s("down_done"), n)
                act.wait_ge(s("y_stored"), act.snap(16 * n))
                A.activation(yb[:, 0:BANK], bank[6][:, :], ACT.Copy).then_inc(s("bank6_free"), 1)
                if more and splits:
                    split(e + 1, "D0")
                if more:
                    b_silu(act.snap(n + 1), 0)
                act.wait_ge(s("bank6_free"), act.snap(n + 1))
                act.wait_ge(s("bank7_free"), act.snap(n + 1))
                act.dma_start(y_rows[bass.ds(b * P, P), :], yb).then_inc(s("y_stored"), 16)
                if not more:
                    split(e + 1, "B")
                    split(e + 1, "D0")
                if splits:
                    if more:
                        split(e + 1, "D1")
                own.restart()
                if more:
                    act.wait_ge(s("up_done"), act.snap(2 * n + 1))

            act.sem_inc(s("bank6_free"), 1)
            act.sem_inc(s("y_stored"), 16)
            act.wait_ge(s("out_done"), TILES)
            act.wait_ge(s("mTp_done"), TILES)
            act.wait_ge(s("lg_done"), TILES)
            act.wait_ge(s("ssm_stored"), 16 * XC)
            act.wait_ge(s("out_stored"), 32)
            for part in SPLITS:
                split(0, part)
            b_xT(1)
            b_silu(1, 0)
            own.restart()
            act.wait_ge(s("up_done"), 1)
            each_block(act, one_block)

            def c_pT(t, n):
                T = rows(t)
                act.wait_ge(s("pTp_done"), n)
                A.activation(p_hi[:, :, 0:T], bank[0][:, 0:PC * P].rearrange("p (c t) -> p c t", c=PC)[:, :, 0:T], ACT.Copy).then_inc(s("ph_ready"), 1)

            def c_anT(t, n):
                T = rows(t)
                act.wait_ge(s("anTp_done"), n)
                part = lambda b: bank[b].rearrange("p (c t) -> p c t", c=4)[:, :, 0:T]
                own.did(A.activation(a_hi[:, 0:4, 0:T], part(3), ACT.Copy))
                own.wait()
                A.activation(a_hi[:, 4:8, 0:T], part(4), ACT.Copy).then_inc(s("ah_ready"), 1)

            def c_hsq(t, n):
                T = rows(t)
                act.wait_ge(s("hc_ready"), n)
                A.activation(an[0:T, :], hrow(t), ACT.Square, accum_out=ssc[0:T, :]).then_inc(s("ssc_ready"), 1)

            def c_esq(t, n):
                T = rows(t)
                act.wait_ge(s("ple_done"), n)
                own.did(A.activation(junk[0:T, 0:BANK], bank[1][0:T, :], ACT.Square, accum_out=sse[0:T, 0:1]))
                A.activation(junk[0:T, BANK:], bank[2][0:T, :], ACT.Square, accum_out=sse[0:T, 1:2]).then_inc(s("sse_ready"), 1)

            def c_sig(t, n, half):
                T = rows(t)
                act.wait_ge(s(f"pg{half}_done"), n)
                A.activation(gate[0:T, half * BANK:(half + 1) * BANK], bank[5 + half][0:T, :], ACT.Sigmoid).then_inc(s(f"sig{half}_ready"), 1)

            def c_fsq(t, n, p):
                T = rows(t)
                act.wait_ge(s("hf_ready"), n)
                A.activation(gate[0:T, :], hrow(t), ACT.Square, accum_out=ssf[0:T, :]).then_inc(s("ssf_ready"), 1)

            act.wait_ge(s("w_split"), STEPS * NE + 2 * KC + PC)
            c_hsq(0, 1)
            c_pT(0, 1)
            c_anT(0, 1)
            own.restart()

            def c_tile(t, n, p):
                more = rows(t) != S
                n2 = n + 1 if isinstance(n, int) else act.snap(n + 1)
                c_esq(t, n)
                if more:
                    c_hsq(t + 1, n2)
                if p is not None:
                    c_fsq(t - 1, p, None)
                    act.wait_ge(s("ssf_ready"), p)
                c_sig(t, n, 0)
                if more:
                    c_pT(t + 1, n2)
                    c_anT(t + 1, n2)
                c_sig(t, n, 1)
                own.restart()

            c_tile(0, 1, None)
            with act.Fori(1, NT - 1) as t:
                c_tile(t, act.snap(t + 1), t)
            c_tile(NT - 1, NT, NT - 1)
            c_tile(NT, TILES, NT)
            c_fsq(NT, TILES, None)

        @block.gpsimd
        def _(pool):
            G = nc.gpsimd
            own = Own(pool, s("pool_own"))
            own.did(G.memset(ident[:, :], 0.0))
            own.did(G.memset(ones[:, :], 1.0))
            own.did(G.memset(half_neg[:, :], -0.5))
            norm_eps = {D: norm_c[:, 0:1], GM: norm_c[:, 1:2]}
            own.did(G.memset(norm_c[:, 0:1], D * EPS))
            own.did(G.memset(norm_c[:, 1:2], GM * EPS))
            own.did(G.memset(wsn, 0.0))
            own.wait()
            G.affine_select(out=ident[:, :], in_=ident[:, :], compare_op=ALU.not_equal, fill=1.0, base=0, pattern=[[-1, P]],
                            channel_multiplier=1).then_inc(s("ident_ready"), 1)
            own.did(G.affine_select(out=incl[:, :], in_=ones[:, :], compare_op=ALU.is_ge, fill=0.0, base=0, pattern=[[1, P]], channel_multiplier=-1))
            own.wait()
            G.affine_select(out=strict[:, :], in_=ones[:, :], compare_op=ALU.is_gt, fill=0.0, base=0, pattern=[[-1, P]],
                            channel_multiplier=1).then_inc(s("incl_ready"), 1)
            def rstd(sum_, var, out, T, count):
                own.did(G.tensor_tensor(var[0:T], sum_[0:T], norm_eps[count][0:T, :], ALU.add))
                own.wait()
                own.did(G.tensor_tensor(var[0:T], var[0:T], half_neg[0:T, 0:1], ALU.pow))
                own.wait()
                return G.tensor_scalar(out[0:T], var[0:T], float(count) ** 0.5, None, ALU.mult)

            def x_norm(t, n):
                T = rows(t)
                pool.wait_ge(s("ssx_ready"), n)
                own.did(rstd(ssx, vx, rx, T, D))
                own.wait()
                G.tensor_tensor(xn[0:T, :], hrow(t), rx[0:T, :].to_broadcast([T, D]), ALU.mult).then_inc(s("xn_ready"), 1)

            def m_norm(t, n):
                T = rows(t)
                pool.wait_ge(s("ssh_ready"), n)
                own.did(rstd(ssh, vh, rh, T, D))
                own.wait()
                G.tensor_tensor(xn[0:T, :], hrow(t), rh[0:T, :].to_broadcast([T, D]), ALU.mult).then_inc(s("m_ready"), 1)

            def tile(t, n, p):
                T = rows(t)
                if T != S:
                    x_norm(t + 1, n + 1 if isinstance(n, int) else pool.snap(n + 1))
                pool.wait_ge(s("ssv_ready"), n)
                rstd(ssv, vvv, rv, T, GM).then_inc(s("rv_ready"), 1)
                if not (isinstance(t, int) and t == 0):
                    m_norm(t - 1, p)
                if not (isinstance(t, int) and t == 0):
                    pool.wait_ge(s("m_stored"), 16 * p if isinstance(p, int) else pool.snap(16 * p))
                pool.wait_ge(s("vy_ready"), n)
                G.tensor_tensor(ry[0:T], vy[0:T], half_neg[0:T, 0:GROUPS], ALU.pow).then_inc(s("ry_ready"), 1)
                own.restart()

            x_norm(0, 1)
            wsn3 = wsn.rearrange("p (h t) -> p h t", h=GMH)
            for b in range(NSEQ):
                pool.dma_start(wsn3[b * NTOK:(b + 1) * NTOK, :, b * NTOK:(b + 1) * NTOK],
                               i["w_spatial"][0, :, 0:NTOK, 0:NTOK].rearrange("h t s -> t h s")).then_inc(s("sample_w_loaded"), 16)
                pool.dma_start(bs_s[b * NTOK:(b + 1) * NTOK, :], i["b_spatial"][0, :, 0:NTOK].rearrange("h t -> t h"),
                               allow_slow_non_contiguous=True).then_inc(s("sample_w_loaded"), 16)
            own.did(G.affine_select(out=seq_cols[:, :], in_=ones[0:S, 0:NSEQ], compare_op=ALU.is_ge, fill=0.0, base=0, pattern=[[-NTOK, NSEQ]], channel_multiplier=1))
            own.wait()
            own.did(G.affine_select(out=seq_cols[:, :], in_=seq_cols[:, :], compare_op=ALU.is_ge, fill=0.0, base=NTOK - 1, pattern=[[NTOK, NSEQ]], channel_multiplier=-1))
            own.wait()
            own.did(G.tensor_tensor(incl_s.rearrange("p (b t) -> p b t", b=NSEQ), bc(seq_cols[:, :], S, NSEQ, NTOK), incl[0:S, 0:S].rearrange("p (b t) -> p b t", b=NSEQ), ALU.mult))
            pool.wait_ge(s("incl_ready"), 1)
            own.did(G.tensor_tensor(strict_s.rearrange("p (b t) -> p b t", b=NSEQ), bc(seq_cols[:, :], S, NSEQ, NTOK), strict[0:S, 0:S].rearrange("p (b t) -> p b t", b=NSEQ), ALU.mult))
            own.did(G.memset(seq_rows[:, :, :], 1.0))
            own.wait()
            own.did(G.affine_select(out=seq_rows[:, :, :], in_=seq_rows[:, :, :], compare_op=ALU.is_ge, fill=0.0, base=0, pattern=[[-NTOK, NSEQ], [1, S]], channel_multiplier=0))
            own.wait()
            G.affine_select(out=seq_rows[:, :, :], in_=seq_rows[:, :, :], compare_op=ALU.is_ge, fill=0.0, base=NTOK - 1, pattern=[[NTOK, NSEQ], [-1, S]],
                            channel_multiplier=0).then_inc(s("seq_ready"), 1)

            tile(0, 1, 0)
            with pool.Fori(1, NT - 1) as t:
                tile(t, pool.snap(t + 1), t)
            tile(NT - 1, NT, NT - 1)
            tile(NT, TILES, NT)
            m_norm(NT, TILES)
            pool.wait_ge(s("m_stored"), 16 * TILES)
            pool.wait_ge(s("mTp_done"), TILES)
            pool.wait_ge(s("out_done"), TILES)
            pool.wait_ge(s("lg_ready"), TILES)
            own.did(G.iota(R["iota"], [[1, P]], base=0, channel_multiplier=0, allow_small_or_imprecise_dtypes=True))
            own.did(G.iota(R["tok"], [[P, TILES]], base=0, channel_multiplier=1, allow_small_or_imprecise_dtypes=True))
            own.did(G.memset(R["valid"], 1.0))
            own.did(G.iota(R["first"], [[P, BLOCKS]], base=0, channel_multiplier=0, allow_small_or_imprecise_dtypes=True))
            own.did(G.memset(R["upto"], 1.0))
            own.wait()
            own.did(G.affine_select(out=R["upto"], in_=R["upto"], compare_op=ALU.is_ge, fill=0.0, base=0, pattern=[[1, NE], [-1, NE]],
                                    channel_multiplier=0))
            own.wait()
            G.affine_select(out=R["valid"], in_=R["valid"], compare_op=ALU.is_ge, fill=0.0, base=SEQ + S - 1, pattern=[[-P, TILES]],
                            channel_multiplier=-1).then_inc(s("iota_ready"), 1)

            def gather(b, rows_used, before):
                if rows_used is not None:
                    pool.wait_ge(s("xTp_done"), rows_used)
                    pool.wait_ge(s("gathered"), before)
                pool.wait_ge(s("tokens_ready"), 1)
                own.did(G.tensor_copy(index_u[:, 0:1], token_u[:, bass.ds(b, 1)]))
                own.wait()
                pool.indirect_dma_start(xg, None, m_rows, bass.IndirectOffsetOnAxis(ap=index_u[:, 0:1], axis=0)).then_inc(s("gathered"), 16)
                own.restart()

            gather(0, None, None)
            total = blocks_in_all(pool)
            with pool.Fori(0, total) as b:
                n = pool.snap(b + 1)
                gather(n, n, pool.snap(16 * n))

            def c_gather(t, n, p):
                T = rows(t)
                for q, dst, name in ((0, ya, "ya_loaded"), (1, y2, "y2_loaded")):
                    if p is not None:
                        pool.wait_ge(s("hc_ready"), p)
                    own.did(G.tensor_copy(index_u[0:T, q:q + 1], slots_u[0:T, q, bass.ds(t, 1)]))
                    own.wait()
                    pool.indirect_dma_start(dst[0:T, :], None, y_rows[0:BLOCKS * P, :], bass.IndirectOffsetOnAxis(ap=index_u[0:T, q:q + 1], axis=0)
                                            ).then_inc(s(name), 16)

            def c_an(t, n):
                T = rows(t)
                pool.wait_ge(s("ssc_ready"), n)
                own.did(rstd(ssc, vc, rc, T, D))
                own.wait()
                G.tensor_tensor(an[0:T, :], hrow(t), rc[0:T, :].to_broadcast([T, D]), ALU.mult).then_inc(s("an_ready"), 1)

            def c_re(t, n):
                T = rows(t)
                pool.wait_ge(s("sse_ready"), n)
                own.did(G.tensor_tensor(ve[0:T], sse[0:T, 0:1], sse[0:T, 1:2], ALU.add))
                own.wait()
                rstd(ve, ve, re_, T, D).then_inc(s("re_ready"), 1)

            def c_rf(t, n):
                T = rows(t)
                pool.wait_ge(s("ssf_ready"), n)
                rstd(ssf, vf, rf, T, D).then_inc(s("rf_ready"), 1)

            pool.wait_ge(s("blocks_over"), 2)
            c_gather(0, 1, None)
            c_an(0, 1)
            c_gather(1, 2, 1)
            own.restart()

            def c_tile(t, n, p):
                n2 = n + 1 if isinstance(n, int) else pool.snap(n + 1)
                c_re(t, n)
                if rows(t) != S:
                    c_an(t + 1, n2)
                if p is not None:
                    c_rf(t - 1, p)
                if not (isinstance(t, int) and t >= NT - 1):
                    c_gather(t + 2, None, n2)
                own.restart()

            c_tile(0, 1, None)
            with pool.Fori(1, NT - 2) as t:
                c_tile(t, pool.snap(t + 1), t)
            c_tile(NT - 2, NT - 1, NT - 2)
            c_tile(NT - 1, NT, NT - 1)
            c_tile(NT, TILES, NT)
            c_rf(NT, TILES)


_OUTS = ("y_p", "y_s", "conv_p", "ssm_p", "conv_s", "ssm_s", "v_s")


def declare(nc, arrays, mybir_):
    ins = {name: nc.dram_tensor(f"in_{name}", a.shape, F32, kind="ExternalInput").ap() for name, a in arrays.items()}
    depth, nseq, taps, conv = arrays["state_conv"].shape
    _, _, heads, hp, n = arrays["state_ssm"].shape
    batch = arrays["x_prompt"].shape[0]
    ntok = arrays["x_sample"].shape[1]
    shapes = dict(y_p=arrays["x_prompt"].shape, y_s=arrays["x_sample"].shape, conv_p=(depth, batch, taps, conv),
                  ssm_p=(depth, batch, heads, hp, n), conv_s=(depth, nseq, taps, conv), ssm_s=(depth, nseq, heads, hp, n),
                  v_s=(depth, nseq, ntok, arrays["gmlp_norm"].shape[1]))
    outs = {name: nc.dram_tensor(f"out_{name}", shapes[name], F32, kind="ExternalOutput").ap() for name in _OUTS}
    return ins, outs


def kernel(**inputs):
    import numpy as np
    import concourse.bacc as bacc
    from concourse.bass_utils import run_bass_kernel_spmd

    nc = bacc.Bacc("TRN2", target_bir_lowering=False, num_devices=1)
    arrays = {name: np.ascontiguousarray(a) for name, a in inputs.items()}
    i, o = declare(nc, arrays, mybir)
    build(nc, i, o)
    r = run_bass_kernel_spmd(nc, [{f"in_{name}": a for name, a in arrays.items()}], core_ids=[0])
    return tuple(r.results[0][f"out_{name}"] for name in _OUTS)
```
